# Optimizing a Trainium2 kernel written in Bass

```python
import math
import jax, jax.numpy as jnp
from jax import lax
import numpy as np

D_MODEL = 1024
BATCH = 1
SEQ = 512
DEPTH = 1
DEC_BATCH = 1
DEC_SEQ = 64
PAST_LEN = 512

CHUNK = 64
N_META = 16
EPS = 1e-6
ATT_HEADS = 8
ATT_KV_HEADS = 4
ATT_HEAD_DIM = 64
ATT_GROUP = ATT_HEADS // ATT_KV_HEADS
ATT_WIDTH = ATT_HEADS * ATT_HEAD_DIM
ATT_KV_WIDTH = ATT_KV_HEADS * ATT_HEAD_DIM
Q_BLOCK = 128
FORGET_BIAS_INIT = 3.0
HG_HEADS = 4
HG_KEY_DIM = 128
HG_VAL_DIM = 128
HG_KEY_WIDTH = HG_HEADS * HG_KEY_DIM
HG_VAL_WIDTH = HG_HEADS * HG_VAL_DIM
MIX_WIDTH = ATT_WIDTH + HG_VAL_WIDTH
IN_SPLITS = (ATT_WIDTH, ATT_KV_WIDTH, ATT_KV_WIDTH, ATT_HEADS,
             HG_KEY_WIDTH, HG_KEY_WIDTH, HG_VAL_WIDTH, HG_VAL_WIDTH)
IN_OFFSETS = tuple(int(o) for o in np.cumsum((0,) + IN_SPLITS))
IN_WIDTH = IN_OFFSETS[-1]
PEER_HEADS = 8
PEER_N_KEYS = 128
PEER_N_EXPERTS = PEER_N_KEYS * PEER_N_KEYS
PEER_TOPK = 16
PEER_HALF = 128
PEER_QUERY_DIM = 2 * PEER_HALF
PEER_TOKEN_BLOCK = 256

kernel_name = "fox_hgrn2_peer_streaming_step"

def rms_norm(x, gain):
    x32 = x.astype(jnp.float32)
    y = x32 * lax.rsqrt(jnp.mean(x32 * x32, axis=-1, keepdims=True) + EPS)
    return (y * gain.astype(jnp.float32)).astype(x.dtype)

def mixer_projections(h, w_in, b_forget, lower_bound):
    B, T, _ = h.shape
    p = jnp.einsum('btd,dp->btp', h, w_in)
    q, k, v, fg, hq, hf, hi, hg = [p[..., IN_OFFSETS[n]:IN_OFFSETS[n + 1]] for n in range(len(IN_SPLITS))]
    q = q.reshape(B, T, ATT_HEADS, ATT_HEAD_DIM)
    k = k.reshape(B, T, ATT_KV_HEADS, ATT_HEAD_DIM)
    v = v.reshape(B, T, ATT_KV_HEADS, ATT_HEAD_DIM)
    logf_att = jax.nn.log_sigmoid((fg + b_forget).astype(jnp.float32))
    hq = jax.nn.silu(hq.astype(jnp.float32)).reshape(B, T, HG_HEADS, HG_KEY_DIM)
    f = lower_bound + (1.0 - lower_bound) * jax.nn.sigmoid(hf.astype(jnp.float32))
    hk = (1.0 - f).reshape(B, T, HG_HEADS, HG_KEY_DIM)
    hlogf = jnp.log(f).reshape(B, T, HG_HEADS, HG_KEY_DIM)
    hi = hi.astype(jnp.float32).reshape(B, T, HG_HEADS, HG_VAL_DIM)
    return q, k, v, logf_att, hq, hk, hlogf, hi, hg

def fox_attend(q, fq, qpos, k, v, fk, kpos):
    B, Tq = q.shape[:2]
    Tk = k.shape[1]
    qg = q.reshape(B, Tq, ATT_KV_HEADS, ATT_GROUP, ATT_HEAD_DIM)
    s = jnp.einsum('bqkgd,bskd->bkgqs', qg, k).astype(jnp.float32) * (ATT_HEAD_DIM ** -0.5)
    fq_g = fq.reshape(B, Tq, ATT_KV_HEADS, ATT_GROUP).transpose(0, 2, 3, 1)[..., None]
    fk_g = fk.reshape(B, Tk, ATT_KV_HEADS, ATT_GROUP).transpose(0, 2, 3, 1)[..., None, :]
    mask = kpos[None, :] <= qpos[:, None]
    s = jnp.where(mask, s + fq_g - fk_g, -jnp.inf)
    p = jax.nn.softmax(s, axis=-1).astype(v.dtype)
    o = jnp.einsum('bkgqs,bskd->bqkgd', p, v)
    return o.reshape(B, Tq, ATT_WIDTH)

def fox_prompt(q, k, v, logf):
    B, L = q.shape[:2]
    F = jnp.cumsum(logf, axis=1)
    nb = -(-L // Q_BLOCK)
    pad = nb * Q_BLOCK - L
    qp = jnp.pad(q, ((0, 0), (0, pad), (0, 0), (0, 0)))
    Fp = jnp.pad(F, ((0, 0), (0, pad), (0, 0)))
    q_blocks = qp.reshape(B, nb, Q_BLOCK, ATT_HEADS, ATT_HEAD_DIM).transpose(1, 0, 2, 3, 4)
    F_blocks = Fp.reshape(B, nb, Q_BLOCK, ATT_HEADS).transpose(1, 0, 2, 3)
    qpos_blocks = jnp.arange(nb * Q_BLOCK).reshape(nb, Q_BLOCK)
    kpos = jnp.arange(L)
    out = lax.map(lambda a: fox_attend(a[0], a[1], a[2], k, v, F, kpos),
                  (q_blocks, F_blocks, qpos_blocks))
    return out.transpose(1, 0, 2, 3).reshape(B, nb * Q_BLOCK, ATT_WIDTH)[:, :L]

def fox_sample(q, k, v, logf, cache_k, cache_v, cache_logf):
    T = q.shape[1]
    P = cache_k.shape[1]
    k_all = jnp.concatenate([cache_k.astype(k.dtype), k], axis=1)
    v_all = jnp.concatenate([cache_v.astype(v.dtype), v], axis=1)
    F = jnp.cumsum(jnp.concatenate([cache_logf.astype(jnp.float32), logf], axis=1), axis=1)
    kpos = jnp.arange(P + T)
    qpos = P + jnp.arange(T)
    return fox_attend(q, F[:, P:], qpos, k_all, v_all, F, kpos)

def hgrn_chunk(S, q, k, logf, i):
    C = q.shape[1]
    G = jnp.cumsum(logf, axis=1)
    t = jnp.arange(C)
    causal = (t[None, :] <= t[:, None])[None, :, :, None, None]
    decay = jnp.exp(jnp.where(causal, G[:, :, None] - G[:, None, :], -jnp.inf))
    scores = jnp.einsum('bthk,btshk,bshk->bhts', q, decay, k)
    o = (jnp.einsum('bhts,bshv->bthv', scores, i)
         + jnp.einsum('bthk,bhkv->bthv', q * jnp.exp(G), S))
    G_end = G[:, -1]
    S_new = (jnp.exp(G_end)[..., None] * S
             + jnp.einsum('bshk,bshv->bhkv', k * jnp.exp(G_end[:, None] - G), i))
    return o, S_new

def hgrn_prompt(q, k, logf, i):
    B = q.shape[0]
    S0 = jnp.zeros((B, HG_HEADS, HG_KEY_DIM, HG_VAL_DIM), jnp.float32)
    o_meta, S = hgrn_chunk(S0, q[:, :N_META], k[:, :N_META], logf[:, :N_META], i[:, :N_META])
    n_real = q.shape[1] - N_META
    nc = n_real // CHUNK

    def to_chunks(a):
        a = a[:, N_META:]
        return jnp.moveaxis(a.reshape(B, nc, CHUNK, *a.shape[2:]), 1, 0)

    def step(S_c, xs):
        o_c, S_c = hgrn_chunk(S_c, *xs)
        return S_c, o_c

    S, o_rest = lax.scan(step, S, (to_chunks(q), to_chunks(k), to_chunks(logf), to_chunks(i)))
    o_rest = jnp.moveaxis(o_rest, 0, 1).reshape(B, n_real, HG_HEADS, HG_VAL_DIM)
    return jnp.concatenate([o_meta, o_rest], axis=1), S

def hgrn_output(o, g_out, norm_gain, dtype):
    B, T = o.shape[:2]
    o = o * lax.rsqrt(jnp.mean(o * o, axis=-1, keepdims=True) + EPS)
    o = o * norm_gain.astype(jnp.float32).reshape(HG_HEADS, HG_VAL_DIM)
    return o.reshape(B, T, HG_VAL_WIDTH).astype(dtype) * jax.nn.silu(g_out)

def peer_ffn(x, w_query, sub_keys, expert_u, expert_v):
    N = x.shape[0]
    nb = -(-N // PEER_TOKEN_BLOCK)
    xb_all = jnp.pad(x, ((0, nb * PEER_TOKEN_BLOCK - N), (0, 0))).reshape(nb, PEER_TOKEN_BLOCK, D_MODEL)

    def block(xb):
        T = xb.shape[0]
        q = (xb @ w_query).reshape(T, PEER_HEADS, 2, PEER_HALF)
        s = jnp.einsum('thcd,hcnd->thcn', q, sub_keys)
        sa, ia = lax.top_k(s[:, :, 0], PEER_TOPK)
        sb, ib = lax.top_k(s[:, :, 1], PEER_TOPK)
        cand = (sa[..., :, None] + sb[..., None, :]).reshape(T, PEER_HEADS, PEER_TOPK * PEER_TOPK)
        cidx = (ia[..., :, None] * PEER_N_KEYS + ib[..., None, :]).reshape(T, PEER_HEADS, PEER_TOPK * PEER_TOPK)
        top_s, top_j = lax.top_k(cand, PEER_TOPK)
        eidx = jnp.take_along_axis(cidx, top_j, axis=-1)
        gate = jax.nn.softmax(top_s.astype(jnp.float32), axis=-1).astype(xb.dtype)
        act = jax.nn.gelu(jnp.einsum('thkd,td->thk', expert_u[eidx], xb), approximate=False)
        return jnp.einsum('thk,thkd->td', gate * act, expert_v[eidx])

    y = lax.map(block, xb_all)
    return y.reshape(nb * PEER_TOKEN_BLOCK, D_MODEL)[:N]

def trunk_layer(x, w_in, b_forget, lower_bound, hg_norm_gain, w_out, norm1_gain, norm2_gain,
                peer_w_query, peer_sub_keys, peer_expert_u, peer_expert_v, cache=None):
    h = rms_norm(x, norm1_gain)
    q, k, v, logf, hq, hk, hlogf, hi, hg = mixer_projections(h, w_in, b_forget, lower_bound)
    if cache is None:
        att = fox_prompt(q, k, v, logf)
        o, S = hgrn_prompt(hq, hk, hlogf, hi)
    else:
        cache_k, cache_v, cache_logf, state = cache
        att = fox_sample(q, k, v, logf, cache_k, cache_v, cache_logf)
        o, S = hgrn_chunk(state.astype(jnp.float32), hq, hk, hlogf, hi)
    mix = jnp.concatenate([att.astype(x.dtype), hgrn_output(o, hg, hg_norm_gain, x.dtype)], axis=-1)
    x = x + jnp.einsum('btm,md->btd', mix, w_out)
    h2 = rms_norm(x, norm2_gain)
    x = x + peer_ffn(h2.reshape(-1, D_MODEL), peer_w_query, peer_sub_keys,
                     peer_expert_u, peer_expert_v).reshape(x.shape)
    return x, (k, v, logf.astype(x.dtype), S.astype(x.dtype))

def setup_inputs(seed: int = 0) -> dict:
    key = jax.random.key(seed)
    ks = jax.random.split(key, 19)
    f32 = jnp.float32

    def nrm(k, shape, scale):
        return jax.random.normal(k, shape, f32) * scale

    return {
        "x_prompt": nrm(ks[0], (BATCH, SEQ, D_MODEL), 1.0),
        "x_sample": nrm(ks[1], (DEC_BATCH, DEC_SEQ, D_MODEL), 1.0),
        "cache_k": nrm(ks[2], (DEPTH, DEC_BATCH, PAST_LEN, ATT_KV_HEADS, ATT_HEAD_DIM), 1.0),
        "cache_v": nrm(ks[3], (DEPTH, DEC_BATCH, PAST_LEN, ATT_KV_HEADS, ATT_HEAD_DIM), 1.0),
        "cache_logf": jax.nn.log_sigmoid(FORGET_BIAS_INIT + nrm(ks[4], (DEPTH, DEC_BATCH, PAST_LEN, ATT_HEADS), 1.0)),
        "state_hgrn": nrm(ks[5], (DEPTH, DEC_BATCH, HG_HEADS, HG_KEY_DIM, HG_VAL_DIM), 0.5),
        "meta_tokens": nrm(ks[6], (N_META, D_MODEL), 1.0),
        "w_in": nrm(ks[7], (DEPTH, D_MODEL, IN_WIDTH), D_MODEL ** -0.5),
        "b_forget": FORGET_BIAS_INIT + nrm(ks[8], (DEPTH, ATT_HEADS), 0.1),
        "hg_lb_logits": nrm(ks[9], (DEPTH + 1, HG_KEY_WIDTH), 0.5),
        "hg_norm_gain": 1.0 + nrm(ks[10], (DEPTH, HG_VAL_WIDTH), 0.02),
        "w_out": nrm(ks[11], (DEPTH, MIX_WIDTH, D_MODEL), MIX_WIDTH ** -0.5),
        "norm1_gain": 1.0 + nrm(ks[12], (DEPTH, D_MODEL), 0.02),
        "norm2_gain": 1.0 + nrm(ks[13], (DEPTH, D_MODEL), 0.02),
        "peer_w_query": nrm(ks[14], (DEPTH, D_MODEL, PEER_HEADS * PEER_QUERY_DIM), D_MODEL ** -0.5),
        "peer_sub_keys": nrm(ks[15], (DEPTH, PEER_HEADS, 2, PEER_N_KEYS, PEER_HALF), PEER_HALF ** -0.5),
        "peer_expert_u": nrm(ks[16], (DEPTH, PEER_N_EXPERTS, D_MODEL), D_MODEL ** -0.5),
        "peer_expert_v": nrm(ks[17], (DEPTH, PEER_N_EXPERTS, D_MODEL), PEER_HEADS ** -0.5),
        "final_norm_gain": 1.0 + nrm(ks[18], (D_MODEL,), 0.02),
    }

def reference(x_prompt, x_sample, cache_k, cache_v, cache_logf, state_hgrn, meta_tokens,
              w_in, b_forget, hg_lb_logits, hg_norm_gain, w_out, norm1_gain, norm2_gain,
              peer_w_query, peer_sub_keys, peer_expert_u, peer_expert_v, final_norm_gain):
    lower_bounds = jnp.cumsum(jax.nn.softmax(hg_lb_logits.astype(jnp.float32), axis=0), axis=0)[:DEPTH]
    B = x_prompt.shape[0]
    meta = jnp.broadcast_to(meta_tokens.astype(x_prompt.dtype)[None], (B, N_META, D_MODEL))
    xp = jnp.concatenate([meta, x_prompt], axis=1)
    xs = x_sample
    prompt_states = [[], [], [], []]
    sample_states = [[], [], [], []]
    for l in range(DEPTH):
        params = (w_in[l], b_forget[l], lower_bounds[l], hg_norm_gain[l], w_out[l], norm1_gain[l],
                  norm2_gain[l], peer_w_query[l], peer_sub_keys[l], peer_expert_u[l], peer_expert_v[l])
        xp, sp = trunk_layer(xp, *params)
        xs, ss = trunk_layer(xs, *params, cache=(cache_k[l], cache_v[l], cache_logf[l], state_hgrn[l]))
        for n in range(4):
            prompt_states[n].append(sp[n])
            sample_states[n].append(ss[n])
    y_prompt = rms_norm(xp, final_norm_gain)[:, N_META:]
    y_sample = rms_norm(xs, final_norm_gain)
    new_k_prompt = jnp.stack(prompt_states[0])
    new_v_prompt = jnp.stack(prompt_states[1])
    new_logf_prompt = jnp.stack(prompt_states[2])
    new_state_prompt = jnp.stack(prompt_states[3])
    new_k_sample = jnp.stack(sample_states[0])
    new_v_sample = jnp.stack(sample_states[1])
    new_logf_sample = jnp.stack(sample_states[2])
    new_state_sample = jnp.stack(sample_states[3])
    return (y_prompt, y_sample, new_k_prompt, new_v_prompt, new_logf_prompt, new_state_prompt,
            new_k_sample, new_v_sample, new_logf_sample, new_state_sample)


_drawn_inputs = setup_inputs


def setup_inputs(seed=0):
    import zlib

    import numpy as np

    out = dict(_drawn_inputs(seed))
    spreads = {}
    factors = {'cache_logf': 10.075, 'hg_norm_gain': 3.152, 'final_norm_gain': 8.407, 'norm2_gain': 3.485}
    for name, (base, spread) in spreads.items():
        noise = np.random.default_rng([zlib.crc32(name.encode()), seed]).standard_normal(out[name].shape)
        drawn = base * np.exp(spread * noise) if base else spread * noise
        out[name] = __import__('jax').numpy.asarray(drawn.astype(out[name].dtype))
    for name, factor in factors.items():
        out[name] = (out[name] * factor).astype(out[name].dtype)
    return out
```

```python
from contextlib import ExitStack

import concourse.bass as bass
from concourse import mybir

F32 = mybir.dt.float32
I32 = mybir.dt.int32
U32 = mybir.dt.uint32
ALU = mybir.AluOpType
ACT = mybir.ActivationFunctionType
AX_X = mybir.AxisListType.X

P = 128
D = 1024
DC = D // P
EPS = 1e-6
N_META = 16
N_SAMPLE = 64
SEQ = 512
PAST = 512
TILES = 1 + SEQ // P
HEADS = 8
KV_HEADS = 4
KV_W = 256
HD = 64
HG = 4
HK = 128
HW = HG * HK
IN_W = 3080
FG0 = 1024
GROUP_COLS = [0, 512, 1032, 1544, 2056, 2568]
G_Q, G_KV, G_HQ, G_HF, G_HI, G_HGATE = range(6)
SQ, SK, SV, SLF, SHQ, SHK, SHL, SHI, SHG = 0, 512, 768, 1024, 1032, 1544, 2056, 2568, 3080
ST_W = 3592
PH = 8
NKEY = 128
TOPK = 16
SLOTS = PH * TOPK
GROUP = 16
S_GROUPS = SLOTS // 2 // GROUP
T_GROUPS = SLOTS // GROUP
GROUPS = S_GROUPS + (TILES - 1) * T_GROUPS
RING_U = 8
RING_V = 8
LEVELS = [64, 32, 16, 8, 4, 2, 1]
NL = len(LEVELS)
NEG = -1e30
SCALE = HD ** -0.5
META0 = 64
META1 = META0 + N_META
PROMPT_KEYS = N_META + SEQ
SAMPLE_KEYS = PAST + N_SAMPLE
C_ID, C_FOLD, C_TRI, C_TRIS, C_MASK, C_LEV = 0, 128, 256, 384, 512, 640
C_IOTA = C_LEV + (NL + 1) * P
C_ONE = C_IOTA + TOPK
C_W = C_ONE + P


def build(nc, x_prompt, x_sample, cache_kt, cache_v, cache_logf, state_hgrn, meta_tokens, w_in,
          b_forget, hg_lb_logits, hg_norm_gain, w_out, norm1_gain, norm2_gain, peer_w_query,
          sub_keys_t, peer_expert_u, peer_expert_v, final_norm_gain, constants,
          y_prompt, y_sample, new_k_prompt, new_v_prompt, new_logf_prompt, new_state_prompt,
          new_k_sample, new_v_sample, new_logf_sample, new_state_sample):
    with ExitStack() as ctx:
        def sb(name, shape, dt=F32):
            return ctx.enter_context(nc.sbuf_tensor(name, shape, dt))

        def sem(name):
            return ctx.enter_context(nc.semaphore(name))

        PA, PB, PC, PD = [ctx.enter_context(nc.psum_tensor(n, [P, D], F32)) for n in ("PA", "PB", "PC", "PD")]
        staged = nc.dram_tensor("staged", (TILES, P, ST_W), F32, kind="Internal").ap()
        x1_dram = nc.dram_tensor("x1_dram", (TILES, P, D), F32, kind="Internal").ap()
        h2_dram = nc.dram_tensor("h2_dram", (TILES, P, D), F32, kind="Internal").ap()

        arena = sb("arena", [P, DC * IN_W])
        w_in_sb = arena[:, :].rearrange("p (c n) -> p c n", c=DC)
        w_out_sb = arena[:, 0:DC * D].rearrange("p (c n) -> p c n", c=DC)
        w_query_sb = arena[:, DC * D:DC * 3 * D].rearrange("p (c n) -> p c n", c=DC)
        n_u, n_v = RING_U * D, RING_V * D
        ring_u = arena[:, 0:n_u].rearrange("p (r n) -> p r n", r=RING_U)
        ring_v = arena[:, n_u:n_u + n_v].rearrange("p (r n) -> p r n", r=RING_V)
        h2_all = arena[:, n_u + n_v:n_u + n_v + TILES * D]

        consts = sb("consts", [P, C_W])
        ident = consts[:, C_ID:C_ID + P]
        tri_tile = [consts[:, C_TRIS:C_TRIS + P]] + [consts[:, C_TRI:C_TRI + P]] * (TILES - 1)
        xt = sb("xt", [P, D])
        act = sb("act", [P, ST_W])
        keys_t = act[:, 0:2 * PH * NKEY]
        gain = sb("gain", [P, D])
        hgain = sb("hgain", [P, HW])
        idx_all = sb("idx_all", [P, GROUPS * GROUP], I32)
        gate_all = sb("gate_all", [P, GROUPS * GROUP])
        rows = sb("rows", [P, D])
        rows_t = sb("rows_t", [P, D])
        w1 = sb("w1", [P, 2048])
        w2 = sb("w2", [P, 2048])
        k_pr = sb("k_pr", [P, HEADS * PROMPT_KEYS])
        k_prompt = k_pr[:, :].rearrange("p (h k) -> p h k", h=HEADS)
        rows_t2 = [k_pr[:, 0:D], k_pr[:, D:2 * D]]
        lb = k_pr[:, 2 * D:2 * D + 2 * HW]
        lev = sb("lev", [P, TILES * D])
        k_sample = lev[:, 0:HEADS * SAMPLE_KEYS].rearrange("p (h k) -> p h k", h=HEADS)
        x1_all = lev[:, :]
        qa = sb("qa", [P, D])
        v_pr = sb("v_pr", [P, TILES, KV_W])
        state = sb("state", [P, 2, HW])
        small = sb("small", [P, 172])
        ss, rstd = small[:, 0:4], small[:, 4:8]
        b_fg = small[:, 8:16]
        fg_u, fg_a, fg_e, fg_l = (small[:, 16 + 8 * i:24 + 8 * i] for i in range(4))
        negmax = small[:, 48:56]
        psums = small[:, 56:64]
        carry = small[0:1, 64:72]
        e_end = small[:, 72:80]
        cache_lf = small[:, 80:112]
        gsum = small[:, 112:120]
        dots = small[:, 120:136]
        wgt = small[:, 136:152]
        acts = small[:, 152:168]
        newton = small[:, 168:172]

        tk_left = lev[:, 0:2048].rearrange("p (m n) -> p m n", n=NKEY)
        tk_val = lev[:, 2048:2304].rearrange("p (m k) -> p m k", k=TOPK)
        tk_idx = lev[:, 2304:2560].bitcast(U32).rearrange("p (m k) -> p m k", k=TOPK)
        tk_idxf = lev[:, 2560:2816].rearrange("p (m k) -> p m k", k=TOPK)
        top_val = lev[:, 2816:2944].rearrange("p (h k) -> p h k", k=TOPK)
        top_j = lev[:, 2944:3072].bitcast(U32).rearrange("p (h k) -> p h k", k=TOPK)
        j_part = [lev[:, 3072 + 128 * c:3200 + 128 * c].bitcast(U32) for c in range(2)]
        j_partf = [lev[:, 3328 + 128 * c:3456 + 128 * c] for c in range(2)]
        e_part = [lev[:, 3584 + 128 * c:3712 + 128 * c] for c in range(2)]
        idx_new = lev[:, 3840:3968].bitcast(I32)
        gate_new = lev[:, 3968:4096]

        const_in, gain_in, final_gain_in, lb_in, hgain_in = (sem(n) for n in (
            "const_in", "gain_in", "final_gain_in", "lb_in", "hgain_in"))
        x_clear, x_in, lb_less, lb_exp, h_ready, tr_done, ht_evac = (sem(n) for n in (
            "x_clear", "x_in", "lb_less", "lb_exp", "h_ready", "tr_done", "ht_evac"))
        fg_done, fg_used, fg_abs, fg_ln, proj_done, e_done, f_ready = (sem(n) for n in (
            "fg_done", "fg_used", "fg_abs", "fg_ln", "proj_done", "e_done", "f_ready"))
        staged_act, staged_dve, stored, dve_step, act_step = (sem(n) for n in (
            "staged_act", "staged_dve", "stored", "dve_step", "act_step"))
        cleared, past_in, act_in, wq_in, x2_in, keys_in = (sem(n) for n in (
            "cleared", "past_in", "act_in", "wq_in", "x2_in", "keys_in"))
        qk_turned, q_ready, k_ready, f_done, f_q, f_k = (sem(n) for n in (
            "qk_turned", "q_ready", "k_ready", "f_done", "f_q", "f_k"))
        sc_done, sc_max, p_done, pt_done, pt_evac, o_done, att_done = (sem(n) for n in (
            "sc_done", "sc_max", "p_done", "pt_done", "pt_evac", "o_done", "att_done"))
        hg_in, hg_in_evac, lev_ready, lev_exp, lev_mul, ke_done, ke_evac = (sem(n) for n in (
            "hg_in", "hg_in_evac", "lev_ready", "lev_exp", "lev_mul", "ke_done", "ke_evac"))
        gram_done, at_ready, ho_done, ho_evac, st_done, st_new, mix_ready = (sem(n) for n in (
            "gram_done", "at_ready", "ho_done", "ho_evac", "st_done", "st_new", "mix_ready"))
        mixt_done, mixt_evac, out_done, x1_ready, h2_ready, x1_saved, h2t_done, h2t_evac = (sem(n) for n in (
            "mixt_done", "mixt_evac", "out_done", "x1_ready", "h2_ready", "x1_saved", "h2t_done", "h2t_evac"))
        pq_done, pq_evac, ps_done, ps_read, less_max, gate_exp, top_done, idx_in = (sem(n) for n in (
            "pq_done", "pq_evac", "ps_done", "ps_read", "less_max", "gate_exp", "top_done", "idx_in"))
        b_in, u_free, v_free, gelu_done, wgt_done, diag_done, y_done, y_added = (sem(n) for n in (
            "b_in", "u_free", "v_free", "gelu_done", "wgt_done", "diag_done", "y_done", "y_added"))
        y_ready, y_saved, state_saved = (sem(n) for n in ("y_ready", "y_saved", "state_saved"))
        square_ready, root_ready = sem("square_ready"), sem("root_ready")
        w_in_in = [sem(f"w_in_in{c}") for c in range(DC)]
        u_in = [sem(f"u_in{i}") for i in range(RING_U)]
        v_in = [sem(f"v_in{i}") for i in range(RING_V)]

        def problems(t):
            if t:
                return [(0, P, k_prompt, N_META + P * t, [(0, N_META)] + [(N_META + P * b, P) for b in range(t)])]
            past = [(P * b, P) for b in range(PAST // P)]
            return [(0, N_SAMPLE, k_sample, SAMPLE_KEYS, past + [(PAST, N_SAMPLE)]),
                    (META0, N_META, k_prompt, N_META, [(0, N_META)])]

        def value_rows(t, q0, block, n, g):
            cols = slice(HD * g, HD * (g + 1))
            if t or q0 == META0:
                return v_pr[0:n, block, cols]
            if block < PAST // P:
                return rows_t[:, KV_W * block + HD * g:KV_W * block + HD * (g + 1)]
            return act[0:n, SV + HD * g:SV + HD * (g + 1)]

        def f_blocks(t):
            own = act[:, SLF:SLF + HEADS]
            if t:
                return [(own, 0, P, k_prompt, N_META + P * (t - 1), 0, True)]
            out = [(cache_lf[:, HEADS * b:HEADS * (b + 1)], 0, P, k_sample, P * b, None, b > 0)
                   for b in range(PAST // P)]
            return out + [(own, 0, N_SAMPLE, k_sample, PAST, 0, True), (own, META0, N_META, k_prompt, 0, META0, False)]

        def f_before(t):
            return sum(len(f_blocks(i)) for i in range(t))

        def fq_before(t):
            return sum(1 for i in range(t) for blk in f_blocks(i) if blk[5] is not None)

        def heads_before(t):
            return HEADS * sum(len(problems(i)) for i in range(t))

        def first_level(t):
            return 0 if t else 1

        def ends(t):
            return [(0, 0, P, PB)] if t else [(1, 0, N_SAMPLE, PB), (0, META0, N_META, PD)]

        def ends_before(t):
            return sum(len(ends(i)) for i in range(t))

        def stores_by(t):
            return 16 * (7 + 4 * t)

        def halves(ap, n, m):
            return ap.rearrange("p (a two m) -> p a two m", two=2, m=m)

        block = ctx.enter_context(nc.Block())

        @block.sync
        def _(sp):
            sp.dma_start(consts[:, :], constants).then_inc(const_in, 16)
            sp.dma_start(gain[:, :], norm1_gain[0].partition_broadcast(P)).then_inc(gain_in, 16)
            sp.dma_start(b_fg, b_forget[0].partition_broadcast(P)).then_inc(lb_in, 16)
            sp.dma_start(lb[:, 0:HW], hg_lb_logits[0].partition_broadcast(P)).then_inc(lb_in, 16)
            sp.dma_start(lb[:, HW:2 * HW], hg_lb_logits[1].partition_broadcast(P)).then_inc(lb_in, 16)
            sp.dma_start(hgain[:, :], hg_norm_gain[0].partition_broadcast(P)).then_inc(hgain_in, 16)
            sp.wait_ge(x_clear, 1)
            sp.dma_start(xt[0:N_SAMPLE, :], x_sample[0]).then_inc(x_in, 16)
            sp.dma_start(xt[META0:META1, :], meta_tokens).then_inc(x_in, 16)
            for c in range(DC):
                sp.dma_start(w_in_sb[:, c, :], w_in[0, c * P:(c + 1) * P, :]).then_inc(w_in_in[c], 16)
            for t in range(TILES):
                if t + 1 < TILES:
                    sp.wait_ge(h_ready, t + 1)
                    sp.dma_start(xt[:, :], x_prompt[0, t * P:(t + 1) * P, :]).then_inc(x_in, 16)
                sp.wait_ge(staged_act, 4 * (t + 1))
                sp.wait_ge(staged_dve, 4 * (t + 1))
                sp.dma_start(staged[t], act[:, :]).then_inc(stored, 16)
                for of_sample, of_prompt, at, n in ((new_k_sample, new_k_prompt, SK, KV_W),
                                                    (new_v_sample, new_v_prompt, SV, KV_W),
                                                    (new_logf_sample, new_logf_prompt, SLF, HEADS)):
                    if t:
                        first = N_META + (t - 1) * P
                        sp.dma_start(of_prompt[first:first + P], act[:, at:at + n]).then_inc(stored, 16)
                    else:
                        sp.dma_start(of_sample, act[0:N_SAMPLE, at:at + n]).then_inc(stored, 16)
                        sp.dma_start(of_prompt[0:N_META], act[META0:META1, at:at + n]).then_inc(stored, 16)

            sp.wait_ge(proj_done, 6 * TILES)
            sp.dma_start(gain[:, :], norm2_gain[0].partition_broadcast(P)).then_inc(gain_in, 16)
            for c in range(DC):
                sp.dma_start(w_out_sb[:, c, :], w_out[0, c * P:(c + 1) * P, :]).then_inc(wq_in, 16)
            for c in range(DC):
                sp.dma_start(w_query_sb[:, c, :], peer_w_query[0, c * P:(c + 1) * P, :]).then_inc(wq_in, 16)
            sp.wait_ge(stored, stores_by(TILES - 1))
            sp.wait_ge(cleared, 6)
            for par in range(2):
                sp.dma_start(k_sample[0:HD, par:HEADS:2, 0:PAST], cache_kt).then_inc(past_in, 16)
            sp.dma_start(rows_t[:, :].rearrange("p (b n) -> p b n", n=KV_W),
                         cache_v.rearrange("(b p) n -> p b n", p=P)).then_inc(past_in, 16)
            sp.dma_start(cache_lf.rearrange("p (b h) -> p b h", h=HEADS),
                         cache_logf.rearrange("(b p) h -> p b h", p=P)).then_inc(past_in, 16)
            sp.dma_start(state[:, 1, :].rearrange("p (h v) -> p h v", h=HG),
                         state_hgrn.rearrange("h k v -> k h v")).then_inc(past_in, 16)
            sp.dma_start(v_pr[0:N_META, 0, :], staged[0, META0:META1, SV:SV + KV_W]).then_inc(past_in, 16)
            for t in range(1, TILES):
                sp.dma_start(v_pr[:, t, :], staged[t, :, SV:SV + KV_W]).then_inc(past_in, 16)
            for t in range(TILES):
                if t:
                    sp.wait_ge(ps_done, t)
                    sp.wait_ge(x1_saved, 32 * t)
                sp.dma_start(act[:, :], staged[t]).then_inc(act_in, 16)
                if t:
                    sp.dma_start(xt[:, :], x_prompt[0, (t - 1) * P:t * P, :]).then_inc(x2_in, 16)
                else:
                    sp.dma_start(xt[0:N_SAMPLE, :], x_sample[0]).then_inc(x2_in, 16)
                    sp.dma_start(xt[META0:META1, :], meta_tokens).then_inc(x2_in, 16)
                sp.wait_ge(mix_ready, t + 1)
                sp.wait_ge(st_done, ends_before(t + 1))
                sp.dma_start(keys_t, sub_keys_t).then_inc(keys_in, 16)
                if t == 0:
                    sp.wait_ge(st_new, 1)
                    sp.dma_start(new_state_sample.rearrange("h k v -> k h v"),
                                 state[:, 1, :].rearrange("p (h v) -> p h v", h=HG)).then_inc(state_saved, 16)
                sp.wait_ge(x1_ready, t + 1)
                sp.dma_start(x1_dram[t], xt[:, :]).then_inc(x1_saved, 16)
                sp.wait_ge(h2_ready, t + 1)
                sp.dma_start(h2_dram[t], rows[:, :]).then_inc(x1_saved, 16)
                if t == 0:
                    sp.wait_ge(top_done, 1)
                    half = SLOTS // 2
                    for lo in (0, half):
                        sp.dma_start(idx_all[lo:lo + half, 0:half], idx_new[0:half, lo:lo + half]).then_inc(idx_in, 16)
                        sp.dma_start(gate_all[lo:lo + half, 0:half], gate_new[0:half, lo:lo + half]).then_inc(idx_in, 16)
            sp.wait_ge(st_new, ends_before(TILES))
            sp.dma_start(new_state_prompt.rearrange("h k v -> k h v"),
                         state[:, 0, :].rearrange("p (h v) -> p h v", h=HG)).then_inc(state_saved, 16)

            sp.wait_ge(pq_done, 2 * TILES)
            sp.wait_ge(x1_saved, 32 * TILES)
            sp.dma_start(rows[:, :], final_norm_gain.partition_broadcast(P)).then_inc(final_gain_in, 16)
            for t in range(1, TILES):
                sp.dma_start(h2_all[:, t * D:(t + 1) * D], h2_dram[t]).then_inc(b_in, 16)
            for lo in (0, N_SAMPLE):
                sp.dma_start(h2_all[lo:lo + N_SAMPLE, 0:D], h2_dram[0, 0:N_SAMPLE]).then_inc(b_in, 16)
            sp.wait_ge(top_done, TILES)
            for t in range(TILES):
                sp.dma_start(x1_all[:, t * D:(t + 1) * D], x1_dram[t]).then_inc(b_in, 16)
            for t in range(TILES):
                sp.wait_ge(y_ready, t + 1)
                if t:
                    sp.dma_start(y_prompt[0, (t - 1) * P:t * P, :], x1_all[:, t * D:(t + 1) * D]).then_inc(y_saved, 16)
                else:
                    sp.dma_start(y_sample[0], x1_all[0:N_SAMPLE, 0:D]).then_inc(y_saved, 16)
            sp.wait_ge(y_saved, 16 * TILES)
            sp.wait_ge(state_saved, 32)

        @block.gpsimd
        def _(pool):
            pool.wait_ge(top_done, TILES)
            pool.wait_ge(idx_in, 64)

            def gather(k, table, ring, depth, free, arrived):
                pool.wait_ge(free, k + 1)
                pool.indirect_dma_start(ring[:, k % depth, :], None, table[0],
                                        bass.IndirectOffsetOnAxis(ap=idx_all[:, k:k + 1], axis=0)
                                        ).then_inc(arrived[k % depth], 16)

            for k in range(GROUP):
                gather(k, peer_expert_u, ring_u, RING_U, u_free, u_in)
            for k in range(GROUPS * GROUP):
                if k + GROUP < GROUPS * GROUP:
                    gather(k + GROUP, peer_expert_u, ring_u, RING_U, u_free, u_in)
                gather(k, peer_expert_v, ring_v, RING_V, v_free, v_in)

        @block.scalar
        def _(eng):
            steps = [0]

            def link(ins):
                steps[0] += 1
                ins.then_inc(act_step, 1)
                eng.wait_ge(act_step, steps[0])

            roots = [0]

            def inverse_root(n):
                roots[0] += 1
                eng.wait_ge(square_ready, roots[0])
                link(eng.activation(rstd[:, 0:n], ss[:, 0:n], ACT.Ln))
                eng.activation(rstd[:, 0:n], rstd[:, 0:n], ACT.Exp, scale=-0.5).then_inc(root_ready, 1)

            eng.wait_ge(lb_less, 1)
            eng.activation(lb, lb, ACT.Exp).then_inc(lb_exp, 1)
            inverse_root(1)

            def turn_evac(t):
                eng.wait_ge(tr_done, t + 1)
                if t >= 2:
                    eng.wait_ge(proj_done, 6 * (t - 1))
                eng.activation(rows_t2[t % 2], PA[:, :], ACT.Copy).then_inc(ht_evac, 1)

            turn_evac(0)
            for t in range(TILES):
                eng.wait_ge(fg_abs, t + 1)
                link(eng.activation(fg_e, fg_a, ACT.Exp, scale=-1.0))
                eng.activation(fg_l, fg_e, ACT.Ln, bias=1.0).then_inc(fg_ln, 1)
                if t + 1 < TILES:
                    inverse_root(1)
                if t:
                    eng.wait_ge(stored, stores_by(t - 1))
                eng.wait_ge(proj_done, 6 * t + 1)
                eng.activation(act[:, SQ:SQ + 512], PB[:, 0:512], ACT.Copy).then_inc(staged_act, 1)
                eng.wait_ge(proj_done, 6 * t + 2)
                eng.activation(act[:, SK:SK + 512], PB[:, 512:1024], ACT.Copy).then_inc(staged_act, 1)
                if t + 1 < TILES:
                    turn_evac(t + 1)
                eng.wait_ge(proj_done, 6 * t + 3)
                if t:
                    eng.wait_ge(staged_dve, 4 * t)
                eng.activation(w2[:, 0:512], PC[:, 0:512], ACT.Exp, scale=-1.0).then_inc(e_done, 1)
                eng.wait_ge(proj_done, 6 * t + 4)
                if t:
                    eng.wait_ge(staged_act, 4 * t)
                eng.activation(w2[:, 512:1024], PC[:, 512:1024], ACT.Exp, scale=-1.0).then_inc(e_done, 1)
                eng.wait_ge(f_ready, t + 1)
                eng.activation(act[:, SHL:SHL + 512], w2[:, 512:1024], ACT.Ln).then_inc(staged_act, 1)
                eng.wait_ge(proj_done, 6 * t + 5)
                eng.activation(act[:, SHI:SHI + 512], PD[:, 0:512], ACT.Copy).then_inc(staged_act, 1)
                eng.wait_ge(proj_done, 6 * t + 6)
                eng.activation(w2[:, 1024:1536], PD[:, 512:1024], ACT.Exp, scale=-1.0).then_inc(e_done, 1)

            for t in range(TILES):
                eng.wait_ge(qk_turned, t + 1)
                if t == 0:
                    eng.wait_ge(cleared, 6)
                eng.activation(qa[0:HD, :], PA[0:HD, :], ACT.Copy, scale=SCALE).then_inc(q_ready, 1)
                for b, (_, _, n, _, _, q0, _) in enumerate(f_blocks(t)):
                    if q0 is not None:
                        eng.wait_ge(f_k, 2 * (f_before(t) + b + 1))
                        eng.activation(qa[64:65, :].rearrange("p (h q) -> p h q", h=HEADS)[:, :, q0:q0 + n],
                                       PC[0:1, :].rearrange("p (h q) -> p h q", h=HEADS)[:, :, 0:n],
                                       ACT.Copy).then_inc(f_q, 1)

                def exponentials(a, q, h):
                    _, m, _, n, _ = q
                    eng.wait_ge(sc_max, a + 1)
                    if a >= 2:
                        eng.wait_ge(pt_done, a - 1)
                    eng.activation(w1[0:m, D * (a % 2):D * (a % 2) + n], (PA, PB)[a % 2][0:m, 0:n], ACT.Exp,
                                   bias=negmax[0:m, h:h + 1], accum_out=psums[0:m, h:h + 1]).then_inc(p_done, 1)

                def turned(a, q):
                    _, m, _, _, blocks = q
                    eng.wait_ge(pt_done, a + 1)
                    if a >= 2:
                        eng.wait_ge(o_done, a - 1)
                    src = PC[:, 0:5 * P].rearrange("p (b q) -> p b q", q=P)
                    dst = w2[:, D * (a % 2):D * (a % 2) + 5 * P].rearrange("p (b q) -> p b q", q=P)
                    whole = [i for i, (_, k) in enumerate(blocks) if k == P]
                    short = [(i, k) for i, (_, k) in enumerate(blocks) if k < P][0]
                    if whole:
                        eng.activation(dst[:, whole[0]:whole[-1] + 1, 0:m], src[:, whole[0]:whole[-1] + 1, 0:m],
                                       ACT.Copy).then_inc(pt_evac, 1)
                    i, k = short
                    eng.activation(dst[0:k, i, 0:m], src[0:k, i, 0:m], ACT.Copy).then_inc(pt_evac, 1 if whole else 2)

                a = heads_before(t)
                for n_q, q in enumerate(problems(t)):
                    if n_q:
                        eng.wait_ge(att_done, 1)
                    for h in range(HEADS):
                        exponentials(a + h, q, h)
                        if h:
                            turned(a + h - 1, q)
                    turned(a + HEADS - 1, q)
                    a += HEADS

                eng.wait_ge(hg_in, t + 1)
                eng.activation(w1[:, 0:D], PA[:, :], ACT.Copy).then_inc(hg_in_evac, 1)
                eng.activation(w1[:, D:D + HW], PB[:, 0:HW], ACT.Copy).then_inc(hg_in_evac, 1)
                eng.wait_ge(lev_ready, t + 1)
                exps = lev[:, first_level(t) * HW:(NL + 2) * HW]
                eng.activation(exps, exps, ACT.Exp).then_inc(lev_exp, 1)
                eng.wait_ge(ke_done, t + 1)
                eng.activation(w2[:, 0:HW], PB[:, HW:2 * HW], ACT.Copy).then_inc(ke_evac, 1)
                eng.wait_ge(ho_done, HG * (t + 1))
                eng.activation(w1[:, 0:HW], PD[:, HW:2 * HW], ACT.Copy).then_inc(ho_evac, 1)
                inverse_root(HG)
                eng.wait_ge(mixt_done, t + 1)
                eng.activation(rows_t[:, :], PA[:, :], ACT.Copy).then_inc(mixt_evac, 1)
                inverse_root(1)
                eng.wait_ge(h2t_done, t + 1)
                eng.activation(rows_t[:, :], PA[:, :], ACT.Copy).then_inc(h2t_evac, 1)
                for n, psum in enumerate((PC, PD)):
                    eng.wait_ge(pq_done, 2 * t + n + 1)
                    eng.activation(w1[:, D * n:D * (n + 1)], psum[:, :], ACT.Copy).then_inc(pq_evac, 1)
                eng.wait_ge(less_max, t + 1)
                eng.activation(gate_new, gate_new, ACT.Exp).then_inc(gate_exp, 1)

            def group(n, base):
                eng.wait_ge(u_free, n * GROUP + (RING_U + GROUP))
                eng.activation(acts, dots, ACT.Gelu).then_inc(gelu_done, 1)
                eng.wait_ge(wgt_done, n + 1)
                eng.wait_ge(v_free, n * GROUP + RING_V)
                for j in range(GROUP):
                    eng.activation(w1[:, j * P:(j + 1) * P], base, ACT.Copy,
                                   scale=wgt[:, j:j + 1]).then_inc(diag_done, 1)

            eng.wait_ge(idx_in, 64)
            with eng.Fori(0, S_GROUPS) as n:
                group(n, consts[:, C_FOLD:C_FOLD + P])
            with eng.Fori(S_GROUPS, GROUPS) as n:
                group(n, ident)
            for t in range(TILES):
                inverse_root(1)

        @block.tensor
        def _(pe):
            pe.wait_ge(const_in, 16)

            def turn_rows(t):
                pe.wait_ge(h_ready, t + 1)
                if t:
                    pe.wait_ge(ht_evac, t)
                    pe.wait_ge(fg_used, t)
                for c in range(DC):
                    last = pe.transpose(PA[:, c * P:(c + 1) * P], rows[:, c * P:(c + 1) * P], ident)
                last.then_inc(tr_done, 1)

            group_psum = [PB[:, 0:512], PB[:, 512:1024], PC[:, 0:512], PC[:, 512:1024], PD[:, 0:512], PD[:, 512:1024]]
            turn_rows(0)
            for t in range(TILES):
                pe.wait_ge(ht_evac, t + 1)
                frees = [(staged_act, 4 * t - 3), (staged_act, 4 * t - 2), (staged_dve, 4 * t - 2),
                         (e_done, 3 * t - 1), (staged_act, 4 * t), (staged_dve, 4 * t)]

                def columns(out, first, n, done):
                    for c in range(DC):
                        if t == 0:
                            pe.wait_ge(w_in_in[c], 16)
                        last = pe.matmul(out, rows_t2[t % 2][:, c * P:(c + 1) * P], w_in_sb[:, c, first:first + n],
                                         start=(c == 0), stop=(c == DC - 1))
                    last.then_inc(done, 1)

                columns(PA[:, 0:HEADS], FG0, HEADS, fg_done)
                for g, first in enumerate(GROUP_COLS):
                    if t:
                        pe.wait_ge(*frees[g])
                    columns(group_psum[g], first, 512, proj_done)
                    if g == G_KV and t + 1 < TILES:
                        turn_rows(t + 1)

            for t in range(TILES):
                pe.wait_ge(act_in, 16 * (t + 1))
                if t:
                    pe.wait_ge(ps_read, t)
                else:
                    pe.wait_ge(staged_act, 4 * TILES)
                    pe.wait_ge(staged_dve, 4 * TILES)
                for h in range(HEADS):
                    pe.transpose(PA[0:HD, h * P:(h + 1) * P], act[:, SQ + HD * h:SQ + HD * (h + 1)], ident)
                for g in range(KV_HEADS):
                    last = pe.transpose(PB[0:HD, g * P:(g + 1) * P], act[:, SK + HD * g:SK + HD * (g + 1)], ident)
                last.then_inc(qk_turned, 1)
                if t == 0:
                    pe.wait_ge(past_in, 16 * (6 + TILES - 1))
                for b, (gates, r0, n, _, _, _, goes_on) in enumerate(f_blocks(t)):
                    i = f_before(t) + b
                    if i:
                        pe.wait_ge(f_k, 2 * i)
                    if fq_before(t) + (b == len(f_blocks(t)) - 1 and t == 0):
                        pe.wait_ge(f_q, fq_before(t) + (b == len(f_blocks(t)) - 1 and t == 0))
                    if t:
                        pe.wait_ge(pq_evac, 2 * t)
                    for h in range(HEADS):
                        out = PC[0:1, h * P:h * P + n]
                        last = pe.matmul(out, gates[r0:r0 + n, h:h + 1],
                                         consts[r0:r0 + n, C_TRI + r0:C_TRI + r0 + n], start=True, stop=not goes_on)
                        if goes_on:
                            last = pe.matmul(out, carry[:, h:h + 1], consts[0:1, C_ONE:C_ONE + n], start=False, stop=True)
                    last.then_inc(f_done, 1)

                pe.wait_ge(q_ready, t + 1)
                pe.wait_ge(k_ready, 2 * (t + 1))
                pe.wait_ge(f_q, fq_before(t + 1))
                pe.wait_ge(f_k, 2 * f_before(t + 1))

                def scores(a, q, h):
                    q0, m, keys, n, _ = q
                    if a >= 2:
                        pe.wait_ge(p_done, a - 1)
                    for k0 in range(0, n, 512):
                        k1 = min(n, k0 + 512)
                        last = pe.matmul((PA, PB)[a % 2][0:m, k0:k1], qa[:, h * P + q0:h * P + q0 + m],
                                         keys[:, h, k0:k1], start=True, stop=True)
                    last.then_inc(sc_done, 1)

                def values(a, q, h):
                    q0, m, _, _, blocks = q
                    pe.wait_ge(p_done, a + 1)
                    if a:
                        pe.wait_ge(pt_evac, 2 * a)
                    for i, (k0, k) in enumerate(blocks):
                        p0 = D * (a % 2) + k0
                        last = pe.transpose(PC[0:k, i * P:i * P + m], w1[0:m, p0:p0 + k], ident[0:m, 0:m])
                    last.then_inc(pt_done, 1)
                    pe.wait_ge(pt_evac, 2 * (a + 1))
                    for i, (k0, k) in enumerate(blocks):
                        at = D * (a % 2) + i * P
                        last = pe.matmul(PD[0:m, h * HD:(h + 1) * HD], w2[0:k, at:at + m],
                                         value_rows(t, q0, i, k, h // (HEADS // KV_HEADS)),
                                         start=(i == 0), stop=(i == len(blocks) - 1))
                    last.then_inc(o_done, 1)

                a = heads_before(t)
                for n_q, q in enumerate(problems(t)):
                    if n_q:
                        pe.wait_ge(att_done, 1)
                    for h in range(HEADS):
                        scores(a + h, q, h)
                        if h:
                            values(a + h - 1, q, h - 1)
                    values(a + HEADS - 1, q, HEADS - 1)
                    a += HEADS

                pe.wait_ge(p_done, a)
                tri = consts[:, (C_TRI if t else C_TRIS):(C_TRI if t else C_TRIS) + P]
                for h in range(HG):
                    cols = slice(h * HK, (h + 1) * HK)
                    pe.matmul(PA[:, cols], act[:, SHL + h * HK:SHL + (h + 1) * HK], tri, start=True, stop=True)
                for h in range(HG):
                    pe.transpose(PA[:, HW + h * HK:HW + (h + 1) * HK], act[:, SHQ + h * HK:SHQ + (h + 1) * HK], ident)
                for h in range(HG):
                    last = pe.transpose(PB[:, h * HK:(h + 1) * HK], act[:, SHK + h * HK:SHK + (h + 1) * HK], ident)
                last.then_inc(hg_in, 1)
                pe.wait_ge(hg_in_evac, 2 * (t + 1))
                pe.wait_ge(lev_mul, t + 1)
                for h in range(HG):
                    last = pe.transpose(PB[:, HW + h * HK:HW + (h + 1) * HK],
                                        lev[:, NL * HW + h * HK:NL * HW + (h + 1) * HK], ident)
                last.then_inc(ke_done, 1)

                def grams(h):
                    if h >= 2:
                        pe.wait_ge(at_ready, HG * t + h - 1)
                    psum = (PC, PA)[h % 2]
                    for l in range(first_level(t), NL):
                        both = lev[:, l * HW + h * HK:l * HW + (h + 1) * HK]
                        pe.matmul(psum[:, l * P:(l + 1) * P], both, both, start=True, stop=True)
                    pe.matmul(psum[:, NL * P:(NL + 1) * P], w1[:, D + h * HK:D + (h + 1) * HK],
                              w1[:, HW + h * HK:HW + (h + 1) * HK], start=True, stop=True).then_inc(gram_done, 1)

                def outputs(h):
                    pe.wait_ge(at_ready, HG * t + h + 1)
                    m = P if t else N_SAMPLE
                    col = HW + h * HK
                    pe.matmul(PD[:, col:col + HK], w1[:, D + HW + h * P:D + HW + (h + 1) * P],
                              act[:, SHI + h * HK:SHI + (h + 1) * HK], start=True, stop=False, skip_group_check=True)
                    pe.matmul(PD[0:m, col:col + HK], lev[:, (NL + 1) * HW + h * HK:(NL + 1) * HW + h * HK + m],
                              state[:, 0 if t else 1, h * HK:(h + 1) * HK], start=False, stop=True,
                              skip_group_check=True).then_inc(ho_done, 1)

                if t:
                    pe.wait_ge(st_new, ends_before(t))
                for h in range(HG):
                    grams(h)
                    if h:
                        outputs(h - 1)
                outputs(HG - 1)
                pe.wait_ge(ke_evac, t + 1)
                pe.wait_ge(att_done, heads_before(t + 1) // HEADS)
                for _, r0, n, psum in ends(t):
                    for h in range(HG):
                        last = pe.matmul(psum[:, h * HK:(h + 1) * HK], w2[r0:r0 + n, h * HK:(h + 1) * HK],
                                         act[r0:r0 + n, SHI + h * HK:SHI + (h + 1) * HK], start=True, stop=True)
                    last.then_inc(st_done, 1)

                pe.wait_ge(mix_ready, t + 1)
                for c in range(DC):
                    last = pe.transpose(PA[:, c * P:(c + 1) * P], rows[:, c * P:(c + 1) * P], ident)
                last.then_inc(mixt_done, 1)
                pe.wait_ge(mixt_evac, t + 1)
                pe.wait_ge(st_new, ends_before(t + 1))
                if t == 0:
                    pe.wait_ge(wq_in, 16 * 2 * DC)
                for half in range(2):
                    for c in range(DC):
                        last = pe.matmul(PB[:, half * 512:(half + 1) * 512], rows_t[:, c * P:(c + 1) * P],
                                         w_out_sb[:, c, half * 512:(half + 1) * 512], start=(c == 0), stop=(c == DC - 1))
                last.then_inc(out_done, 1)
                pe.wait_ge(h2_ready, t + 1)
                for c in range(DC):
                    last = pe.transpose(PA[:, c * P:(c + 1) * P], rows[:, c * P:(c + 1) * P], ident)
                last.then_inc(h2t_done, 1)
                pe.wait_ge(h2t_evac, t + 1)
                for n, psum in enumerate((PC, PD)):
                    if n:
                        pe.wait_ge(ho_evac, t + 1)
                    for m in range(PH):
                        first = (n * PH + m) * P
                        for c in range(DC):
                            last = pe.matmul(psum[:, m * P:(m + 1) * P], w_query_sb[:, c, first:first + P],
                                             rows_t[:, c * P:(c + 1) * P], start=(c == 0), stop=(c == DC - 1))
                    last.then_inc(pq_done, 1)
                pe.wait_ge(keys_in, 16 * (t + 1))
                pe.wait_ge(x1_ready, t + 1)
                for n, psum in enumerate((PA, PB)):
                    pe.wait_ge(pq_evac, 2 * t + n + 1)
                    for m in range(PH):
                        i = n * PH + m
                        last = pe.matmul(psum[:, m * NKEY:(m + 1) * NKEY], w1[:, i * P:(i + 1) * P],
                                         keys_t[:, i * NKEY:(i + 1) * NKEY], start=True, stop=True)
                last.then_inc(ps_done, 1)

            pe.wait_ge(ps_read, TILES)
            with pe.Fori(0, GROUPS) as n:
                pe.wait_ge(y_added, n)
                for j in range(GROUP):
                    pe.wait_ge(v_in[j % RING_V], n * (16 * GROUP // RING_V) + 16 * (j // RING_V + 1))
                    pe.wait_ge(diag_done, n * GROUP + (j + 1))
                    for half in range(2):
                        last = pe.matmul(PA[:, half * 512:(half + 1) * 512], w1[:, j * P:(j + 1) * P],
                                         ring_v[:, j % RING_V, half * 512:(half + 1) * 512],
                                         start=(j == 0), stop=(j == GROUP - 1))
                    last.then_inc(v_free, 1)

        @block.vector
        def _(eng):
            steps = [0]

            def link(ins):
                steps[0] += 1
                ins.then_inc(dve_step, 1)
                eng.wait_ge(dve_step, steps[0])

            roots = [0]

            def inverse_root(n, width):
                roots[0] += 1
                x, y, z = ss[:, 0:n], rstd[:, 0:n], newton[:, 0:n]
                eng.tensor_scalar(x, x, 1.0 / width, EPS, ALU.mult, ALU.add).then_inc(square_ready, 1)
                eng.wait_ge(root_ready, roots[0])
                link(eng.tensor_tensor(z, y, y, ALU.mult))
                link(eng.tensor_tensor(z, z, x, ALU.mult))
                link(eng.tensor_scalar(z, z, -0.5, 1.5, ALU.mult, ALU.add))
                link(eng.tensor_tensor(y, y, z, ALU.mult))

            def mean_square(src, scratch):
                link(eng.tensor_tensor_reduce(scratch, src, src, 1.0, 0.0, ALU.mult, ALU.add, ss[:, 0:1]))
                inverse_root(1, D)

            eng.memset(xt[:, :], 0.0).then_inc(x_clear, 1)
            eng.wait_ge(lb_in, 48)
            link(eng.tensor_tensor(act[:, 0:HW], lb[:, 0:HW], lb[:, HW:2 * HW], ALU.max))
            link(eng.tensor_tensor(lb[:, 0:HW], lb[:, 0:HW], act[:, 0:HW], ALU.subtract))
            eng.tensor_tensor(lb[:, HW:2 * HW], lb[:, HW:2 * HW], act[:, 0:HW], ALU.subtract).then_inc(lb_less, 1)
            eng.wait_ge(lb_exp, 1)
            link(eng.tensor_tensor(act[:, 0:HW], lb[:, 0:HW], lb[:, HW:2 * HW], ALU.add))
            link(eng.reciprocal(act[:, 0:HW], act[:, 0:HW]))
            link(eng.tensor_tensor(lb[:, 0:HW], lb[:, 0:HW], act[:, 0:HW], ALU.mult))
            link(eng.tensor_scalar(lb[:, HW:2 * HW], lb[:, 0:HW], -1.0, 1.0, ALU.mult, ALU.add))

            def normalise(t):
                eng.wait_ge(x_in, 16 * (t + 2))
                mean_square(xt[:, :], w1[:, 0:D])
                if t:
                    eng.wait_ge(tr_done, t)
                eng.scalar_tensor_tensor(out=rows[:, :], in0=xt[:, :], scalar=rstd[:, 0:1], in1=gain[:, :],
                                         op0=ALU.mult, op1=ALU.mult).then_inc(h_ready, 1)

            eng.wait_ge(gain_in, 16)
            normalise(0)
            for t in range(TILES):
                eng.wait_ge(fg_done, t + 1)
                eng.tensor_tensor(fg_u, PA[:, 0:HEADS], b_fg, ALU.add).then_inc(fg_used, 1)
                eng.wait_ge(fg_used, t + 1)
                eng.scalar_tensor_tensor(out=fg_a, in0=fg_u, scalar=-1.0, in1=fg_u, op0=ALU.mult, op1=ALU.max).then_inc(fg_abs, 1)
                if t + 1 < TILES:
                    normalise(t + 1)
                if t:
                    eng.wait_ge(stored, stores_by(t - 1))
                eng.wait_ge(fg_ln, t + 1)
                eng.scalar_tensor_tensor(out=act[:, SLF:SLF + HEADS], in0=fg_u, scalar=0.0, in1=fg_l,
                                         op0=ALU.min, op1=ALU.subtract).then_inc(staged_dve, 1)

                def sigmoid(e):
                    link(eng.tensor_scalar(e, e, 1.0, None, ALU.add))
                    link(eng.reciprocal(e, e))

                eng.wait_ge(e_done, 3 * t + 1)
                sigmoid(w2[:, 0:512])
                eng.tensor_tensor(act[:, SHQ:SHQ + 512], PC[:, 0:512], w2[:, 0:512], ALU.mult).then_inc(staged_dve, 1)
                eng.wait_ge(e_done, 3 * t + 2)
                f = w2[:, 512:1024]
                sigmoid(f)
                link(eng.tensor_tensor(f, f, lb[:, HW:2 * HW], ALU.mult))
                eng.tensor_tensor(f, f, lb[:, 0:HW], ALU.add).then_inc(f_ready, 1)
                eng.wait_ge(f_ready, t + 1)
                eng.tensor_scalar(act[:, SHK:SHK + 512], f, -1.0, 1.0, ALU.mult, ALU.add).then_inc(staged_dve, 1)
                eng.wait_ge(e_done, 3 * t + 3)
                sigmoid(w2[:, 1024:1536])
                eng.tensor_tensor(act[:, SHG:SHG + 512], PD[:, 512:1024], w2[:, 1024:1536],
                                  ALU.mult).then_inc(staged_dve, 1)

            eng.wait_ge(proj_done, 6 * TILES)
            for i, buf in enumerate((k_pr, lev, qa)):
                eng.memset(buf[64:P, :], 0.0).then_inc(cleared, 1)
            eng.wait_ge(cleared, 3)
            for buf, row in ((k_pr, 64), (lev, 64), (qa, 96)):
                eng.memset(buf[row:row + 1, :], 1.0).then_inc(cleared, 1)
            link(eng.memset(state[:, 0, :], 0.0))

            for t in range(TILES):
                eng.wait_ge(qk_turned, t + 1)
                turned = PB[0:HD, 0:KV_HEADS * P].rearrange("p (g q) -> p g q", q=P)
                eng.wait_ge(cleared, 6)
                for par in range(2):
                    if t:
                        first = N_META + P * (t - 1)
                        eng.tensor_copy(k_prompt[0:HD, par:HEADS:2, first:first + P], turned).then_inc(k_ready, 1)
                    else:
                        link(eng.tensor_copy(k_sample[0:HD, par:HEADS:2, PAST:SAMPLE_KEYS], turned[:, :, 0:N_SAMPLE]))
                        eng.tensor_copy(k_prompt[0:HD, par:HEADS:2, 0:N_META],
                                        turned[:, :, META0:META1]).then_inc(k_ready, 1)
                for b, (_, _, n, keys, first, _, _) in enumerate(f_blocks(t)):
                    eng.wait_ge(f_done, f_before(t) + b + 1)
                    sums = PC[0:1, :].rearrange("p (h q) -> p h q", h=HEADS)
                    eng.tensor_scalar(keys[96:97, :, first:first + n], sums[:, :, 0:n], -1.0, None,
                                      ALU.mult).then_inc(f_k, 1)
                    eng.tensor_copy(carry, sums[:, :, n - 1]).then_inc(f_k, 1)

                a = heads_before(t)
                for n_q, (q0, m, _, n, _) in enumerate(problems(t)):
                    for h in range(HEADS):
                        eng.wait_ge(sc_done, a + 1)
                        psum = (PA, PB)[a % 2]
                        for k0 in ([n - m] if n // 512 == (n - m) // 512 or n <= 512 else [n - m, 512]):
                            k1 = 512 if (n > 512 and k0 < 512) else n
                            j = k0 - (n - m)
                            link(eng.tensor_tensor(psum[0:m, k0:k1], psum[0:m, k0:k1],
                                                   consts[0:m, C_MASK + j:C_MASK + j + k1 - k0], ALU.add))
                        link(eng.tensor_reduce(negmax[0:m, h:h + 1], psum[0:m, 0:n], AX_X, ALU.max))
                        eng.tensor_scalar(negmax[0:m, h:h + 1], negmax[0:m, h:h + 1], -1.0, None,
                                          ALU.mult).then_inc(sc_max, 1)
                        a += 1
                    eng.wait_ge(p_done, a)
                    link(eng.reciprocal(psums[0:m, :], psums[0:m, :]))
                    eng.wait_ge(o_done, a)
                    if t and n_q == 0:
                        eng.wait_ge(x1_saved, 32 * t)
                        eng.wait_ge(h2t_done, t)
                    eng.tensor_tensor(rows[q0:q0 + m, 0:HW].rearrange("p (h d) -> p h d", d=HD),
                                      PD[0:m, 0:HW].rearrange("p (h d) -> p h d", d=HD),
                                      psums[0:m, :].unsqueeze(2).to_broadcast([m, HEADS, HD]),
                                      ALU.mult).then_inc(att_done, 1)

                eng.wait_ge(hg_in_evac, 2 * (t + 1))
                sums = w1[:, 0:HW]
                sums_h = sums.rearrange("p (h q) -> p h q", h=HG)
                if t == 0:
                    link(eng.memset(lev[:, NL * HW:(NL + 1) * HW], 0.0))
                for l in range(first_level(t), NL):
                    m = LEVELS[l]
                    out, src = halves(lev[:, l * HW:(l + 1) * HW], HW // (2 * m), m), halves(sums, HW // (2 * m), m)
                    mid = src[:, :, 0, m - 1:m].to_broadcast([P, HW // (2 * m), m])
                    eng.tensor_tensor(out[:, :, 0, :], mid, src[:, :, 0, :], ALU.subtract)
                    eng.tensor_tensor(out[:, :, 1, :], src[:, :, 1, :], mid, ALU.subtract)
                to_end = lev[:, NL * HW:(NL + 1) * HW].rearrange("p (h q) -> p h q", h=HG)
                for _, r0, n, _ in ends(t):
                    eng.tensor_tensor(to_end[:, :, r0:r0 + n],
                                      sums_h[:, :, r0 + n - 1:r0 + n].to_broadcast([P, HG, n]),
                                      sums_h[:, :, r0:r0 + n], ALU.subtract)
                eng.tensor_copy(lev[:, (NL + 1) * HW:(NL + 2) * HW], sums).then_inc(lev_ready, 1)
                eng.wait_ge(lev_exp, t + 1)
                queries, keys = w1[:, HW:2 * HW], w1[:, 2 * HW:3 * HW]
                for l in range(first_level(t), NL):
                    m = LEVELS[l]
                    both = halves(lev[:, l * HW:(l + 1) * HW], HW // (2 * m), m)
                    for side, what in ((0, keys), (1, queries)):
                        eng.tensor_tensor(both[:, :, side, :], both[:, :, side, :],
                                          halves(what, HW // (2 * m), m)[:, :, side, :], ALU.mult)
                eng.tensor_tensor(lev[:, NL * HW:(NL + 1) * HW], lev[:, NL * HW:(NL + 1) * HW], keys, ALU.mult)
                from_start = lev[:, (NL + 1) * HW:(NL + 2) * HW]
                if ends_before(t):
                    eng.wait_ge(st_new, ends_before(t))
                for i, (_, r0, n, _) in enumerate(ends(t)):
                    link(eng.tensor_copy(e_end[:, HG * i:HG * (i + 1)],
                                         from_start.rearrange("p (h q) -> p h q", h=HG)[:, :, r0 + n - 1]))
                eng.tensor_tensor(from_start, from_start, queries, ALU.mult).then_inc(lev_mul, 1)
                for h in range(HG):
                    eng.wait_ge(gram_done, HG * t + h + 1)
                    masked = w2[:, D:2 * D]
                    c0 = first_level(t) * P
                    link(eng.tensor_tensor(masked[:, c0:D], (PC, PA)[h % 2][:, c0:D],
                                           consts[:, C_LEV + c0:C_LEV + D], ALU.mult))
                    eng.tensor_reduce(w1[:, D + HW + h * P:D + HW + (h + 1) * P],
                                      masked[:, c0:D].rearrange("p (l q) -> p q l", q=P),
                                      AX_X, ALU.add).then_inc(at_ready, 1)
                    eng.wait_ge(at_ready, HG * t + h + 1)
                for i, (which, _, _, psum) in enumerate(ends(t)):
                    eng.wait_ge(ho_done, HG * (t + 1))
                    eng.wait_ge(st_done, ends_before(t) + i + 1)
                    for h in range(HG):
                        s = state[:, which, h * HK:(h + 1) * HK]
                        last = eng.scalar_tensor_tensor(out=s, in0=s, scalar=e_end[:, HG * i + h:HG * i + h + 1],
                                                        in1=psum[:, h * HK:(h + 1) * HK], op0=ALU.mult, op1=ALU.add)
                    last.then_inc(st_new, 1)
                eng.wait_ge(ho_evac, t + 1)
                eng.wait_ge(hgain_in, 16)
                o = w1[:, 0:HW]
                o_h = o.rearrange("p (h v) -> p h v", h=HG)
                link(eng.tensor_tensor(w2[:, D:D + HW], o, o, ALU.mult))
                link(eng.tensor_reduce(ss[:, 0:HG], w2[:, D:D + HW].rearrange("p (h v) -> p h v", h=HG), AX_X, ALU.add))
                inverse_root(HG, HK)
                link(eng.tensor_tensor(o_h, o_h, rstd[:, 0:HG].unsqueeze(2).to_broadcast([P, HG, HK]), ALU.mult))
                link(eng.tensor_tensor(o, o, hgain[:, :], ALU.mult))
                if t == 0:
                    link(eng.memset(rows[96:P, 0:HW], 0.0))
                eng.tensor_tensor(rows[:, HW:2 * HW], o, act[:, SHG:SHG + HW], ALU.mult).then_inc(mix_ready, 1)

                eng.wait_ge(out_done, t + 1)
                eng.wait_ge(x2_in, 16 * (t + 2))
                eng.tensor_tensor(xt[:, :], xt[:, :], PB[:, :], ALU.add).then_inc(x1_ready, 1)
                eng.wait_ge(x1_ready, t + 1)
                mean_square(xt[:, :], w2[:, 0:D])
                eng.wait_ge(mixt_done, t + 1)
                eng.wait_ge(gain_in, 32)
                eng.scalar_tensor_tensor(out=rows[:, :], in0=xt[:, :], scalar=rstd[:, 0:1], in1=gain[:, :],
                                         op0=ALU.mult, op1=ALU.mult).then_inc(h2_ready, 1)

                eng.wait_ge(ps_done, t + 1)
                if t == 1:
                    eng.wait_ge(idx_in, 64)
                scores = [(PA, PB)[i // PH][:, (i % PH) * NKEY:(i % PH + 1) * NKEY] for i in range(2 * PH)]

                def sixteen(values, left, val, idx, read=None):
                    n = len(values)
                    for i in range(n):
                        last = eng.max(val[:, i, 0:8], values[i])
                    link(last)
                    for i in range(n):
                        eng.max_index(idx[:, i, 0:8], val[:, i, 0:8], values[i])
                        last = eng.match_replace(left[i], val[:, i, 0:8], values[i], NEG)
                    link(last)
                    if read is not None:
                        eng.sem_inc(read, 1)
                    for i in range(n):
                        last = eng.max(val[:, i, 8:16], left[i])
                    link(last)
                    for i in range(n):
                        last = eng.max_index(idx[:, i, 8:16], val[:, i, 8:16], left[i])
                    link(last)

                sixteen(scores, [tk_left[:, i, :] for i in range(2 * PH)], tk_val, tk_idx, ps_read)
                cand = w1[:, :].rearrange("p (h i j) -> p h i j", h=PH, i=TOPK)
                val_h = tk_val.rearrange("p (h c) k -> p h c k", c=2)
                link(eng.tensor_tensor(cand, val_h[:, :, 0, :].unsqueeze(3).to_broadcast([P, PH, TOPK, TOPK]),
                                       val_h[:, :, 1, :].unsqueeze(2).to_broadcast([P, PH, TOPK, TOPK]), ALU.add))
                pairs = TOPK * TOPK
                sixteen([w1[:, h * pairs:(h + 1) * pairs] for h in range(PH)],
                        [w2[:, h * pairs:(h + 1) * pairs] for h in range(PH)], top_val, top_j)
                gates = gate_new.rearrange("p (h k) -> p h k", k=TOPK)
                eng.tensor_tensor(gates, top_val, top_val[:, :, 0:1].to_broadcast([P, PH, TOPK]),
                                  ALU.subtract).then_inc(less_max, 1)
                top_jf = lev[:, 2944:3072].bitcast(U32)
                link(eng.tensor_scalar(j_part[0], top_jf, 4, None, ALU.logical_shift_right))
                link(eng.tensor_scalar(j_part[1], top_jf, 15, None, ALU.bitwise_and))
                link(eng.tensor_copy(tk_idxf, tk_idx))
                idx_h = tk_idxf.rearrange("p (h c) k -> p h c k", c=2)
                same = w2[:, :].rearrange("p (h k i) -> p h k i", h=PH, i=TOPK)
                shape = [P, PH, TOPK, TOPK]
                for c in range(2):
                    link(eng.tensor_copy(j_partf[c], j_part[c]))
                    j = j_partf[c].rearrange("p (h k) -> p h k", k=TOPK)
                    iota = consts[:, C_IOTA:C_IOTA + TOPK].unsqueeze(1).unsqueeze(1)
                    link(eng.tensor_tensor(same, j.unsqueeze(3).to_broadcast(shape), iota.to_broadcast(shape),
                                           ALU.is_equal))
                    link(eng.tensor_tensor(same, same, idx_h[:, :, c, :].unsqueeze(2).to_broadcast(shape), ALU.mult))
                    link(eng.tensor_reduce(e_part[c].rearrange("p (h k) -> p h k", k=TOPK), same, AX_X, ALU.add))
                link(eng.scalar_tensor_tensor(out=e_part[0], in0=e_part[0], scalar=float(NKEY), in1=e_part[1],
                                              op0=ALU.mult, op1=ALU.add))
                first = (S_GROUPS + T_GROUPS * (t - 1)) * GROUP
                link(eng.tensor_copy(idx_all[:, first:first + SLOTS] if t else idx_new, e_part[0]))
                eng.wait_ge(gate_exp, t + 1)
                link(eng.tensor_reduce(gsum, gates, AX_X, ALU.add))
                link(eng.reciprocal(gsum, gsum))
                gates_to = gate_all[:, first:first + SLOTS].rearrange("p (h k) -> p h k", k=TOPK) if t else gates
                eng.tensor_tensor(gates_to, gates, gsum.unsqueeze(2).to_broadcast([P, PH, TOPK]),
                                  ALU.mult).then_inc(top_done, 1)

            eng.wait_ge(b_in, 16 * (2 * TILES + 1))
            eng.wait_ge(final_gain_in, 16)
            eng.sem_inc(u_free, RING_U)
            eng.sem_inc(v_free, RING_V)

            def tile_of(n):
                return bass.ds(((n + (T_GROUPS - S_GROUPS)) // T_GROUPS) * D, D)

            def dot(n, j):
                eng.wait_ge(u_in[j % RING_U], n * (16 * GROUP // RING_U) + 16 * (j // RING_U + 1))
                slot = ring_u[:, j % RING_U, :]
                eng.scalar_tensor_tensor(out=slot, in0=slot, scalar=1.0, in1=h2_all[:, tile_of(n)],
                                         op0=ALU.mult, op1=ALU.mult, accum_out=dots[:, j:j + 1]).then_inc(u_free, 1)

            def add_values(n):
                eng.wait_ge(v_free, n * GROUP + (RING_V + GROUP))
                rows_n = x1_all[:, tile_of(n)]
                eng.tensor_tensor(rows_n, rows_n, PA[:, :], ALU.add).then_inc(y_added, 1)

            def weights(n):
                eng.wait_ge(gelu_done, n + 1)
                eng.wait_ge(diag_done, n * GROUP)
                eng.tensor_tensor(wgt, acts, gate_all[:, bass.ds(n * GROUP, GROUP)], ALU.mult).then_inc(wgt_done, 1)

            for j in range(GROUP):
                dot(0, j)
            weights(0)
            with eng.Fori(1, GROUPS) as n:
                for j in range(GROUP):
                    dot(n, j)
                weights(n)
                add_values(n - 1)
            add_values(GROUPS - 1)
            eng.wait_ge(y_added, GROUPS)
            for t in range(TILES):
                x1 = x1_all[:, t * D:(t + 1) * D]
                mean_square(x1, w2[:, 0:D])
                eng.scalar_tensor_tensor(out=x1, in0=x1, scalar=rstd[:, 0:1], in1=rows[:, :],
                                         op0=ALU.mult, op1=ALU.mult).then_inc(y_ready, 1)


def constant_columns():
    import numpy as np
    r = np.arange(P)
    s, t = r[:, None], r[None, :]
    upper = (s <= t)
    cols = [s == t, (s % N_SAMPLE == t) & (t < N_SAMPLE), upper, upper & (s // 64 == t // 64),
            np.where(t <= s, 0.0, NEG)]
    for m in LEVELS:
        cols.append((s // (2 * m) == t // (2 * m)) & (s // m % 2 == 0) & (t // m % 2 == 1))
    cols.append(s == t)
    cols.append(np.broadcast_to(np.arange(TOPK)[None, :], (P, TOPK)))
    cols.append(np.ones((P, P)))
    return np.concatenate([np.asarray(c, np.float32) for c in cols], axis=1)


_OUTS = [("y_prompt", (1, SEQ, D)), ("y_sample", (1, N_SAMPLE, D)),
         ("new_k_prompt", (N_META + SEQ, KV_W)), ("new_v_prompt", (N_META + SEQ, KV_W)),
         ("new_logf_prompt", (N_META + SEQ, HEADS)), ("new_state_prompt", (HG, HK, HK)),
         ("new_k_sample", (N_SAMPLE, KV_W)), ("new_v_sample", (N_SAMPLE, KV_W)),
         ("new_logf_sample", (N_SAMPLE, HEADS)), ("new_state_sample", (HG, HK, HK))]


def kernel(x_prompt, x_sample, cache_k, cache_v, cache_logf, state_hgrn, meta_tokens, w_in, b_forget,
           hg_lb_logits, hg_norm_gain, w_out, norm1_gain, norm2_gain, peer_w_query, peer_sub_keys,
           peer_expert_u, peer_expert_v, final_norm_gain):
    import numpy as np
    import concourse.bacc as bacc
    from concourse.bass_utils import run_bass_kernel_spmd

    def plain(a):
        return np.ascontiguousarray(np.asarray(a))

    cache_k, cache_v = plain(cache_k), plain(cache_v)
    arrays = {
        "x_prompt": plain(x_prompt), "x_sample": plain(x_sample),
        "cache_kt": plain(cache_k[0, 0].transpose(2, 1, 0)),
        "cache_v": cache_v.reshape(PAST, KV_W), "cache_logf": plain(cache_logf)[0, 0],
        "state_hgrn": plain(state_hgrn)[0, 0], "meta_tokens": plain(meta_tokens), "w_in": plain(w_in),
        "b_forget": plain(b_forget), "hg_lb_logits": plain(hg_lb_logits), "hg_norm_gain": plain(hg_norm_gain),
        "w_out": plain(w_out), "norm1_gain": plain(norm1_gain), "norm2_gain": plain(norm2_gain),
        "peer_w_query": plain(peer_w_query),
        "sub_keys_t": plain(plain(peer_sub_keys)[0].reshape(2 * PH, NKEY, P).transpose(2, 0, 1)).reshape(P, 2 * PH * NKEY),
        "peer_expert_u": plain(peer_expert_u), "peer_expert_v": plain(peer_expert_v),
        "final_norm_gain": plain(final_norm_gain), "constants": constant_columns(),
    }
    arrays = {n: plain(a) for n, a in arrays.items()}
    nc = bacc.Bacc("TRN2", target_bir_lowering=False, num_devices=1)
    args = {n: nc.dram_tensor(n, a.shape, F32, kind="ExternalInput").ap() for n, a in arrays.items()}
    for n, shape in _OUTS:
        args[n] = nc.dram_tensor(n, shape, F32, kind="ExternalOutput").ap()
    build(nc, **args)
    got = run_bass_kernel_spmd(nc, [arrays], core_ids=[0]).results[0]
    shapes = [(1, SEQ, D), (1, N_SAMPLE, D), (1, 1, N_META + SEQ, KV_HEADS, HD), (1, 1, N_META + SEQ, KV_HEADS, HD),
              (1, 1, N_META + SEQ, HEADS), (1, 1, HG, HK, HK), (1, 1, N_SAMPLE, KV_HEADS, HD),
              (1, 1, N_SAMPLE, KV_HEADS, HD), (1, 1, N_SAMPLE, HEADS), (1, 1, HG, HK, HK)]
    return tuple(np.asarray(got[n]).reshape(s) for (n, _), s in zip(_OUTS, shapes))
```

```python
from contextlib import ExitStack

import concourse.bass as bass
from concourse import mybir

F32 = mybir.dt.float32
I32 = mybir.dt.int32
U32 = mybir.dt.uint32
ALU = mybir.AluOpType
ACT = mybir.ActivationFunctionType
AX_X = mybir.AxisListType.X

P = 128
D = 1024
DC = D // P
EPS = 1e-6
N_META = 16
N_SAMPLE = 64
SEQ = 512
PAST = 512
TILES = 1 + SEQ // P
HEADS = 8
KV_HEADS = 4
KV_W = 256
HD = 64
HG = 4
HK = 128
HW = HG * HK
IN_W = 3080
FG0 = 1024
GROUP_COLS = [0, 512, 1032, 1544, 2056, 2568]
G_Q, G_KV, G_HQ, G_HF, G_HI, G_HGATE = range(6)
SQ, SK, SV, SLF, SHQ, SHK, SHL, SHI, SHG = 0, 512, 768, 1024, 1032, 1544, 2056, 2568, 3080
ST_W = 3592
PH = 8
NKEY = 128
TOPK = 16
SLOTS = PH * TOPK
GROUP = 16
S_GROUPS = SLOTS // 2 // GROUP
T_GROUPS = SLOTS // GROUP
GROUPS = S_GROUPS + (TILES - 1) * T_GROUPS
RING_U = 8
DVE_SLOTS = [1, 4, 7, 9, 12, 15]
PE_SLOTS = [j for j in range(GROUP) if j not in DVE_SLOTS]
ND, NPE = len(DVE_SLOTS), len(PE_SLOTS)
RING_S = 8
WO_RING = 5
LEVELS = [64, 32, 16, 8, 4, 2, 1]
NL = len(LEVELS)
NEG = -1e30
DOTS_START, DOTS_HEAD, DOTS_STEP, DOTS_OUT = 10, 5, 6, 14
SCALE = HD ** -0.5
META0 = 64
META1 = META0 + N_META
PROMPT_KEYS = N_META + SEQ
SAMPLE_KEYS = PAST + N_SAMPLE
C_ID, C_FOLD, C_TRI, C_TRIS, C_MASK, C_ONE, C_IOTA = 0, 128, 256, 384, 512, 640, 768
C_LEV = C_IOTA + TOPK


def build(nc, x_prompt, x_sample, cache_kt, cache_v, cache_logf, state_hgrn, meta_tokens, w_in,
          b_forget, hg_lb_logits, hg_norm_gain, w_out, norm1_gain, norm2_gain, peer_w_query,
          sub_keys_t, peer_expert_u, peer_expert_v, final_norm_gain, constants,
          y_prompt, y_sample, new_k_prompt, new_v_prompt, new_logf_prompt, new_state_prompt,
          new_k_sample, new_v_sample, new_logf_sample, new_state_sample):
    with ExitStack() as ctx:
        def sb(name, shape, dt=F32):
            return ctx.enter_context(nc.sbuf_tensor(name, shape, dt))

        def sem(name):
            return ctx.enter_context(nc.semaphore(name))

        PA, PB, PC, PD = [ctx.enter_context(nc.psum_tensor(n, [P, D], F32)) for n in ("PA", "PB", "PC", "PD")]
        staged = nc.dram_tensor("staged", (TILES, P, ST_W), F32, kind="Internal").ap()
        x1_dram = nc.dram_tensor("x1_dram", (TILES, P, D), F32, kind="Internal").ap()
        h2_dram = nc.dram_tensor("h2_dram", (TILES, P, D), F32, kind="Internal").ap()

        arena = sb("arena", [P, DC * IN_W])
        w_in_sb = arena[:, :].rearrange("p (c n) -> p c n", c=DC)
        w_query_sb = arena[:, 0:DC * 2 * D].rearrange("p (c n) -> p c n", c=DC)
        ring_u = arena[:, 2 * DC * D:(2 * DC + RING_U) * D].rearrange("p (r n) -> p r n", r=RING_U)
        ring_s = arena[:, 0:RING_S * D].rearrange("p (r n) -> p r n", r=RING_S)
        ring_p = arena[:, 0:NPE * D].rearrange("p (r n) -> p r n", r=NPE)
        ring_d = arena[:, NPE * D:(NPE + ND) * D].rearrange("p (r n) -> p r n", r=ND)

        consts = sb("consts", [P, C_LEV])
        level_masks = sb("level_masks", [P, (NL + 1) * P], mybir.dt.bfloat16)
        ident = consts[:, C_ID:C_ID + P]
        act = sb("act", [P, ST_W])
        keys_t = act[:, 0:2 * PH * NKEY]
        gain = sb("gain", [P, D])
        hgain = sb("hgain", [P, HW])
        idx_all = sb("idx_all", [P, GROUPS * GROUP], I32)
        gate_all = sb("gate_all", [P, GROUPS * GROUP])
        dots_all = sb("dots_all", [P, GROUPS * GROUP])
        h2 = sb("h2", [P, D])
        rows = sb("rows", [P, D])
        rows_t = sb("rows_t", [P, D])
        w1 = sb("w1", [P, 2048])
        w2 = sb("w2", [P, 2048])
        xt = rows_t
        xm = w2[:, D:2 * D]
        k_pr = sb("k_pr", [P, HEADS * PROMPT_KEYS])
        k_prompt = k_pr[:, :].rearrange("p (h k) -> p h k", h=HEADS)
        rows_t2 = [k_pr[:, 0:D], k_pr[:, D:2 * D]]
        lb = k_pr[:, 2 * D:2 * D + 2 * HW]
        lev = sb("lev", [P, TILES * D])
        k_sample = lev[:, 0:HEADS * SAMPLE_KEYS].rearrange("p (h k) -> p h k", h=HEADS)
        w_out_sb = lev[:, :].rearrange("p (r n) -> p r n", r=WO_RING)
        x1_all = lev[:, :]
        qa = sb("qa", [P, D])
        v_pr = sb("v_pr", [P, TILES, KV_W])
        state = sb("state", [P, 2, HW])
        small = sb("small", [P, 124])
        ss, rstd = small[:, 0:4], small[:, 4:8]
        b_fg = small[:, 8:16]
        fg_u, fg_a, fg_e, fg_l = (small[:, 16 + 8 * i:24 + 8 * i] for i in range(4))
        negmax = small[:, 48:56]
        psums = small[:, 56:64]
        carry = small[0:1, 64:72]
        e_end = small[:, 72:80]
        cache_lf = small[:, 80:112]
        gsum = small[:, 112:120]
        newton = small[:, 120:124]

        tk_left = lev[:, 0:2048].rearrange("p (m n) -> p m n", n=NKEY)
        tk_val = lev[:, 2048:2304].rearrange("p (m k) -> p m k", k=TOPK)
        tk_idx = lev[:, 2304:2560].bitcast(U32).rearrange("p (m k) -> p m k", k=TOPK)
        tk_idxf = lev[:, 2560:2816].rearrange("p (m k) -> p m k", k=TOPK)
        top_val = lev[:, 2816:2944].rearrange("p (h k) -> p h k", k=TOPK)
        top_j = lev[:, 2944:3072].bitcast(U32).rearrange("p (h k) -> p h k", k=TOPK)
        j_part = [lev[:, 3072 + 128 * c:3200 + 128 * c].bitcast(U32) for c in range(2)]
        j_partf = [lev[:, 3328 + 128 * c:3456 + 128 * c] for c in range(2)]
        e_part = [lev[:, 3584 + 128 * c:3712 + 128 * c] for c in range(2)]
        idx_new = lev[:, 3840:3968].bitcast(I32)
        gate_new = lev[:, 3968:4096]

        const_in, gain_in, final_gain_in, lb_in, hgain_in = (sem(n) for n in (
            "const_in", "gain_in", "final_gain_in", "lb_in", "hgain_in"))
        x_clear, x_in, lb_less, lb_exp, h_ready, tr_done, ht_evac = (sem(n) for n in (
            "x_clear", "x_in", "lb_less", "lb_exp", "h_ready", "tr_done", "ht_evac"))
        fg_done, fg_used, fg_abs, fg_ln, proj_done, e_done, f_ready = (sem(n) for n in (
            "fg_done", "fg_used", "fg_abs", "fg_ln", "proj_done", "e_done", "f_ready"))
        staged_act, staged_dve, stored, dve_step, act_step = (sem(n) for n in (
            "staged_act", "staged_dve", "stored", "dve_step", "act_step"))
        cleared, past_in, act_in, wq_in, x2_in, keys_in = (sem(n) for n in (
            "cleared", "past_in", "act_in", "wq_in", "x2_in", "keys_in"))
        qk_turned, q_ready, k_ready, f_done, f_q, f_k = (sem(n) for n in (
            "qk_turned", "q_ready", "k_ready", "f_done", "f_q", "f_k"))
        sc_done, sc_max, p_done, pt_done, pt_evac, o_done, att_done = (sem(n) for n in (
            "sc_done", "sc_max", "p_done", "pt_done", "pt_evac", "o_done", "att_done"))
        hg_in, hg_in_evac, lev_ready, lev_exp, lev_mul, ke_done, ke_evac = (sem(n) for n in (
            "hg_in", "hg_in_evac", "lev_ready", "lev_exp", "lev_mul", "ke_done", "ke_evac"))
        gram_done, at_ready, ho_done, ho_evac, st_done, st_new, mix_ready = (sem(n) for n in (
            "gram_done", "at_ready", "ho_done", "ho_evac", "st_done", "st_new", "mix_ready"))
        mixt_done, mixt_evac, out_done, x1_ready, h2_ready, x1_saved, h2t_done, h2t_evac = (sem(n) for n in (
            "mixt_done", "mixt_evac", "out_done", "x1_ready", "h2_ready", "x1_saved", "h2t_done", "h2t_evac"))
        pq_done, pq_evac, ps_done, ps_read, less_max, gate_exp, top_done, idx_in = (sem(n) for n in (
            "pq_done", "pq_evac", "ps_done", "ps_read", "less_max", "gate_exp", "top_done", "idx_in"))
        b_in, u_free, s_free, p_free, d_free, gelu_done, wgt_done, diag_done, y_added = (sem(n) for n in (
            "b_in", "u_free", "s_free", "p_free", "d_free", "gelu_done", "wgt_done", "diag_done", "y_added"))
        masks_in, masks_ready, h2_copied, h2_doubled, wo_used, y_done = (sem(n) for n in (
            "masks_in", "masks_ready", "h2_copied", "h2_doubled", "wo_used", "y_done"))
        y_ready, y_saved, state_saved = (sem(n) for n in ("y_ready", "y_saved", "state_saved"))
        square_ready, root_ready = sem("square_ready"), sem("root_ready")
        w_in_in = [sem(f"w_in_in{c}") for c in range(DC)]
        u_in = [sem(f"u_in{i}") for i in range(RING_U)]
        s_in = [sem(f"s_in{i}") for i in range(RING_S)]
        p_in = [sem(f"p_in{i}") for i in range(NPE)]
        d_in = [sem(f"d_in{i}") for i in range(ND)]
        wo_in = [sem(f"wo_in{i}") for i in range(WO_RING)]

        def problems(t):
            if t:
                return [(0, P, k_prompt, N_META + P * t, [(0, N_META)] + [(N_META + P * b, P) for b in range(t)])]
            past = [(P * b, P) for b in range(PAST // P)]
            return [(0, N_SAMPLE, k_sample, SAMPLE_KEYS, past + [(PAST, N_SAMPLE)]),
                    (META0, N_META, k_prompt, N_META, [(0, N_META)])]

        def value_rows(t, q0, block, n, g):
            cols = slice(HD * g, HD * (g + 1))
            if t or q0 == META0:
                return v_pr[0:n, block, cols]
            if block < PAST // P:
                return rows_t[:, KV_W * block + HD * g:KV_W * block + HD * (g + 1)]
            return act[0:n, SV + HD * g:SV + HD * (g + 1)]

        def f_blocks(t):
            own = act[:, SLF:SLF + HEADS]
            if t:
                return [(own, 0, P, k_prompt, N_META + P * (t - 1), 0, True)]
            out = [(cache_lf[:, HEADS * b:HEADS * (b + 1)], 0, P, k_sample, P * b, None, b > 0)
                   for b in range(PAST // P)]
            return out + [(own, 0, N_SAMPLE, k_sample, PAST, 0, True), (own, META0, N_META, k_prompt, 0, META0, False)]

        def f_before(t):
            return sum(len(f_blocks(i)) for i in range(t))

        def fq_before(t):
            return sum(1 for i in range(t) for blk in f_blocks(i) if blk[5] is not None)

        def heads_before(t):
            return HEADS * sum(len(problems(i)) for i in range(t))

        def first_level(t):
            return 0 if t else 1

        def ends(t):
            return [(0, 0, P, PB)] if t else [(1, 0, N_SAMPLE, PB), (0, META0, N_META, PD)]

        def ends_before(t):
            return sum(len(ends(i)) for i in range(t))

        def stores_by(t):
            return 16 * (7 + 4 * t)

        def columns_of(t):
            first = (S_GROUPS + T_GROUPS * (t - 1)) * GROUP
            return range(first, first + SLOTS) if t else range(SLOTS // 2)

        def halves(ap, n, m):
            return ap.rearrange("p (a two m) -> p a two m", two=2, m=m)

        block = ctx.enter_context(nc.Block())

        @block.sync
        def _(sp):
            sp.dma_start(consts[:, :], constants[:, 0:C_LEV]).then_inc(const_in, 16)
            sp.dma_start(w1[:, 0:(NL + 1) * P], constants[:, C_LEV:C_LEV + (NL + 1) * P]).then_inc(masks_in, 16)
            sp.dma_start(gain[:, :], norm1_gain[0].partition_broadcast(P)).then_inc(gain_in, 16)
            sp.dma_start(b_fg, b_forget[0].partition_broadcast(P)).then_inc(lb_in, 16)
            sp.dma_start(lb[:, 0:HW], hg_lb_logits[0].partition_broadcast(P)).then_inc(lb_in, 16)
            sp.dma_start(lb[:, HW:2 * HW], hg_lb_logits[1].partition_broadcast(P)).then_inc(lb_in, 16)
            sp.dma_start(hgain[:, :], hg_norm_gain[0].partition_broadcast(P)).then_inc(hgain_in, 16)
            sp.wait_ge(x_clear, 1)
            sp.dma_start(xt[0:N_SAMPLE, :], x_sample[0]).then_inc(x_in, 16)
            sp.dma_start(xt[META0:META1, :], meta_tokens).then_inc(x_in, 16)
            for c in range(DC):
                sp.dma_start(w_in_sb[:, c, :], w_in[0, c * P:(c + 1) * P, :]).then_inc(w_in_in[c], 16)
            for t in range(TILES):
                if t + 1 < TILES:
                    sp.wait_ge(h_ready, t + 1)
                    sp.dma_start(xt[:, :], x_prompt[0, t * P:(t + 1) * P, :]).then_inc(x_in, 16)
                sp.wait_ge(staged_act, 4 * (t + 1))
                sp.wait_ge(staged_dve, 4 * (t + 1))
                sp.dma_start(staged[t], act[:, :]).then_inc(stored, 16)
                for of_sample, of_prompt, at, n in ((new_k_sample, new_k_prompt, SK, KV_W),
                                                    (new_v_sample, new_v_prompt, SV, KV_W),
                                                    (new_logf_sample, new_logf_prompt, SLF, HEADS)):
                    if t:
                        first = N_META + (t - 1) * P
                        sp.dma_start(of_prompt[first:first + P], act[:, at:at + n]).then_inc(stored, 16)
                    else:
                        sp.dma_start(of_sample, act[0:N_SAMPLE, at:at + n]).then_inc(stored, 16)
                        sp.dma_start(of_prompt[0:N_META], act[META0:META1, at:at + n]).then_inc(stored, 16)

            sp.wait_ge(proj_done, 6 * TILES)
            sp.dma_start(gain[:, :], norm2_gain[0].partition_broadcast(P)).then_inc(gain_in, 16)
            for c in range(DC):
                sp.dma_start(w_query_sb[:, c, :], peer_w_query[0, c * P:(c + 1) * P, :]).then_inc(wq_in, 16)
            sp.wait_ge(stored, stores_by(TILES - 1))
            sp.wait_ge(cleared, 6)
            for par in range(2):
                sp.dma_start(k_sample[0:HD, par:HEADS:2, 0:PAST], cache_kt).then_inc(past_in, 16)
            sp.dma_start(rows_t[:, :].rearrange("p (b n) -> p b n", n=KV_W),
                         cache_v.rearrange("(b p) n -> p b n", p=P)).then_inc(past_in, 16)
            sp.dma_start(cache_lf.rearrange("p (b h) -> p b h", h=HEADS),
                         cache_logf.rearrange("(b p) h -> p b h", p=P)).then_inc(past_in, 16)
            sp.dma_start(state[:, 1, :].rearrange("p (h v) -> p h v", h=HG),
                         state_hgrn.rearrange("h k v -> k h v")).then_inc(past_in, 16)
            sp.dma_start(v_pr[0:N_META, 0, :], staged[0, META0:META1, SV:SV + KV_W]).then_inc(past_in, 16)
            for t in range(1, TILES):
                sp.dma_start(v_pr[:, t, :], staged[t, :, SV:SV + KV_W]).then_inc(past_in, 16)
            for t in range(TILES):
                if t:
                    sp.wait_ge(ps_done, t)
                sp.dma_start(act[:, :], staged[t]).then_inc(act_in, 16)
                sp.wait_ge(at_ready, HG * (t + 1))
                if t:
                    sp.dma_start(xm, x_prompt[0, (t - 1) * P:t * P, :]).then_inc(x2_in, 16)
                else:
                    sp.dma_start(xm[0:N_SAMPLE, :], x_sample[0]).then_inc(x2_in, 16)
                    sp.dma_start(xm[META0:META1, :], meta_tokens).then_inc(x2_in, 16)

                def load_w_out(c):
                    slot = c % WO_RING
                    sp.dma_start(w_out_sb[:, slot, :], w_out[0, c * P:(c + 1) * P, :]).then_inc(wo_in[slot], 16)

                sp.wait_ge(ho_done, HG * (t + 1))
                for c in range(WO_RING):
                    load_w_out(c)
                sp.wait_ge(mix_ready, t + 1)
                sp.wait_ge(st_done, ends_before(t + 1))
                sp.dma_start(keys_t, sub_keys_t).then_inc(keys_in, 16)
                for c in range(WO_RING, DC):
                    sp.wait_ge(wo_used, DC * t + c - WO_RING + 1)
                    load_w_out(c)
                if t == 0:
                    sp.wait_ge(st_new, 1)
                    sp.dma_start(new_state_sample.rearrange("h k v -> k h v"),
                                 state[:, 1, :].rearrange("p (h v) -> p h v", h=HG)).then_inc(state_saved, 16)
                sp.wait_ge(x1_ready, t + 1)
                sp.dma_start(x1_dram[t], xm).then_inc(x1_saved, 16)
                if t == 0:
                    sp.wait_ge(h2_copied, 1)
                    sp.dma_start(h2[N_SAMPLE:P, :], rows[0:N_SAMPLE, :]).then_inc(h2_doubled, 16)
                if t == 0:
                    sp.wait_ge(top_done, 1)
                    half = SLOTS // 2
                    for lo in (0, half):
                        sp.dma_start(idx_all[lo:lo + half, 0:half], idx_new[0:half, lo:lo + half]).then_inc(idx_in, 16)
                        sp.dma_start(gate_all[lo:lo + half, 0:half], gate_new[0:half, lo:lo + half]).then_inc(idx_in, 16)
            sp.wait_ge(st_new, ends_before(TILES))
            sp.dma_start(new_state_prompt.rearrange("h k v -> k h v"),
                         state[:, 0, :].rearrange("p (h v) -> p h v", h=HG)).then_inc(state_saved, 16)

            sp.wait_ge(h2_copied, TILES)
            sp.dma_start(rows[:, :], final_norm_gain.partition_broadcast(P)).then_inc(final_gain_in, 16)
            sp.wait_ge(top_done, TILES)
            sp.wait_ge(x1_saved, 16 * TILES)
            for t in range(TILES):
                sp.dma_start(x1_all[:, t * D:(t + 1) * D], x1_dram[t]).then_inc(b_in, 16)
            for t in range(TILES):
                sp.wait_ge(y_ready, t + 1)
                if t:
                    sp.dma_start(y_prompt[0, (t - 1) * P:t * P, :], x1_all[:, t * D:(t + 1) * D]).then_inc(y_saved, 16)
                else:
                    sp.dma_start(y_sample[0], x1_all[0:N_SAMPLE, 0:D]).then_inc(y_saved, 16)
            sp.wait_ge(y_saved, 16 * TILES)
            sp.wait_ge(state_saved, 32)

        @block.gpsimd
        def _(pool):
            def gather(k, table, slot, free, count, arrived):
                pool.wait_ge(free, count)
                pool.indirect_dma_start(slot, None, table[0],
                                        bass.IndirectOffsetOnAxis(ap=idx_all[:, k:k + 1], axis=0)
                                        ).then_inc(arrived, 16)

            def gather_key(k):
                gather(k, peer_expert_u, ring_u[:, k % RING_U, :], u_free, k + 1, u_in[k % RING_U])

            last_keys = columns_of(TILES - 1)
            for t in range(TILES - 1):
                pool.wait_ge(top_done, t + 1)
                if t == 0:
                    pool.wait_ge(idx_in, 64)
                for k in columns_of(t):
                    gather_key(k)
            pool.wait_ge(top_done, TILES)
            for k in columns_of(0):
                gather_key(last_keys[k])
                gather(k, peer_expert_v, ring_s[:, k % RING_S, :], s_free, k + 1, s_in[k % RING_S])
            pool.wait_ge(s_free, RING_S + len(columns_of(0)))
            beside = list(last_keys)[len(columns_of(0)):]
            for n in range(GROUPS - S_GROUPS):
                for j in range(GROUP):
                    k = (S_GROUPS + n) * GROUP + j
                    if n * GROUP + j < len(beside):
                        gather_key(beside[n * GROUP + j])
                    if j in DVE_SLOTS:
                        i = DVE_SLOTS.index(j)
                        gather(k, peer_expert_v, ring_d[:, i, :], d_free, ND * n + i + 1, d_in[i])
                    else:
                        i = PE_SLOTS.index(j)
                        gather(k, peer_expert_v, ring_p[:, i, :], p_free, NPE * n + i + 1, p_in[i])

        @block.scalar
        def _(eng):
            steps = [0]

            def link(ins):
                steps[0] += 1
                ins.then_inc(act_step, 1)
                eng.wait_ge(act_step, steps[0])

            roots = [0]

            def inverse_root(n):
                roots[0] += 1
                eng.wait_ge(square_ready, roots[0])
                link(eng.activation(rstd[:, 0:n], ss[:, 0:n], ACT.Ln))
                eng.activation(rstd[:, 0:n], rstd[:, 0:n], ACT.Exp, scale=-0.5).then_inc(root_ready, 1)

            eng.wait_ge(lb_less, 1)
            eng.activation(lb, lb, ACT.Exp).then_inc(lb_exp, 1)
            inverse_root(1)

            def turn_evac(t):
                eng.wait_ge(tr_done, t + 1)
                if t >= 2:
                    eng.wait_ge(proj_done, 6 * (t - 1))
                eng.activation(rows_t2[t % 2], PA[:, :], ACT.Copy).then_inc(ht_evac, 1)

            turn_evac(0)
            for t in range(TILES):
                eng.wait_ge(fg_abs, t + 1)
                link(eng.activation(fg_e, fg_a, ACT.Exp, scale=-1.0))
                eng.activation(fg_l, fg_e, ACT.Ln, bias=1.0).then_inc(fg_ln, 1)
                if t + 1 < TILES:
                    inverse_root(1)
                if t:
                    eng.wait_ge(stored, stores_by(t - 1))
                eng.wait_ge(proj_done, 6 * t + 1)
                eng.activation(act[:, SQ:SQ + 512], PB[:, 0:512], ACT.Copy).then_inc(staged_act, 1)
                eng.wait_ge(proj_done, 6 * t + 2)
                eng.activation(act[:, SK:SK + 512], PB[:, 512:1024], ACT.Copy).then_inc(staged_act, 1)
                if t + 1 < TILES:
                    turn_evac(t + 1)
                eng.wait_ge(proj_done, 6 * t + 3)
                if t:
                    eng.wait_ge(staged_dve, 4 * t)
                eng.activation(w2[:, 0:512], PC[:, 0:512], ACT.Exp, scale=-1.0).then_inc(e_done, 1)
                eng.wait_ge(proj_done, 6 * t + 4)
                if t:
                    eng.wait_ge(staged_act, 4 * t)
                eng.activation(w2[:, 512:1024], PC[:, 512:1024], ACT.Exp, scale=-1.0).then_inc(e_done, 1)
                eng.wait_ge(f_ready, t + 1)
                eng.activation(act[:, SHL:SHL + 512], w2[:, 512:1024], ACT.Ln).then_inc(staged_act, 1)
                eng.wait_ge(proj_done, 6 * t + 5)
                eng.activation(act[:, SHI:SHI + 512], PD[:, 0:512], ACT.Copy).then_inc(staged_act, 1)
                eng.wait_ge(proj_done, 6 * t + 6)
                eng.activation(w2[:, 1024:1536], PD[:, 512:1024], ACT.Exp, scale=-1.0).then_inc(e_done, 1)

            for t in range(TILES):
                eng.wait_ge(qk_turned, t + 1)
                if t == 0:
                    eng.wait_ge(cleared, 6)
                eng.activation(qa[0:HD, :], PA[0:HD, :], ACT.Copy, scale=SCALE).then_inc(q_ready, 1)
                for b, (_, _, n, _, _, q0, _) in enumerate(f_blocks(t)):
                    if q0 is not None:
                        eng.wait_ge(f_k, 2 * (f_before(t) + b + 1))
                        eng.activation(qa[64:65, :].rearrange("p (h q) -> p h q", h=HEADS)[:, :, q0:q0 + n],
                                       PC[0:1, :].rearrange("p (h q) -> p h q", h=HEADS)[:, :, 0:n],
                                       ACT.Copy).then_inc(f_q, 1)

                def exponentials(a, q, h):
                    _, m, _, n, _ = q
                    eng.wait_ge(sc_max, a + 1)
                    if a >= 2:
                        eng.wait_ge(pt_done, a - 1)
                    eng.activation(w1[0:m, D * (a % 2):D * (a % 2) + n], (PA, PB)[a % 2][0:m, 0:n], ACT.Exp,
                                   bias=negmax[0:m, h:h + 1], accum_out=psums[0:m, h:h + 1]).then_inc(p_done, 1)

                def turned(a, q):
                    _, m, _, _, blocks = q
                    eng.wait_ge(pt_done, a + 1)
                    if a >= 2:
                        eng.wait_ge(o_done, a - 1)
                    src = PC[:, 0:5 * P].rearrange("p (b q) -> p b q", q=P)
                    dst = w2[:, D * (a % 2):D * (a % 2) + 5 * P].rearrange("p (b q) -> p b q", q=P)
                    whole = [i for i, (_, k) in enumerate(blocks) if k == P]
                    short = [(i, k) for i, (_, k) in enumerate(blocks) if k < P][0]
                    if whole:
                        eng.activation(dst[:, whole[0]:whole[-1] + 1, 0:m], src[:, whole[0]:whole[-1] + 1, 0:m],
                                       ACT.Copy).then_inc(pt_evac, 1)
                    i, k = short
                    eng.activation(dst[0:k, i, 0:m], src[0:k, i, 0:m], ACT.Copy).then_inc(pt_evac, 1 if whole else 2)

                a = heads_before(t)
                for n_q, q in enumerate(problems(t)):
                    if n_q:
                        eng.wait_ge(att_done, 1)
                    for h in range(HEADS):
                        exponentials(a + h, q, h)
                        if h:
                            turned(a + h - 1, q)
                    turned(a + HEADS - 1, q)
                    a += HEADS

                eng.wait_ge(hg_in, t + 1)
                eng.activation(w1[:, 0:D], PA[:, :], ACT.Copy).then_inc(hg_in_evac, 1)
                eng.activation(w1[:, D:D + HW], PB[:, 0:HW], ACT.Copy).then_inc(hg_in_evac, 1)
                eng.wait_ge(lev_ready, t + 1)
                exps = lev[:, first_level(t) * HW:(NL + 2) * HW]
                eng.activation(exps, exps, ACT.Exp).then_inc(lev_exp, 1)
                eng.wait_ge(ke_done, t + 1)
                eng.activation(w2[:, 0:HW], PB[:, HW:2 * HW], ACT.Copy).then_inc(ke_evac, 1)
                eng.wait_ge(ho_done, HG * (t + 1))
                eng.activation(w1[:, 0:HW], PD[:, HW:2 * HW], ACT.Copy).then_inc(ho_evac, 1)
                inverse_root(HG)
                eng.wait_ge(mixt_done, t + 1)
                eng.activation(rows_t[:, :], PA[:, :], ACT.Copy).then_inc(mixt_evac, 1)
                inverse_root(1)
                eng.wait_ge(h2t_done, t + 1)
                eng.activation(rows_t[:, :], PA[:, :], ACT.Copy).then_inc(h2t_evac, 1)
                for n, psum in enumerate((PC, PD)):
                    eng.wait_ge(pq_done, 2 * t + n + 1)
                    eng.activation(w1[:, D * n:D * (n + 1)], psum[:, :], ACT.Copy).then_inc(pq_evac, 1)
                if t:
                    eng.wait_ge(u_free, RING_U + columns_of(t)[0])
                n = P if t else N_SAMPLE
                eng.activation(h2[0:n, :], rows[0:n, :], ACT.Copy).then_inc(h2_copied, 1)
                eng.wait_ge(less_max, t + 1)
                eng.activation(gate_new, gate_new, ACT.Exp).then_inc(gate_exp, 1)

            last_first = columns_of(TILES - 1)[0]
            eng.wait_ge(u_free, RING_U + last_first)
            eng.activation(dots_all[:, 0:last_first], dots_all[:, 0:last_first], ACT.Gelu).then_inc(gelu_done, 1)
            eng.wait_ge(wgt_done, 1)
            eng.wait_ge(top_done, TILES)
            for k in columns_of(0):
                if k >= GROUP:
                    eng.wait_ge(s_free, RING_S + k - GROUP + 1)
                j = k % GROUP
                eng.activation(w1[:, j * P:(j + 1) * P], consts[:, C_FOLD:C_FOLD + P], ACT.Copy,
                               scale=dots_all[:, k:k + 1]).then_inc(diag_done, 1)
            inverse_root(1)
            eng.wait_ge(s_free, RING_S + len(columns_of(0)))
            for t in range(1, TILES):
                if t == TILES - 1:
                    eng.wait_ge(u_free, RING_U + GROUPS * GROUP)
                    eng.activation(dots_all[:, last_first:], dots_all[:, last_first:], ACT.Gelu).then_inc(gelu_done, 1)
                    eng.wait_ge(wgt_done, 2)
                first = (t - 1) * T_GROUPS
                with eng.Fori(0, T_GROUPS // 2) as pair:
                    for half in range(2):
                        eng.wait_ge(p_free, pair * (2 * NPE) + (first + half) * NPE)
                        for i, j in enumerate(PE_SLOTS):
                            at = pair * (2 * GROUP) + ((S_GROUPS + first + half) * GROUP + j)
                            eng.activation((w1, w2)[half][:, i * P:(i + 1) * P], ident, ACT.Copy,
                                           scale=dots_all[:, bass.ds(at, 1)]).then_inc(diag_done, 1)
                inverse_root(1)

        @block.tensor
        def _(pe):
            pe.wait_ge(const_in, 16)

            def turn_rows(t):
                pe.wait_ge(h_ready, t + 1)
                if t:
                    pe.wait_ge(ht_evac, t)
                    pe.wait_ge(fg_used, t)
                for c in range(DC):
                    last = pe.transpose(PA[:, c * P:(c + 1) * P], rows[:, c * P:(c + 1) * P], ident)
                last.then_inc(tr_done, 1)

            group_psum = [PB[:, 0:512], PB[:, 512:1024], PC[:, 0:512], PC[:, 512:1024], PD[:, 0:512], PD[:, 512:1024]]
            turn_rows(0)
            for t in range(TILES):
                pe.wait_ge(ht_evac, t + 1)
                frees = [(staged_act, 4 * t - 3), (staged_act, 4 * t - 2), (staged_dve, 4 * t - 2),
                         (e_done, 3 * t - 1), (staged_act, 4 * t), (staged_dve, 4 * t)]

                def columns(out, first, n, done):
                    for c in range(DC):
                        if t == 0:
                            pe.wait_ge(w_in_in[c], 16)
                        last = pe.matmul(out, rows_t2[t % 2][:, c * P:(c + 1) * P], w_in_sb[:, c, first:first + n],
                                         start=(c == 0), stop=(c == DC - 1))
                    last.then_inc(done, 1)

                columns(PA[:, 0:HEADS], FG0, HEADS, fg_done)
                for g, first in enumerate(GROUP_COLS):
                    if t:
                        pe.wait_ge(*frees[g])
                    columns(group_psum[g], first, 512, proj_done)
                    if g == G_KV and t + 1 < TILES:
                        turn_rows(t + 1)

            for t in range(TILES):
                pe.wait_ge(act_in, 16 * (t + 1))
                if t:
                    pe.wait_ge(ps_read, t)
                else:
                    pe.wait_ge(staged_act, 4 * TILES)
                    pe.wait_ge(staged_dve, 4 * TILES)
                for h in range(HEADS):
                    pe.transpose(PA[0:HD, h * P:(h + 1) * P], act[:, SQ + HD * h:SQ + HD * (h + 1)], ident)
                for g in range(KV_HEADS):
                    last = pe.transpose(PB[0:HD, g * P:(g + 1) * P], act[:, SK + HD * g:SK + HD * (g + 1)], ident)
                last.then_inc(qk_turned, 1)
                if t == 0:
                    pe.wait_ge(past_in, 16 * (6 + TILES - 1))
                for b, (gates, r0, n, _, _, _, goes_on) in enumerate(f_blocks(t)):
                    i = f_before(t) + b
                    if i:
                        pe.wait_ge(f_k, 2 * i)
                    if fq_before(t) + (b == len(f_blocks(t)) - 1 and t == 0):
                        pe.wait_ge(f_q, fq_before(t) + (b == len(f_blocks(t)) - 1 and t == 0))
                    if t:
                        pe.wait_ge(pq_evac, 2 * t)
                    for h in range(HEADS):
                        out = PC[0:1, h * P:h * P + n]
                        last = pe.matmul(out, gates[r0:r0 + n, h:h + 1],
                                         consts[r0:r0 + n, C_TRI + r0:C_TRI + r0 + n], start=True, stop=not goes_on)
                        if goes_on:
                            last = pe.matmul(out, carry[:, h:h + 1], consts[0:1, C_ONE:C_ONE + n], start=False, stop=True)
                    last.then_inc(f_done, 1)

                pe.wait_ge(q_ready, t + 1)
                pe.wait_ge(k_ready, 2 * (t + 1))
                pe.wait_ge(f_q, fq_before(t + 1))
                pe.wait_ge(f_k, 2 * f_before(t + 1))

                def scores(a, q, h):
                    q0, m, keys, n, _ = q
                    if a >= 2:
                        pe.wait_ge(p_done, a - 1)
                    for k0 in range(0, n, 512):
                        k1 = min(n, k0 + 512)
                        last = pe.matmul((PA, PB)[a % 2][0:m, k0:k1], qa[:, h * P + q0:h * P + q0 + m],
                                         keys[:, h, k0:k1], start=True, stop=True)
                    last.then_inc(sc_done, 1)

                def values(a, q, h):
                    q0, m, _, _, blocks = q
                    pe.wait_ge(p_done, a + 1)
                    if a:
                        pe.wait_ge(pt_evac, 2 * a)
                    for i, (k0, k) in enumerate(blocks):
                        p0 = D * (a % 2) + k0
                        last = pe.transpose(PC[0:k, i * P:i * P + m], w1[0:m, p0:p0 + k], ident[0:m, 0:m])
                    last.then_inc(pt_done, 1)
                    pe.wait_ge(pt_evac, 2 * (a + 1))
                    for i, (k0, k) in enumerate(blocks):
                        at = D * (a % 2) + i * P
                        last = pe.matmul(PD[0:m, h * HD:(h + 1) * HD], w2[0:k, at:at + m],
                                         value_rows(t, q0, i, k, h // (HEADS // KV_HEADS)),
                                         start=(i == 0), stop=(i == len(blocks) - 1))
                    last.then_inc(o_done, 1)

                a = heads_before(t)
                for n_q, q in enumerate(problems(t)):
                    if n_q:
                        pe.wait_ge(att_done, 1)
                    for h in range(HEADS):
                        scores(a + h, q, h)
                        if h:
                            values(a + h - 1, q, h - 1)
                    values(a + HEADS - 1, q, HEADS - 1)
                    a += HEADS

                pe.wait_ge(p_done, a)
                tri = consts[:, (C_TRI if t else C_TRIS):(C_TRI if t else C_TRIS) + P]
                for h in range(HG):
                    cols = slice(h * HK, (h + 1) * HK)
                    pe.matmul(PA[:, cols], act[:, SHL + h * HK:SHL + (h + 1) * HK], tri, start=True, stop=True)
                for h in range(HG):
                    pe.transpose(PA[:, HW + h * HK:HW + (h + 1) * HK], act[:, SHQ + h * HK:SHQ + (h + 1) * HK], ident)
                for h in range(HG):
                    last = pe.transpose(PB[:, h * HK:(h + 1) * HK], act[:, SHK + h * HK:SHK + (h + 1) * HK], ident)
                last.then_inc(hg_in, 1)
                pe.wait_ge(hg_in_evac, 2 * (t + 1))
                pe.wait_ge(lev_mul, t + 1)
                for h in range(HG):
                    last = pe.transpose(PB[:, HW + h * HK:HW + (h + 1) * HK],
                                        lev[:, NL * HW + h * HK:NL * HW + (h + 1) * HK], ident)
                last.then_inc(ke_done, 1)

                def grams(h):
                    if h >= 2:
                        pe.wait_ge(at_ready, HG * t + h - 1)
                    psum = (PC, PA)[h % 2]
                    for l in range(first_level(t), NL):
                        both = lev[:, l * HW + h * HK:l * HW + (h + 1) * HK]
                        pe.matmul(psum[:, l * P:(l + 1) * P], both, both, start=True, stop=True)
                    pe.matmul(psum[:, NL * P:(NL + 1) * P], w1[:, D + h * HK:D + (h + 1) * HK],
                              w1[:, HW + h * HK:HW + (h + 1) * HK], start=True, stop=True).then_inc(gram_done, 1)

                def outputs(h):
                    pe.wait_ge(at_ready, HG * t + h + 1)
                    m = P if t else N_SAMPLE
                    col = HW + h * HK
                    pe.matmul(PD[:, col:col + HK], w1[:, D + HW + h * P:D + HW + (h + 1) * P],
                              act[:, SHI + h * HK:SHI + (h + 1) * HK], start=True, stop=False, skip_group_check=True)
                    pe.matmul(PD[0:m, col:col + HK], lev[:, (NL + 1) * HW + h * HK:(NL + 1) * HW + h * HK + m],
                              state[:, 0 if t else 1, h * HK:(h + 1) * HK], start=False, stop=True,
                              skip_group_check=True).then_inc(ho_done, 1)

                if t:
                    pe.wait_ge(st_new, ends_before(t))
                for h in range(HG):
                    grams(h)
                    if h:
                        outputs(h - 1)
                outputs(HG - 1)
                pe.wait_ge(ke_evac, t + 1)
                pe.wait_ge(att_done, heads_before(t + 1) // HEADS)
                for _, r0, n, psum in ends(t):
                    for h in range(HG):
                        last = pe.matmul(psum[:, h * HK:(h + 1) * HK], w2[r0:r0 + n, h * HK:(h + 1) * HK],
                                         act[r0:r0 + n, SHI + h * HK:SHI + (h + 1) * HK], start=True, stop=True)
                    last.then_inc(st_done, 1)

                pe.wait_ge(mix_ready, t + 1)
                for c in range(DC):
                    last = pe.transpose(PA[:, c * P:(c + 1) * P], rows[:, c * P:(c + 1) * P], ident)
                last.then_inc(mixt_done, 1)
                pe.wait_ge(mixt_evac, t + 1)
                pe.wait_ge(st_new, ends_before(t + 1))
                for c in range(DC):
                    slot = c % WO_RING
                    per_tile = len(range(slot, DC, WO_RING))
                    pe.wait_ge(wo_in[slot], 16 * (per_tile * t + c // WO_RING + 1))
                    for half in range(2):
                        last = pe.matmul(PB[:, half * 512:(half + 1) * 512], rows_t[:, c * P:(c + 1) * P],
                                         w_out_sb[:, slot, half * 512:(half + 1) * 512],
                                         start=(c == 0), stop=(c == DC - 1))
                    last.then_inc(wo_used, 1)
                pe.wait_ge(h2_ready, t + 1)
                for c in range(DC):
                    last = pe.transpose(PA[:, c * P:(c + 1) * P], rows[:, c * P:(c + 1) * P], ident)
                last.then_inc(h2t_done, 1)
                pe.wait_ge(h2t_evac, t + 1)
                if t == 0:
                    pe.wait_ge(wq_in, 16 * DC)
                for n, psum in enumerate((PC, PD)):
                    if n:
                        pe.wait_ge(ho_evac, t + 1)
                    for m in range(PH):
                        first = (n * PH + m) * P
                        for c in range(DC):
                            last = pe.matmul(psum[:, m * P:(m + 1) * P], w_query_sb[:, c, first:first + P],
                                             rows_t[:, c * P:(c + 1) * P], start=(c == 0), stop=(c == DC - 1))
                    last.then_inc(pq_done, 1)
                pe.wait_ge(keys_in, 16 * (t + 1))
                pe.wait_ge(x1_ready, t + 1)
                for n, psum in enumerate((PA, PB)):
                    pe.wait_ge(pq_evac, 2 * t + n + 1)
                    for m in range(PH):
                        i = n * PH + m
                        last = pe.matmul(psum[:, m * NKEY:(m + 1) * NKEY], w1[:, i * P:(i + 1) * P],
                                         keys_t[:, i * NKEY:(i + 1) * NKEY], start=True, stop=True)
                last.then_inc(ps_done, 1)

            def weighted(psum, diag, value, first, last):
                for half in range(2):
                    ins = pe.matmul(psum[:, half * 512:(half + 1) * 512], diag,
                                    value[:, half * 512:(half + 1) * 512], start=first, stop=last)
                return ins

            n_s = len(columns_of(0))
            for k in columns_of(0):
                pe.wait_ge(s_in[k % RING_S], 16 * (k // RING_S + 1))
                pe.wait_ge(diag_done, k + 1)
                j = k % GROUP
                weighted(PC, w1[:, j * P:(j + 1) * P], ring_s[:, k % RING_S, :], k == 0, k == n_s - 1).then_inc(s_free, 1)
            pe.wait_ge(ps_read, TILES)
            with pe.Fori(0, (GROUPS - S_GROUPS) // 2) as pair:
                for half in range(2):
                    pe.wait_ge(y_added, pair * 2 + half)
                    for i in range(NPE):
                        pe.wait_ge(p_in[i], pair * 32 + 16 * (half + 1))
                        pe.wait_ge(diag_done, pair * (2 * NPE) + (n_s + half * NPE + i + 1))
                        weighted((PA, PB)[half], (w1, w2)[half][:, i * P:(i + 1) * P], ring_p[:, i, :],
                                 i == 0, i == NPE - 1).then_inc(p_free, 1)

        @block.vector
        def _(eng):
            steps = [0]

            def link(ins):
                steps[0] += 1
                ins.then_inc(dve_step, 1)
                eng.wait_ge(dve_step, steps[0])

            roots = [0]

            def inverse_root(n, width):
                roots[0] += 1
                x, y, z = ss[:, 0:n], rstd[:, 0:n], newton[:, 0:n]
                eng.tensor_scalar(x, x, 1.0 / width, EPS, ALU.mult, ALU.add).then_inc(square_ready, 1)
                eng.wait_ge(root_ready, roots[0])
                link(eng.tensor_tensor(z, y, y, ALU.mult))
                link(eng.tensor_tensor(z, z, x, ALU.mult))
                link(eng.tensor_scalar(z, z, -0.5, 1.5, ALU.mult, ALU.add))
                link(eng.tensor_tensor(y, y, z, ALU.mult))

            def mean_square(src, scratch):
                link(eng.tensor_tensor_reduce(scratch, src, src, 1.0, 0.0, ALU.mult, ALU.add, ss[:, 0:1]))
                inverse_root(1, D)

            eng.memset(xt[:, :], 0.0).then_inc(x_clear, 1)
            eng.wait_ge(masks_in, 16)
            eng.tensor_copy(level_masks[:, :], w1[:, 0:(NL + 1) * P]).then_inc(masks_ready, 1)
            eng.wait_ge(masks_ready, 1)
            eng.wait_ge(lb_in, 48)
            link(eng.tensor_tensor(act[:, 0:HW], lb[:, 0:HW], lb[:, HW:2 * HW], ALU.max))
            link(eng.tensor_tensor(lb[:, 0:HW], lb[:, 0:HW], act[:, 0:HW], ALU.subtract))
            eng.tensor_tensor(lb[:, HW:2 * HW], lb[:, HW:2 * HW], act[:, 0:HW], ALU.subtract).then_inc(lb_less, 1)
            eng.wait_ge(lb_exp, 1)
            link(eng.tensor_tensor(act[:, 0:HW], lb[:, 0:HW], lb[:, HW:2 * HW], ALU.add))
            link(eng.reciprocal(act[:, 0:HW], act[:, 0:HW]))
            link(eng.tensor_tensor(lb[:, 0:HW], lb[:, 0:HW], act[:, 0:HW], ALU.mult))
            link(eng.tensor_scalar(lb[:, HW:2 * HW], lb[:, 0:HW], -1.0, 1.0, ALU.mult, ALU.add))

            def normalise(t):
                eng.wait_ge(x_in, 16 * (t + 2))
                mean_square(xt[:, :], w1[:, 0:D])
                if t:
                    eng.wait_ge(tr_done, t)
                eng.scalar_tensor_tensor(out=rows[:, :], in0=xt[:, :], scalar=rstd[:, 0:1], in1=gain[:, :],
                                         op0=ALU.mult, op1=ALU.mult).then_inc(h_ready, 1)

            eng.wait_ge(gain_in, 16)
            normalise(0)
            for t in range(TILES):
                eng.wait_ge(fg_done, t + 1)
                eng.tensor_tensor(fg_u, PA[:, 0:HEADS], b_fg, ALU.add).then_inc(fg_used, 1)
                eng.wait_ge(fg_used, t + 1)
                eng.scalar_tensor_tensor(out=fg_a, in0=fg_u, scalar=-1.0, in1=fg_u, op0=ALU.mult, op1=ALU.max).then_inc(fg_abs, 1)
                if t + 1 < TILES:
                    normalise(t + 1)
                if t:
                    eng.wait_ge(stored, stores_by(t - 1))
                eng.wait_ge(fg_ln, t + 1)
                eng.scalar_tensor_tensor(out=act[:, SLF:SLF + HEADS], in0=fg_u, scalar=0.0, in1=fg_l,
                                         op0=ALU.min, op1=ALU.subtract).then_inc(staged_dve, 1)

                def sigmoid(e):
                    link(eng.tensor_scalar(e, e, 1.0, None, ALU.add))
                    link(eng.reciprocal(e, e))

                eng.wait_ge(e_done, 3 * t + 1)
                sigmoid(w2[:, 0:512])
                eng.tensor_tensor(act[:, SHQ:SHQ + 512], PC[:, 0:512], w2[:, 0:512], ALU.mult).then_inc(staged_dve, 1)
                eng.wait_ge(e_done, 3 * t + 2)
                f = w2[:, 512:1024]
                sigmoid(f)
                link(eng.tensor_tensor(f, f, lb[:, HW:2 * HW], ALU.mult))
                eng.tensor_tensor(f, f, lb[:, 0:HW], ALU.add).then_inc(f_ready, 1)
                eng.wait_ge(f_ready, t + 1)
                eng.tensor_scalar(act[:, SHK:SHK + 512], f, -1.0, 1.0, ALU.mult, ALU.add).then_inc(staged_dve, 1)
                eng.wait_ge(e_done, 3 * t + 3)
                sigmoid(w2[:, 1024:1536])
                eng.tensor_tensor(act[:, SHG:SHG + 512], PD[:, 512:1024], w2[:, 1024:1536],
                                  ALU.mult).then_inc(staged_dve, 1)

            eng.wait_ge(proj_done, 6 * TILES)
            for i, buf in enumerate((k_pr, lev, qa)):
                eng.memset(buf[64:P, :], 0.0).then_inc(cleared, 1)
            eng.wait_ge(cleared, 3)
            for buf, row in ((k_pr, 64), (lev, 64), (qa, 96)):
                eng.memset(buf[row:row + 1, :], 1.0).then_inc(cleared, 1)
            link(eng.memset(state[:, 0, :], 0.0))
            eng.sem_inc(u_free, RING_U)

            taken = [0]

            def dot(k, out, count):
                slot = ring_u[:, k % RING_U, :]
                eng.wait_ge(u_in[k % RING_U], count)
                eng.scalar_tensor_tensor(out=slot, in0=slot, scalar=1.0, in1=h2[:, :], op0=ALU.mult,
                                         op1=ALU.mult, accum_out=out).then_inc(u_free, 1)

            def some_dots(t, share):
                if t == 0:
                    return
                cols = columns_of(t - 1)
                if taken[0] == cols[0]:
                    eng.wait_ge(h2_copied, t)
                    if t == 1:
                        eng.wait_ge(h2_doubled, 16)
                until = min(cols[-1] + 1, taken[0] + (share * len(cols)) // SLOTS)
                for k in range(taken[0], until):
                    dot(k, dots_all[:, k:k + 1], 16 * (k // RING_U + 1))
                taken[0] = until

            for t in range(TILES):
                eng.wait_ge(qk_turned, t + 1)
                turned = PB[0:HD, 0:KV_HEADS * P].rearrange("p (g q) -> p g q", q=P)
                eng.wait_ge(cleared, 6)
                for par in range(2):
                    if t:
                        first = N_META + P * (t - 1)
                        eng.tensor_copy(k_prompt[0:HD, par:HEADS:2, first:first + P], turned).then_inc(k_ready, 1)
                    else:
                        link(eng.tensor_copy(k_sample[0:HD, par:HEADS:2, PAST:SAMPLE_KEYS], turned[:, :, 0:N_SAMPLE]))
                        eng.tensor_copy(k_prompt[0:HD, par:HEADS:2, 0:N_META],
                                        turned[:, :, META0:META1]).then_inc(k_ready, 1)
                for b, (_, _, n, keys, first, _, _) in enumerate(f_blocks(t)):
                    eng.wait_ge(f_done, f_before(t) + b + 1)
                    sums = PC[0:1, :].rearrange("p (h q) -> p h q", h=HEADS)
                    eng.tensor_scalar(keys[96:97, :, first:first + n], sums[:, :, 0:n], -1.0, None,
                                      ALU.mult).then_inc(f_k, 1)
                    eng.tensor_copy(carry, sums[:, :, n - 1]).then_inc(f_k, 1)
                some_dots(t, DOTS_START)

                a = heads_before(t)
                for n_q, (q0, m, _, n, _) in enumerate(problems(t)):
                    for h in range(HEADS):
                        eng.wait_ge(sc_done, a + 1)
                        psum = (PA, PB)[a % 2]
                        for k0 in ([n - m] if n // 512 == (n - m) // 512 or n <= 512 else [n - m, 512]):
                            k1 = 512 if (n > 512 and k0 < 512) else n
                            j = k0 - (n - m)
                            link(eng.tensor_tensor(psum[0:m, k0:k1], psum[0:m, k0:k1],
                                                   consts[0:m, C_MASK + j:C_MASK + j + k1 - k0], ALU.add))
                        link(eng.tensor_reduce(negmax[0:m, h:h + 1], psum[0:m, 0:n], AX_X, ALU.max))
                        eng.tensor_scalar(negmax[0:m, h:h + 1], negmax[0:m, h:h + 1], -1.0, None,
                                          ALU.mult).then_inc(sc_max, 1)
                        a += 1
                        some_dots(t, DOTS_HEAD)
                    eng.wait_ge(p_done, a)
                    link(eng.reciprocal(psums[0:m, :], psums[0:m, :]))
                    eng.wait_ge(o_done, a)
                    if t and n_q == 0:
                        eng.wait_ge(h2_copied, t)
                        eng.wait_ge(h2_doubled, 16)
                        eng.wait_ge(h2t_done, t)
                    eng.tensor_tensor(rows[q0:q0 + m, 0:HW].rearrange("p (h d) -> p h d", d=HD),
                                      PD[0:m, 0:HW].rearrange("p (h d) -> p h d", d=HD),
                                      psums[0:m, :].unsqueeze(2).to_broadcast([m, HEADS, HD]),
                                      ALU.mult).then_inc(att_done, 1)

                eng.wait_ge(hg_in_evac, 2 * (t + 1))
                sums = w1[:, 0:HW]
                sums_h = sums.rearrange("p (h q) -> p h q", h=HG)
                if t == 0:
                    link(eng.memset(lev[:, NL * HW:(NL + 1) * HW], 0.0))
                if t == 1:
                    eng.wait_ge(idx_in, 64)
                for l in range(first_level(t), NL):
                    m = LEVELS[l]
                    out, src = halves(lev[:, l * HW:(l + 1) * HW], HW // (2 * m), m), halves(sums, HW // (2 * m), m)
                    mid = src[:, :, 0, m - 1:m].to_broadcast([P, HW // (2 * m), m])
                    eng.tensor_tensor(out[:, :, 0, :], mid, src[:, :, 0, :], ALU.subtract)
                    eng.tensor_tensor(out[:, :, 1, :], src[:, :, 1, :], mid, ALU.subtract)
                to_end = lev[:, NL * HW:(NL + 1) * HW].rearrange("p (h q) -> p h q", h=HG)
                for _, r0, n, _ in ends(t):
                    eng.tensor_tensor(to_end[:, :, r0:r0 + n],
                                      sums_h[:, :, r0 + n - 1:r0 + n].to_broadcast([P, HG, n]),
                                      sums_h[:, :, r0:r0 + n], ALU.subtract)
                eng.tensor_copy(lev[:, (NL + 1) * HW:(NL + 2) * HW], sums).then_inc(lev_ready, 1)
                some_dots(t, DOTS_STEP)
                eng.wait_ge(lev_exp, t + 1)
                queries, keys = w1[:, HW:2 * HW], w1[:, 2 * HW:3 * HW]
                for l in range(first_level(t), NL):
                    m = LEVELS[l]
                    both = halves(lev[:, l * HW:(l + 1) * HW], HW // (2 * m), m)
                    for side, what in ((0, keys), (1, queries)):
                        eng.tensor_tensor(both[:, :, side, :], both[:, :, side, :],
                                          halves(what, HW // (2 * m), m)[:, :, side, :], ALU.mult)
                eng.tensor_tensor(lev[:, NL * HW:(NL + 1) * HW], lev[:, NL * HW:(NL + 1) * HW], keys, ALU.mult)
                from_start = lev[:, (NL + 1) * HW:(NL + 2) * HW]
                if ends_before(t):
                    eng.wait_ge(st_new, ends_before(t))
                for i, (_, r0, n, _) in enumerate(ends(t)):
                    link(eng.tensor_copy(e_end[:, HG * i:HG * (i + 1)],
                                         from_start.rearrange("p (h q) -> p h q", h=HG)[:, :, r0 + n - 1]))
                eng.tensor_tensor(from_start, from_start, queries, ALU.mult).then_inc(lev_mul, 1)
                some_dots(t, DOTS_STEP)
                for h in range(HG):
                    eng.wait_ge(gram_done, HG * t + h + 1)
                    masked = w2[:, D:2 * D]
                    c0 = first_level(t) * P
                    link(eng.tensor_tensor(masked[:, c0:D], (PC, PA)[h % 2][:, c0:D],
                                           level_masks[:, c0:D], ALU.mult))
                    eng.tensor_reduce(w1[:, D + HW + h * P:D + HW + (h + 1) * P],
                                      masked[:, c0:D].rearrange("p (l q) -> p q l", q=P),
                                      AX_X, ALU.add).then_inc(at_ready, 1)
                    eng.wait_ge(at_ready, HG * t + h + 1)
                for i, (which, _, _, psum) in enumerate(ends(t)):
                    eng.wait_ge(ho_done, HG * (t + 1))
                    eng.wait_ge(st_done, ends_before(t) + i + 1)
                    for h in range(HG):
                        s = state[:, which, h * HK:(h + 1) * HK]
                        last = eng.scalar_tensor_tensor(out=s, in0=s, scalar=e_end[:, HG * i + h:HG * i + h + 1],
                                                        in1=psum[:, h * HK:(h + 1) * HK], op0=ALU.mult, op1=ALU.add)
                    last.then_inc(st_new, 1)
                some_dots(t, DOTS_STEP)
                eng.wait_ge(ho_evac, t + 1)
                eng.wait_ge(hgain_in, 16)
                o = w1[:, 0:HW]
                o_h = o.rearrange("p (h v) -> p h v", h=HG)
                link(eng.tensor_tensor(w2[:, 0:HW], o, o, ALU.mult))
                link(eng.tensor_reduce(ss[:, 0:HG], w2[:, 0:HW].rearrange("p (h v) -> p h v", h=HG), AX_X, ALU.add))
                inverse_root(HG, HK)
                link(eng.tensor_tensor(o_h, o_h, rstd[:, 0:HG].unsqueeze(2).to_broadcast([P, HG, HK]), ALU.mult))
                link(eng.tensor_tensor(o, o, hgain[:, :], ALU.mult))
                if t == 0:
                    link(eng.memset(rows[96:P, 0:HW], 0.0))
                eng.tensor_tensor(rows[:, HW:2 * HW], o, act[:, SHG:SHG + HW], ALU.mult).then_inc(mix_ready, 1)

                some_dots(t, DOTS_OUT)
                eng.wait_ge(wo_used, DC * (t + 1))
                eng.wait_ge(x2_in, 16 * (t + 2))
                n = P if t else META1
                eng.tensor_tensor(xm[0:n, :], xm[0:n, :], PB[0:n, :], ALU.add).then_inc(x1_ready, 1)
                eng.wait_ge(x1_ready, t + 1)
                mean_square(xm, w2[:, 0:D])
                eng.wait_ge(mixt_done, t + 1)
                eng.wait_ge(gain_in, 32)
                eng.scalar_tensor_tensor(out=rows[:, :], in0=xm, scalar=rstd[:, 0:1], in1=gain[:, :],
                                         op0=ALU.mult, op1=ALU.mult).then_inc(h2_ready, 1)
                some_dots(t, SLOTS)

                eng.wait_ge(ps_done, t + 1)
                eng.wait_ge(x1_saved, 16 * (t + 1))
                scores = [(PA, PB)[i // PH][:, (i % PH) * NKEY:(i % PH + 1) * NKEY] for i in range(2 * PH)]

                def sixteen(values, left, val, idx, read=None):
                    n = len(values)
                    for i in range(n):
                        last = eng.max(val[:, i, 0:8], values[i])
                    link(last)
                    for i in range(n):
                        eng.max_index(idx[:, i, 0:8], val[:, i, 0:8], values[i])
                        last = eng.match_replace(left[i], val[:, i, 0:8], values[i], NEG)
                    link(last)
                    if read is not None:
                        eng.sem_inc(read, 1)
                    for i in range(n):
                        last = eng.max(val[:, i, 8:16], left[i])
                    link(last)
                    for i in range(n):
                        last = eng.max_index(idx[:, i, 8:16], val[:, i, 8:16], left[i])
                    link(last)

                sixteen(scores, [tk_left[:, i, :] for i in range(2 * PH)], tk_val, tk_idx, ps_read)
                cand = w1[:, :].rearrange("p (h i j) -> p h i j", h=PH, i=TOPK)
                val_h = tk_val.rearrange("p (h c) k -> p h c k", c=2)
                link(eng.tensor_tensor(cand, val_h[:, :, 0, :].unsqueeze(3).to_broadcast([P, PH, TOPK, TOPK]),
                                       val_h[:, :, 1, :].unsqueeze(2).to_broadcast([P, PH, TOPK, TOPK]), ALU.add))
                pairs = TOPK * TOPK
                sixteen([w1[:, h * pairs:(h + 1) * pairs] for h in range(PH)],
                        [w2[:, h * pairs:(h + 1) * pairs] for h in range(PH)], top_val, top_j)
                gates = gate_new.rearrange("p (h k) -> p h k", k=TOPK)
                eng.tensor_tensor(gates, top_val, top_val[:, :, 0:1].to_broadcast([P, PH, TOPK]),
                                  ALU.subtract).then_inc(less_max, 1)
                top_jf = lev[:, 2944:3072].bitcast(U32)
                link(eng.tensor_scalar(j_part[0], top_jf, 4, None, ALU.logical_shift_right))
                link(eng.tensor_scalar(j_part[1], top_jf, 15, None, ALU.bitwise_and))
                link(eng.tensor_copy(tk_idxf, tk_idx))
                idx_h = tk_idxf.rearrange("p (h c) k -> p h c k", c=2)
                same = w2[:, :].rearrange("p (h k i) -> p h k i", h=PH, i=TOPK)
                shape = [P, PH, TOPK, TOPK]
                for c in range(2):
                    link(eng.tensor_copy(j_partf[c], j_part[c]))
                    j = j_partf[c].rearrange("p (h k) -> p h k", k=TOPK)
                    iota = consts[:, C_IOTA:C_IOTA + TOPK].unsqueeze(1).unsqueeze(1)
                    link(eng.tensor_tensor(same, j.unsqueeze(3).to_broadcast(shape), iota.to_broadcast(shape),
                                           ALU.is_equal))
                    link(eng.tensor_tensor(same, same, idx_h[:, :, c, :].unsqueeze(2).to_broadcast(shape), ALU.mult))
                    link(eng.tensor_reduce(e_part[c].rearrange("p (h k) -> p h k", k=TOPK), same, AX_X, ALU.add))
                link(eng.scalar_tensor_tensor(out=e_part[0], in0=e_part[0], scalar=float(NKEY), in1=e_part[1],
                                              op0=ALU.mult, op1=ALU.add))
                first = (S_GROUPS + T_GROUPS * (t - 1)) * GROUP
                link(eng.tensor_copy(idx_all[:, first:first + SLOTS] if t else idx_new, e_part[0]))
                eng.wait_ge(gate_exp, t + 1)
                link(eng.tensor_reduce(gsum, gates, AX_X, ALU.add))
                link(eng.reciprocal(gsum, gsum))
                gates_to = gate_all[:, first:first + SLOTS].rearrange("p (h k) -> p h k", k=TOPK) if t else gates
                eng.tensor_tensor(gates_to, gates, gsum.unsqueeze(2).to_broadcast([P, PH, TOPK]),
                                  ALU.mult).then_inc(top_done, 1)

            eng.wait_ge(pq_done, 2 * TILES)
            eng.sem_inc(s_free, RING_S)
            last_first = columns_of(TILES - 1)[0]

            def weights(n, first, end):
                eng.wait_ge(gelu_done, n)
                eng.tensor_tensor(dots_all[:, first:end], dots_all[:, first:end], gate_all[:, first:end],
                                  ALU.mult).then_inc(wgt_done, 1)

            def finish(t):
                x1 = x1_all[:, t * D:(t + 1) * D]
                mean_square(x1, rows_t[:, :])
                eng.scalar_tensor_tensor(out=x1, in0=x1, scalar=rstd[:, 0:1], in1=rows[:, :],
                                         op0=ALU.mult, op1=ALU.mult).then_inc(y_ready, 1)

            weights(1, 0, last_first)
            n_s = len(columns_of(0))
            eng.wait_ge(h2_copied, TILES)
            for k in range(last_first, last_first + n_s):
                dot(k, dots_all[:, k:k + 1], 16 * (k // RING_U + 1))
            eng.wait_ge(b_in, 16 * TILES)
            eng.wait_ge(final_gain_in, 16)
            eng.wait_ge(s_free, RING_S + n_s)
            eng.sem_inc(p_free, NPE)
            eng.sem_inc(d_free, ND)
            eng.tensor_tensor(x1_all[:, 0:D], x1_all[:, 0:D], PC[:, :], ALU.add).then_inc(y_done, 1)
            eng.wait_ge(y_done, 1)
            finish(0)

            for t in range(1, TILES):
                x1 = x1_all[:, t * D:(t + 1) * D]
                first = (t - 1) * T_GROUPS

                def groups(p0, p1, with_dots):
                    with eng.Fori(p0, p1) as pair:
                        for half in range(2):
                            if with_dots:
                                for j in range(GROUP):
                                    k = pair * (2 * GROUP) + (last_first + n_s + half * GROUP + j)
                                    at = (n_s + half * GROUP + j) // RING_U
                                    dot(j, dots_all[:, bass.ds(k, 1)],
                                        pair * (32 * GROUP // RING_U) + 16 * (last_first // RING_U + at + 1))
                            for i, j in enumerate(DVE_SLOTS):
                                at = pair * (2 * GROUP) + ((S_GROUPS + first + half) * GROUP + j)
                                eng.wait_ge(d_in[i], pair * 32 + 16 * (first + half + 1))
                                eng.wait_ge(d_free, pair * (2 * ND) + (ND * (first + half + 1) + i))
                                eng.scalar_tensor_tensor(out=x1, in0=ring_d[:, i, :], scalar=dots_all[:, bass.ds(at, 1)],
                                                         in1=x1, op0=ALU.mult, op1=ALU.add).then_inc(d_free, 1)
                            eng.wait_ge(d_free, pair * (2 * ND) + ND * (first + half + 2))
                            eng.wait_ge(p_free, pair * (2 * NPE) + NPE * (first + half + 2))
                            eng.tensor_tensor(x1, x1, (PA, PB)[half][:, :], ALU.add).then_inc(y_added, 1)
                            eng.wait_ge(y_added, pair * 2 + (first + half + 1))

                beside = (len(columns_of(TILES - 1)) - n_s) // (2 * GROUP)
                if t == 1:
                    groups(0, beside, True)
                    groups(beside, T_GROUPS // 2, False)
                else:
                    if t == TILES - 1:
                        weights(2, last_first, GROUPS * GROUP)
                        eng.wait_ge(wgt_done, 2)
                    groups(0, T_GROUPS // 2, False)
                finish(t)


def constant_columns():
    import numpy as np
    r = np.arange(P)
    s, t = r[:, None], r[None, :]
    upper = (s <= t)
    cols = [s == t, (s % N_SAMPLE == t) & (t < N_SAMPLE), upper, upper & (s // 64 == t // 64),
            np.where(t <= s, 0.0, NEG), np.ones((P, P)), np.broadcast_to(np.arange(TOPK)[None, :], (P, TOPK))]
    for m in LEVELS:
        cols.append((s // (2 * m) == t // (2 * m)) & (s // m % 2 == 0) & (t // m % 2 == 1))
    cols.append(s == t)
    return np.concatenate([np.asarray(c, np.float32) for c in cols], axis=1)


_OUTS = [("y_prompt", (1, SEQ, D)), ("y_sample", (1, N_SAMPLE, D)),
         ("new_k_prompt", (N_META + SEQ, KV_W)), ("new_v_prompt", (N_META + SEQ, KV_W)),
         ("new_logf_prompt", (N_META + SEQ, HEADS)), ("new_state_prompt", (HG, HK, HK)),
         ("new_k_sample", (N_SAMPLE, KV_W)), ("new_v_sample", (N_SAMPLE, KV_W)),
         ("new_logf_sample", (N_SAMPLE, HEADS)), ("new_state_sample", (HG, HK, HK))]


def kernel(x_prompt, x_sample, cache_k, cache_v, cache_logf, state_hgrn, meta_tokens, w_in, b_forget,
           hg_lb_logits, hg_norm_gain, w_out, norm1_gain, norm2_gain, peer_w_query, peer_sub_keys,
           peer_expert_u, peer_expert_v, final_norm_gain):
    import numpy as np
    import concourse.bacc as bacc
    from concourse.bass_utils import run_bass_kernel_spmd

    def plain(a):
        return np.ascontiguousarray(np.asarray(a))

    cache_k, cache_v = plain(cache_k), plain(cache_v)
    arrays = {
        "x_prompt": plain(x_prompt), "x_sample": plain(x_sample),
        "cache_kt": plain(cache_k[0, 0].transpose(2, 1, 0)),
        "cache_v": cache_v.reshape(PAST, KV_W), "cache_logf": plain(cache_logf)[0, 0],
        "state_hgrn": plain(state_hgrn)[0, 0], "meta_tokens": plain(meta_tokens), "w_in": plain(w_in),
        "b_forget": plain(b_forget), "hg_lb_logits": plain(hg_lb_logits), "hg_norm_gain": plain(hg_norm_gain),
        "w_out": plain(w_out), "norm1_gain": plain(norm1_gain), "norm2_gain": plain(norm2_gain),
        "peer_w_query": plain(peer_w_query),
        "sub_keys_t": plain(plain(peer_sub_keys)[0].reshape(2 * PH, NKEY, P).transpose(2, 0, 1)).reshape(P, 2 * PH * NKEY),
        "peer_expert_u": plain(peer_expert_u), "peer_expert_v": plain(peer_expert_v),
        "final_norm_gain": plain(final_norm_gain), "constants": constant_columns(),
    }
    arrays = {n: plain(a) for n, a in arrays.items()}
    nc = bacc.Bacc("TRN2", target_bir_lowering=False, num_devices=1)
    args = {n: nc.dram_tensor(n, a.shape, F32, kind="ExternalInput").ap() for n, a in arrays.items()}
    for n, shape in _OUTS:
        args[n] = nc.dram_tensor(n, shape, F32, kind="ExternalOutput").ap()
    build(nc, **args)
    got = run_bass_kernel_spmd(nc, [arrays], core_ids=[0]).results[0]
    shapes = [(1, SEQ, D), (1, N_SAMPLE, D), (1, 1, N_META + SEQ, KV_HEADS, HD), (1, 1, N_META + SEQ, KV_HEADS, HD),
              (1, 1, N_META + SEQ, HEADS), (1, 1, HG, HK, HK), (1, 1, N_SAMPLE, KV_HEADS, HD),
              (1, 1, N_SAMPLE, KV_HEADS, HD), (1, 1, N_SAMPLE, HEADS), (1, 1, HG, HK, HK)]
    return tuple(np.asarray(got[n]).reshape(s) for (n, _), s in zip(_OUTS, shapes))
```

```python
from contextlib import ExitStack

import concourse.bass as bass
from concourse import mybir

F32 = mybir.dt.float32
I32 = mybir.dt.int32
U32 = mybir.dt.uint32
ALU = mybir.AluOpType
ACT = mybir.ActivationFunctionType
AX_X = mybir.AxisListType.X

P = 128
D = 1024
DC = D // P
EPS = 1e-6
N_META = 16
N_SAMPLE = 64
SEQ = 512
PAST = 512
TILES = 1 + SEQ // P
HEADS = 8
KV_HEADS = 4
KV_W = 256
HD = 64
HG = 4
HK = 128
HW = HG * HK
IN_W = 3080
FG0 = 1024
GROUP_COLS = [0, 512, 1032, 1544, 2056, 2568]
G_Q, G_KV, G_HQ, G_HF, G_HI, G_HGATE = range(6)
FIRST_ORDER = [G_HQ, G_HF, G_HI, G_HGATE, G_Q, G_KV]
LATER_ORDER = [G_HQ, G_HF, G_HGATE, G_KV, G_Q, G_HI]
SQ, SK, SV, SLF, SHQ, SHK, SHL, SHI, SHG = 0, 512, 768, 1024, 1032, 1544, 2056, 2568, 3080
ST_W = 3592
PH = 8
NKEY = 128
TOPK = 16
SLOTS = PH * TOPK
GROUP = 16
S_GROUPS = SLOTS // 2 // GROUP
T_GROUPS = SLOTS // GROUP
GROUPS = S_GROUPS + (TILES - 1) * T_GROUPS
RING_U, RING_V, RING_L = 5, 4, 4
EARLY = [64, 96, 96, 32]
PARTS = len(EARLY)
DVE_SLOTS = [1, 4, 7, 9, 12, 15]
PE_SLOTS = [j for j in range(GROUP) if j not in DVE_SLOTS]
ND, NPE = len(DVE_SLOTS), len(PE_SLOTS)
WO_RING = 5
KEYS_FROM = 2
LEVELS = [64, 32, 16, 8, 4, 2, 1]
NL = len(LEVELS)
NEG = -1e30
PLACES = [("start", 9, 4)] + [(f"head{h}", 6, 2) for h in range(HEADS)] + [
    ("levels", 4, 8), ("masks", 8, 3), ("gram1", 0, 2), ("gram2", 0, 2),
    ("norm", 6, 6), ("out", 11, 0), ("rows", SLOTS, 14), ("top", 0, 34)]
FIRST_TOP = 27
LATER = TILES - 1
ITEM_PLACES = [(f"sum{b}", 1) for b in range(3, 6)] + [("start", 1)] + [
    (f"head{h}", 1) for h in range(HEADS)] + [(f"meta{h}", 1) for h in range(HEADS)] + [
    ("levels", 2), ("masks", 1), ("gram1", 1), ("gram2", 1), ("norm", 0), ("out", 0)]
LATER_STORES = 10
ITEMS = 1 + len(GROUP_COLS) * LATER
SCALE = HD ** -0.5
META0 = 64
META1 = META0 + N_META
PROMPT_KEYS = N_META + SEQ
SAMPLE_KEYS = PAST + N_SAMPLE
C_ID, C_FOLD, C_TRI, C_TRIS, C_MASK, C_IOTA = 0, 128, 256, 384, 512, 640
C_LEV = C_IOTA + TOPK


def build(nc, x_prompt, x_sample, cache_kt, cache_v, cache_logf, state_hgrn, meta_tokens, w_in,
          b_forget, hg_lb_logits, hg_norm_gain, w_out, norm1_gain, norm2_gain, peer_w_query,
          sub_keys_t, peer_expert_u, peer_expert_v, final_norm_gain, constants,
          y_prompt, y_sample, new_k_prompt, new_v_prompt, new_logf_prompt, new_state_prompt,
          new_k_sample, new_v_sample, new_logf_sample, new_state_sample):
    with ExitStack() as ctx:
        def sb(name, shape, dt=F32):
            return ctx.enter_context(nc.sbuf_tensor(name, shape, dt))

        def sem(name):
            return ctx.enter_context(nc.semaphore(name))

        PA, PB, PC, PD = [ctx.enter_context(nc.psum_tensor(n, [P, D], F32)) for n in ("PA", "PB", "PC", "PD")]
        staged = nc.dram_tensor("staged", (LATER, P, ST_W), F32, kind="Internal").ap()
        y_dram = nc.dram_tensor("y_dram", (PARTS, P, D), F32, kind="Internal").ap()
        x1_dram = nc.dram_tensor("x1_dram", (TILES, P, D), F32, kind="Internal").ap()

        arena = sb("arena", [P, (2 * DC + RING_U + RING_V) * D])
        x_all = arena[:, 0:LATER * D].rearrange("p (t n) -> p t n", n=D)
        xt_all = arena[:, LATER * D:2 * LATER * D].rearrange("p (t n) -> p t n", n=D)
        buf_e, buf_f, _, _, buf_a, buf_b, buf_c, buf_d = (
            arena[:, i * LATER * 512:(i + 1) * LATER * 512].rearrange("p (t n) -> p t n", n=512) for i in range(8))
        w_ring = [arena[:, first:first + DC * 512].rearrange("p (c n) -> p c n", n=512)
                  for first in (2 * DC * D, 2 * DC * D + DC * 512, 2 * LATER * D, 2 * LATER * D + DC * 512)]
        w_query_sb = arena[:, 0:DC * 2 * D].rearrange("p (c n) -> p c n", c=DC)
        spare = arena[:, 2 * DC * D:(2 * DC + RING_U + RING_V) * D].rearrange("p (r n) -> p r n", n=D)
        ring_u, ring_v = spare[:, 0:RING_U, :], spare[:, RING_U:RING_U + RING_V, :]
        ring_l = spare[:, 0:RING_L, :]
        y_part = spare[:, RING_L:RING_L + PARTS, :]
        ring_p = arena[:, 0:NPE * D].rearrange("p (r n) -> p r n", r=NPE)
        ring_d = arena[:, NPE * D:(NPE + ND) * D].rearrange("p (r n) -> p r n", r=ND)

        consts = sb("consts", [P, C_LEV])
        level_masks = sb("level_masks", [P, (NL + 1) * P], mybir.dt.bfloat16)
        ident = consts[:, C_ID:C_ID + P]
        ones = consts[0:1, C_TRI:C_TRI + P]
        act = sb("act", [P, ST_W])
        keys_t = act[:, 0:2 * PH * NKEY]
        hgain = sb("hgain", [P, HW])
        idx_all = sb("idx_all", [P, GROUPS * GROUP], I32)
        gate_all = sb("gate_all", [P, GROUPS * GROUP])
        dots_all = sb("dots_all", [P, GROUPS * GROUP])
        h2 = sb("h2", [P, D])
        rows = sb("rows", [P, D])
        rows_t = sb("rows_t", [P, D])
        w1 = sb("w1", [P, 2048])
        w2 = sb("w2", [P, 2048])
        diag_v = sb("diag_v", [P, RING_V * P])
        w_fg = diag_v[:, 0:DC * HEADS].rearrange("p (c n) -> p c n", n=HEADS)
        later_u, later_a, later_e, later_f = (
            diag_v[:, DC * HEADS + i * LATER * HEADS:DC * HEADS + (i + 1) * LATER * HEADS].rearrange(
                "p (t n) -> p t n", n=HEADS) for i in range(4))
        gain_1 = xt_all[:, LATER - 1, :]
        gain_2 = w2[:, 0:D]
        xt = rows_t
        queries_t = [w2[:, 0:D], w1[:, 0:D]]
        xm = w2[:, D:2 * D]
        k_pr = sb("k_pr", [P, HEADS * PROMPT_KEYS])
        k_prompt = k_pr[:, :].rearrange("p (h k) -> p h k", h=HEADS)
        lev = sb("lev", [P, TILES * D])
        k_sample = lev[:, 0:HEADS * SAMPLE_KEYS].rearrange("p (h k) -> p h k", h=HEADS)
        w_out_sb = lev[:, :].rearrange("p (r n) -> p r n", r=WO_RING)
        x1_all = lev[:, :]
        qa = sb("qa", [P, D])
        v_pr = sb("v_pr", [P, TILES, KV_W])
        lb = v_pr[:, 1:TILES, :].rearrange("p a b -> p (a b)")
        state = sb("state", [P, 2, HW])
        small = sb("small", [P, 124])
        ss, rstd = small[:, 0:4], small[:, 4:8]
        b_fg = small[:, 8:16]
        fg_u, fg_a, fg_e, fg_l = (small[:, 16 + 8 * i:24 + 8 * i] for i in range(4))
        negmax = small[:, 48:56]
        psums = small[:, 56:64]
        carry = small[0:1, 64:72]
        e_end = small[:, 72:80]
        cache_lf = small[:, 80:112]
        gsum = small[:, 112:120]
        newton = small[:, 120:124]

        tk_left = lev[:, 0:2048].rearrange("p (m n) -> p m n", n=NKEY)
        tk_val = lev[:, 2048:2304].rearrange("p (m k) -> p m k", k=TOPK)
        tk_idx = lev[:, 2304:2560].bitcast(U32).rearrange("p (m k) -> p m k", k=TOPK)
        tk_idxf = lev[:, 2560:2816].rearrange("p (m k) -> p m k", k=TOPK)
        top_val = lev[:, 2816:2944].rearrange("p (h k) -> p h k", k=TOPK)
        top_j = lev[:, 2944:3072].bitcast(U32).rearrange("p (h k) -> p h k", k=TOPK)
        j_part = [lev[:, 3072 + 128 * c:3200 + 128 * c].bitcast(U32) for c in range(2)]
        j_partf = [lev[:, 3328 + 128 * c:3456 + 128 * c] for c in range(2)]
        e_part = [lev[:, 3584 + 128 * c:3712 + 128 * c] for c in range(2)]
        gate_new = lev[:, 3968:4096]

        const_in, gain_in, final_gain_in, lb_in, hgain_in = (sem(n) for n in (
            "const_in", "gain_in", "final_gain_in", "lb_in", "hgain_in"))
        x_clear, x_in, lb_less, lb_exp, h_ready, tr_done, ht_evac = (sem(n) for n in (
            "x_clear", "x_in", "lb_less", "lb_exp", "h_ready", "tr_done", "ht_evac"))
        fg_done, fg_used, fg_abs, fg_ln, proj_done, e_done, f_ready = (sem(n) for n in (
            "fg_done", "fg_used", "fg_abs", "fg_ln", "proj_done", "e_done", "f_ready"))
        staged_act, staged_dve, stored, dve_step, act_step = (sem(n) for n in (
            "staged_act", "staged_dve", "stored", "dve_step", "act_step"))
        cleared, past_in, act_in, wq_in, x2_in, keys_in = (sem(n) for n in (
            "cleared", "past_in", "act_in", "wq_in", "x2_in", "keys_in"))
        qk_turned, q_ready, k_ready, f_done, f_q, f_k = (sem(n) for n in (
            "qk_turned", "q_ready", "k_ready", "f_done", "f_q", "f_k"))
        sc_done, sc_max, p_done, pt_done, pt_evac, o_done, att_done = (sem(n) for n in (
            "sc_done", "sc_max", "p_done", "pt_done", "pt_evac", "o_done", "att_done"))
        hg_in, hg_in_evac, lev_ready, lev_exp, lev_mul, ke_done, ke_evac = (sem(n) for n in (
            "hg_in", "hg_in_evac", "lev_ready", "lev_exp", "lev_mul", "ke_done", "ke_evac"))
        gram_done, at_ready, ho_done, ho_evac, st_done, st_new, mix_ready = (sem(n) for n in (
            "gram_done", "at_ready", "ho_done", "ho_evac", "st_done", "st_new", "mix_ready"))
        mixt_done, mixt_evac, x1_ready, h2_ready, x1_saved, h2t_done, h2t_evac = (sem(n) for n in (
            "mixt_done", "mixt_evac", "x1_ready", "h2_ready", "x1_saved", "h2t_done", "h2t_evac"))
        pq_done, pq_evac, ps_done, ps_read, less_max, gate_exp, top_done = (sem(n) for n in (
            "pq_done", "pq_evac", "ps_done", "ps_read", "less_max", "gate_exp", "top_done"))
        qt_done, qt_evac, chosen = sem("qt_done"), sem("qt_evac"), sem("chosen")
        y_part_in, gain_2_in = sem("y_part_in"), sem("gain_2_in")
        v_free, vdiag_done, l_free, y_part_ready, y_part_saved = (sem(n) for n in (
            "v_free", "vdiag_done", "l_free", "y_part_ready", "y_part_saved"))
        b_in, u_free, p_free, d_free, gelu_done, wgt_done, diag_done = (sem(n) for n in (
            "b_in", "u_free", "p_free", "d_free", "gelu_done", "wgt_done", "diag_done"))
        masks_in, masks_ready, h2_copied, h2_doubled, wo_used = (sem(n) for n in (
            "masks_in", "masks_ready", "h2_copied", "h2_doubled", "wo_used"))
        y_even_added, y_odd_added = sem("y_even_added"), sem("y_odd_added")
        y_ready, y_saved, state_saved = (sem(n) for n in ("y_ready", "y_saved", "state_saved"))
        square_ready, root_ready = sem("square_ready"), sem("root_ready")
        w_in_in = [sem(f"w_in_in{i}") for i in range(4)]
        w_late_in = [sem("w_late_in0"), sem("w_late_in1")]
        w_fg_in, x_later_in, later_ready, later_turned, later_evac = (sem(n) for n in (
            "w_fg_in", "x_later_in", "later_ready", "later_turned", "later_evac"))
        hq_stored = sem("hq_stored")
        item_done, item_evac, item_sigmoid, pool_step, later_done = (sem(n) for n in (
            "item_done", "item_evac", "item_sigmoid", "pool_step", "later_done"))
        later_abs, later_ln, later_hf, later_hf_ln, first_stored, v_in_later = (sem(n) for n in (
            "later_abs", "later_ln", "later_hf", "later_hf_ln", "first_stored", "v_in_later"))
        u_in = [sem(f"u_in{i}") for i in range(RING_U)]
        v_in = [sem(f"v_in{i}") for i in range(RING_V)]
        l_in = [sem(f"l_in{i}") for i in range(RING_L)]
        p_in = [sem(f"p_in{i}") for i in range(NPE)]
        d_in = [sem(f"d_in{i}") for i in range(ND)]
        wo_in = [sem(f"wo_in{i}") for i in range(WO_RING)]

        def problems(t):
            if t:
                return [(0, P, k_prompt, N_META + P * t, [(0, N_META)] + [(N_META + P * b, P) for b in range(t)])]
            past = [(P * b, P) for b in range(PAST // P)]
            return [(0, N_SAMPLE, k_sample, SAMPLE_KEYS, past + [(PAST, N_SAMPLE)]),
                    (META0, N_META, k_prompt, N_META, [(0, N_META)])]

        def value_rows(t, q0, block, n, g):
            cols = slice(HD * g, HD * (g + 1))
            if t or q0 == META0:
                return v_pr[0:n, block, cols]
            if block < PAST // P:
                return rows_t[:, KV_W * block + HD * g:KV_W * block + HD * (g + 1)]
            return act[0:n, SV + HD * g:SV + HD * (g + 1)]

        def f_blocks(t):
            own = act[:, SLF:SLF + HEADS]
            if t:
                return [(own, 0, P, k_prompt, N_META + P * (t - 1), 0, True)]
            out = [(cache_lf[:, HEADS * b:HEADS * (b + 1)], 0, P, k_sample, P * b, None, b > 0)
                   for b in range(PAST // P)]
            return out + [(own, 0, N_SAMPLE, k_sample, PAST, 0, True), (own, META0, N_META, k_prompt, 0, META0, False)]

        def f_before(t):
            return sum(len(f_blocks(i)) for i in range(t))

        def fq_before(t):
            return sum(1 for i in range(t) for blk in f_blocks(i) if blk[5] is not None)

        def heads_before(t):
            return HEADS * sum(len(problems(i)) for i in range(t))

        def first_level(t):
            return 0 if t else 1

        def ends(t):
            return [(0, 0, P, PC)] if t else [(1, 0, N_SAMPLE, PC), (0, META0, N_META, PB)]

        def ends_before(t):
            return sum(len(ends(i)) for i in range(t))

        item_plan, sigmoid_plan, n_items, last_items = {}, {}, 0, []
        for place, n in ITEM_PLACES:
            item_plan[place] = list(range(n_items, n_items + n))
            sigmoid_plan[place] = last_items
            n_items, last_items = n_items + n, item_plan[place]
        assert n_items == ITEMS

        def group_of(item):
            return (item - 1) // LATER, (item - 1) % LATER

        def with_sigmoid(g):
            return LATER_ORDER[g] in (G_HQ, G_HF, G_HGATE)

        w_slot = [0, 1, 2, 3, 0, 1, 0, 1]
        w_fills = [1, 1, 1, 1, 2, 2, 3, 3]

        def w_group(n):
            first = GROUP_COLS[(FIRST_ORDER + LATER_ORDER)[n]]
            return w_in[0, :, first:first + 512].rearrange("(c p) n -> p c n", p=P)

        def top_heads(t):
            return PH if t else PH // 2

        def early_columns(t):
            cols = columns_of(t)
            return cols[0:EARLY[t]] if 0 <= t < PARTS else range(0)

        def columns_of(t):
            first = (S_GROUPS + T_GROUPS * (t - 1)) * GROUP
            return range(first, first + SLOTS) if t else range(SLOTS // 2)

        plan, dots_taken, values_taken = {}, 0, 0
        for t in range(TILES):
            for place, n_dots, n_values in PLACES:
                cols = columns_of(t - 1) if t else range(0)
                n_dots = min((n_dots * len(cols)) // SLOTS, len(cols) - dots_taken)
                of_dots = list(cols[dots_taken:dots_taken + n_dots])
                dots_taken = 0 if place == "top" else dots_taken + n_dots
                tile = t - 1 if place == "top" else t - 2
                early = early_columns(tile)
                n_values = min((n_values * min(len(early), 96)) // 96, len(early) - values_taken)
                if place == "top" and t == 1:
                    n_values = min(FIRST_TOP, len(early))
                if place == "rows" or place == "top" and t == TILES - 1:
                    n_values = len(early) - values_taken
                of_values = list(early[values_taken:values_taken + n_values])
                values_taken = 0 if place == "rows" else values_taken + n_values
                plan[t, place] = (of_dots, of_values, tile)
        value_order = [k for key in plan for k in plan[key][1]]
        value_rank = {k: i for i, k in enumerate(value_order)}

        def late_groups(t):
            return T_GROUPS - len(early_columns(t)) // GROUP

        late = [(t, S_GROUPS + T_GROUPS * t - late_groups(t)) for t in range(1, TILES)]
        late_total = sum(late_groups(t) for t in range(1, TILES))
        late_before = {t: sum(late_groups(i) for i in range(1, t)) for t in range(1, TILES)}

        def score_psum(a, n):
            return PA[:, 0:n] if n > 512 else PA[:, 512 * (a % 2):512 * (a % 2) + n]

        def halves(ap, n, m):
            return ap.rearrange("p (a two m) -> p a two m", two=2, m=m)

        block = ctx.enter_context(nc.Block())

        @block.sync
        def _(sp):
            sp.dma_start(gain_1, norm1_gain[0].partition_broadcast(P)).then_inc(gain_in, 16)
            sp.wait_ge(x_clear, 1)
            sp.dma_start(xt[0:N_SAMPLE, :], x_sample[0]).then_inc(x_in, 16)
            sp.dma_start(xt[META0:META1, :], meta_tokens).then_inc(x_in, 16)
            sp.dma_start(consts[:, :], constants[:, 0:C_LEV]).then_inc(const_in, 16)
            sp.dma_start(w_fg, w_in[0, :, FG0:FG0 + HEADS].rearrange("(c p) n -> p c n", p=P)).then_inc(w_fg_in, 16)
            for n in (0, 1):
                sp.dma_start(w_ring[n], w_group(n)).then_inc(w_in_in[n], 16)
            sp.dma_start(x_all, x_prompt[0].rearrange("(t p) n -> p t n", p=P)).then_inc(x_later_in, 16)
            for n in (2, 3):
                sp.dma_start(w_ring[n], w_group(n)).then_inc(w_in_in[n], 16)
            sp.dma_start(b_fg, b_forget[0].partition_broadcast(P)).then_inc(lb_in, 16)
            sp.dma_start(lb[:, 0:HW], hg_lb_logits[0].partition_broadcast(P)).then_inc(lb_in, 16)
            sp.dma_start(lb[:, HW:2 * HW], hg_lb_logits[1].partition_broadcast(P)).then_inc(lb_in, 16)
            for n in (4, 5):
                sp.wait_ge(proj_done, n - 3)
                sp.dma_start(w_ring[w_slot[n]], w_group(n)).then_inc(w_in_in[w_slot[n]], 16)
            for par in range(2):
                sp.dma_start(k_sample[0:HD, par:HEADS:2, 0:PAST], cache_kt).then_inc(past_in, 16)
            sp.wait_ge(h_ready, 1)
            sp.dma_start(rows_t[:, :].rearrange("p (b n) -> p b n", n=KV_W),
                         cache_v.rearrange("(b p) n -> p b n", p=P)).then_inc(past_in, 16)
            sp.dma_start(cache_lf.rearrange("p (b h) -> p b h", h=HEADS),
                         cache_logf.rearrange("(b p) h -> p b h", p=P)).then_inc(past_in, 16)
            sp.dma_start(state[:, 1, :].rearrange("p (h v) -> p h v", h=HG),
                         state_hgrn.rearrange("h k v -> k h v")).then_inc(past_in, 16)
            sp.wait_ge(later_ready, 1)
            sp.dma_start(w1[:, 0:(NL + 1) * P], constants[:, C_LEV:C_LEV + (NL + 1) * P]).then_inc(masks_in, 16)
            for n in (6, 7):
                sp.wait_ge(proj_done, n - 1)
                sp.dma_start(w_ring[w_slot[n]], w_group(n)).then_inc(w_in_in[w_slot[n]], 16)
            sp.dma_start(hgain[:, :], hg_norm_gain[0].partition_broadcast(P)).then_inc(hgain_in, 16)
            sp.wait_ge(staged_act, 4)
            sp.dma_start(v_pr[0:N_META, 0, :], act[META0:META1, SV:SV + KV_W]).then_inc(past_in, 16)
            sp.wait_ge(staged_dve, 4)
            for of_sample, of_prompt, at, n in ((new_k_sample, new_k_prompt, SK, KV_W),
                                                (new_v_sample, new_v_prompt, SV, KV_W),
                                                (new_logf_sample, new_logf_prompt, SLF, HEADS)):
                sp.dma_start(of_sample, act[0:N_SAMPLE, at:at + n]).then_inc(first_stored, 16)
                sp.dma_start(of_prompt[0:N_META], act[META0:META1, at:at + n]).then_inc(first_stored, 16)
            for t in range(TILES):
                if t:
                    sp.wait_ge(ps_done, t)
                    if t == 1:
                        sp.wait_ge(stored, 16 * LATER_STORES)
                        sp.wait_ge(hq_stored, 16)
                    sp.dma_start(act[:, :], staged[t - 1]).then_inc(act_in, 16)
                sp.wait_ge(at_ready, HG * (t + 1))
                if t:
                    sp.dma_start(xm, x_prompt[0, (t - 1) * P:t * P, :]).then_inc(x2_in, 16)
                else:
                    sp.dma_start(xm[0:N_SAMPLE, :], x_sample[0]).then_inc(x2_in, 16)
                    sp.dma_start(xm[META0:META1, :], meta_tokens).then_inc(x2_in, 16)

                def load_w_out(c):
                    slot = c % WO_RING
                    sp.dma_start(w_out_sb[:, slot, :], w_out[0, c * P:(c + 1) * P, :]).then_inc(wo_in[slot], 16)

                sp.wait_ge(ho_done, HG * (t + 1))
                for c in range(WO_RING):
                    load_w_out(c)
                sp.wait_ge(mix_ready, t + 1)
                sp.wait_ge(st_done, ends_before(t + 1))
                sp.dma_start(gain_2, norm2_gain[0].partition_broadcast(P)).then_inc(gain_2_in, 16)
                if t == 0:
                    sp.wait_ge(first_stored, 16 * 6)
                sp.dma_start(keys_t, sub_keys_t).then_inc(keys_in, 16)
                for c in range(WO_RING, DC):
                    sp.wait_ge(wo_used, DC * t + c - WO_RING + 1)
                    load_w_out(c)
                if t == 0:
                    sp.wait_ge(st_new, 1)
                    sp.dma_start(new_state_sample.rearrange("h k v -> k h v"),
                                 state[:, 1, :].rearrange("p (h v) -> p h v", h=HG)).then_inc(state_saved, 16)
                sp.wait_ge(x1_ready, t + 1)
                sp.dma_start(x1_dram[t], xm).then_inc(x1_saved, 16)
                if t == 0:
                    sp.wait_ge(h2_copied, 1)
                    sp.dma_start(h2[N_SAMPLE:P, :], rows[0:N_SAMPLE, :]).then_inc(h2_doubled, 16)
                if t >= 2:
                    sp.wait_ge(y_part_ready, t - 1)
                    sp.dma_start(y_dram[t - 2], rows_t[:, :]).then_inc(y_part_saved, 16)
            sp.wait_ge(st_new, ends_before(TILES))
            sp.dma_start(new_state_prompt.rearrange("h k v -> k h v"),
                         state[:, 0, :].rearrange("p (h v) -> p h v", h=HG)).then_inc(state_saved, 16)

            sp.wait_ge(h2_copied, TILES)
            sp.dma_start(rows[:, :], final_norm_gain.partition_broadcast(P)).then_inc(final_gain_in, 16)
            sp.wait_ge(top_done, TILES)
            sp.wait_ge(x1_saved, 16 * TILES)
            for t in range(TILES):
                sp.dma_start(x1_all[:, t * D:(t + 1) * D], x1_dram[t]).then_inc(b_in, 16)
            sp.wait_ge(u_free, RING_U + columns_of(TILES - 1)[0])
            sp.wait_ge(v_free, RING_V + len(value_order))
            sp.wait_ge(y_part_ready, PARTS)
            sp.dma_start(y_dram[PARTS - 1], rows_t[:, :]).then_inc(y_part_saved, 16)
            sp.wait_ge(y_part_saved, 16 * PARTS)
            sp.dma_start(y_part, y_dram.rearrange("t p n -> p t n")).then_inc(y_part_in, 16)
            for t in range(TILES):
                sp.wait_ge(y_ready, t + 1)
                if t:
                    sp.dma_start(y_prompt[0, (t - 1) * P:t * P, :], x1_all[:, t * D:(t + 1) * D]).then_inc(y_saved, 16)
                else:
                    sp.dma_start(y_sample[0], x1_all[0:N_SAMPLE, 0:D]).then_inc(y_saved, 16)
            sp.wait_ge(y_saved, 16 * TILES)
            sp.wait_ge(state_saved, 32)

        @block.gpsimd
        def _(pool):
            def gather(k, table, slot, free, count, arrived):
                pool.wait_ge(free, count)
                pool.indirect_dma_start(slot, None, table[0],
                                        bass.IndirectOffsetOnAxis(ap=idx_all[:, k:k + 1], axis=0)
                                        ).then_inc(arrived, 16)

            n_cleared = 0
            for buf, first, end, value in ((qa, 64, P, 0.0), (lev, 64, P, 0.0), (k_pr, 64, P, 0.0), (qa, 96, 97, 1.0),
                                           (lev, 64, 65, 1.0), (k_pr, 64, 65, 1.0), (state[:, 0, :], 0, P, 0.0)):
                pool.memset(buf[first:end, :], value).then_inc(cleared, 1)
                n_cleared += 1
                pool.wait_ge(cleared, n_cleared)

            steps = [0]

            def link(ins):
                steps[0] += 1
                ins.then_inc(pool_step, 1)
                pool.wait_ge(pool_step, steps[0])

            def store(at, src, n=512):
                pool.dma_start(staged.rearrange("t p n -> p t n")[:, :, at:at + n], src).then_inc(stored, 16)

            def to_prompt(out, src):
                pool.dma_start(out[N_META:N_META + SEQ].rearrange("(t p) n -> p t n", p=P), src).then_inc(stored, 16)

            def load_w_query(c):
                pool.dma_start(w_query_sb[:, c, :], peer_w_query[0, c * P:(c + 1) * P, :]).then_inc(wq_in, 16)

            pool.wait_ge(lb_in, 48)
            pool.wait_ge(item_evac, 1)
            link(pool.tensor_tensor(later_u, later_u, b_fg.unsqueeze(1).to_broadcast([P, LATER, HEADS]), ALU.add))
            link(pool.tensor_scalar(later_a, later_u, 0.0, None, ALU.max))
            link(pool.tensor_scalar(later_f, later_u, 0.0, None, ALU.min))
            pool.tensor_tensor(later_a, later_a, later_f, ALU.subtract).then_inc(later_abs, 1)
            pool.wait_ge(later_ln, 1)
            link(pool.tensor_tensor(later_f, later_f, later_e, ALU.subtract))
            store(SLF, later_f, HEADS)
            to_prompt(new_logf_prompt, later_f)
            for g, group in enumerate(LATER_ORDER):
                pool.wait_ge(item_done, 1 + LATER * (g + 1))
                n = len(GROUP_COLS) + g + 2
                if n < 2 * len(GROUP_COLS):
                    pool.dma_start(w_ring[n % 2], w_group(n)).then_inc(w_late_in[n % 2], 16)
                if with_sigmoid(g):
                    pool.wait_ge(item_sigmoid, LATER * (g + 1))
                pool.wait_ge(item_evac, 1 + LATER * (g + 1))
                if group == G_HQ:
                    pool.tensor_tensor(buf_a, buf_a, buf_b, ALU.mult).then_inc(later_done, 1)
                    pool.wait_ge(later_done, 1)
                    pool.dma_start(staged.rearrange("t p n -> p t n")[:, :, SHQ:SHQ + 512], buf_a).then_inc(hq_stored, 16)
                elif group == G_HF:
                    per_tile = [P, LATER, HW]
                    link(pool.tensor_tensor(buf_c, buf_c, lb[:, HW:2 * HW].unsqueeze(1).to_broadcast(per_tile), ALU.mult))
                    link(pool.tensor_tensor(buf_c, buf_c, lb[:, 0:HW].unsqueeze(1).to_broadcast(per_tile), ALU.add))
                    pool.tensor_scalar(buf_d, buf_c, -1.0, 1.0, ALU.mult, ALU.add).then_inc(later_hf, 1)
                    pool.wait_ge(later_hf, 1)
                    store(SHK, buf_d)
                elif group == G_HGATE:
                    pool.tensor_tensor(buf_e, buf_e, buf_f, ALU.mult).then_inc(later_done, 1)
                    pool.wait_ge(later_done, 2)
                    store(SHG, buf_e)
                elif group == G_KV:
                    store(SK, buf_b)
                    to_prompt(new_k_prompt, buf_b[:, :, 0:KV_W])
                    to_prompt(new_v_prompt, buf_b[:, :, KV_W:2 * KV_W])
                    pool.wait_ge(later_hf_ln, 1)
                    store(SHL, buf_c)
                elif group == G_Q:
                    pool.wait_ge(stored, 16 * (LATER_STORES - 2))
                    pool.wait_ge(hq_stored, 16)
                    for c in (0, 5, 6, 7):
                        load_w_query(c)
                    store(SQ, buf_f)
                else:
                    pool.wait_ge(stored, 16 * (LATER_STORES - 1))
                    for c in (1, 2, 3):
                        load_w_query(c)
                    store(SHI, buf_a)
            pool.wait_ge(stored, 16 * LATER_STORES)
            load_w_query(4)
            pool.dma_start(v_pr[:, 1:TILES, :], staged.rearrange("t p n -> p t n")[:, :, SV:SV + KV_W]
                           ).then_inc(v_in_later, 16)
            for t in range(TILES):
                for place, _, _ in PLACES:
                    of_keys, of_values, tile = plan[t, place]
                    if of_keys and of_keys[0] == columns_of(t - 1)[0]:
                        pool.wait_ge(chosen, t)
                    for i in range(max(len(of_keys), len(of_values))):
                        if i < len(of_keys):
                            k = of_keys[i]
                            gather(k, peer_expert_u, ring_u[:, k % RING_U, :], u_free, k + 1, u_in[k % RING_U])
                        if i < len(of_values):
                            k = of_values[i]
                            n = value_rank[k]
                            gather(k, peer_expert_v, ring_v[:, n % RING_V, :], v_free, n + 1, v_in[n % RING_V])

            beside = list(columns_of(TILES - 1))
            m = 0
            for t, group in late:
                for n in range(late_before[t], late_before[t] + late_groups(t)):
                    for j in range(GROUP):
                        k = (group + n - late_before[t]) * GROUP + j
                        if j in DVE_SLOTS:
                            i = DVE_SLOTS.index(j)
                            gather(k, peer_expert_v, ring_d[:, i, :], d_free, ND * n + i + 1, d_in[i])
                        else:
                            i = PE_SLOTS.index(j)
                            gather(k, peer_expert_v, ring_p[:, i, :], p_free, NPE * n + i + 2, p_in[i])
                        if n >= KEYS_FROM and m < len(beside):
                            if m == 0:
                                pool.wait_ge(chosen, TILES)
                            gather(beside[m], peer_expert_u, ring_l[:, m % RING_L, :], l_free, m + 1, l_in[m % RING_L])
                            m += 1

        @block.scalar
        def _(eng):
            steps = [0]

            def link(ins):
                steps[0] += 1
                ins.then_inc(act_step, 1)
                eng.wait_ge(act_step, steps[0])

            roots = [0]

            def inverse_root(n):
                roots[0] += 1
                eng.wait_ge(square_ready, roots[0])
                link(eng.activation(rstd[:, 0:n], ss[:, 0:n], ACT.Ln))
                eng.activation(rstd[:, 0:n], rstd[:, 0:n], ACT.Exp, scale=-0.5).then_inc(root_ready, 1)

            inverse_root(1)
            eng.wait_ge(tr_done, 1)
            eng.activation(h2[:, :], PA[:, :], ACT.Copy).then_inc(ht_evac, 1)
            eng.wait_ge(lb_less, 1)
            eng.activation(lb, lb, ACT.Exp).then_inc(lb_exp, 1)
            inverse_root(LATER)
            eng.wait_ge(fg_abs, 1)
            link(eng.activation(fg_e, fg_a, ACT.Exp, scale=-1.0))
            eng.activation(fg_l, fg_e, ACT.Ln, bias=1.0).then_inc(fg_ln, 1)

            def later_evac_of(t):
                eng.wait_ge(later_turned, t + 1)
                eng.activation(xt_all[:, t, :], PA[:, :], ACT.Copy).then_inc(later_evac, 1)

            eng.wait_ge(proj_done, 1)
            eng.activation(w2[:, 0:512], PC[:, 0:512], ACT.Exp, scale=-1.0).then_inc(e_done, 1)
            eng.wait_ge(proj_done, 2)
            eng.activation(w2[:, 512:1024], PC[:, 512:1024], ACT.Exp, scale=-1.0).then_inc(e_done, 1)
            eng.wait_ge(proj_done, 3)
            eng.activation(act[:, SHI:SHI + 512], PD[:, 0:512], ACT.Copy).then_inc(staged_act, 1)
            later_evac_of(0)
            eng.wait_ge(proj_done, 4)
            eng.activation(w2[:, 1024:1536], PD[:, 512:1024], ACT.Exp, scale=-1.0).then_inc(e_done, 1)
            eng.wait_ge(f_ready, 1)
            eng.activation(act[:, SHL:SHL + 512], w2[:, 512:1024], ACT.Ln).then_inc(staged_act, 1)
            later_evac_of(1)
            eng.wait_ge(proj_done, 5)
            eng.activation(act[:, SQ:SQ + 512], PB[:, 0:512], ACT.Copy).then_inc(staged_act, 1)
            later_evac_of(2)
            eng.wait_ge(proj_done, 6)
            eng.activation(act[:, SK:SK + 512], PB[:, 512:1024], ACT.Copy).then_inc(staged_act, 1)
            later_evac_of(3)

            def item_evacs(t, place):
                if t:
                    return
                for n in item_plan[place]:
                    eng.wait_ge(item_done, n + 1)
                    psum = PD[:, 512 * (n % 2):512 * (n % 2) + 512]
                    if n == 0:
                        eng.activation(later_u, psum[:, 0:LATER * HEADS].rearrange("p (t n) -> p t n", n=HEADS),
                                       ACT.Copy).then_inc(item_evac, 1)
                        continue
                    g, i = group_of(n)
                    group = LATER_ORDER[g]
                    if i == 0 and group == G_KV:
                        eng.wait_ge(later_done, 1)
                    if i == 0 and group == G_Q:
                        eng.wait_ge(later_done, 2)
                    if i == 0 and group == G_HI:
                        eng.wait_ge(hq_stored, 16)
                    raw = {G_HQ: buf_a, G_HGATE: buf_e, G_KV: buf_b, G_Q: buf_f, G_HI: buf_a}.get(group)
                    e = {G_HQ: buf_b, G_HF: buf_c, G_HGATE: buf_f}.get(group)
                    if raw is not None:
                        last = eng.activation(raw[:, i, :], psum, ACT.Copy)
                    if e is not None:
                        last = eng.activation(e[:, i, :], psum, ACT.Exp, scale=-1.0)
                    last.then_inc(item_evac, 1)
                    if group == G_HQ and i == 0:
                        eng.wait_ge(later_abs, 1)
                        link(eng.activation(later_e, later_a, ACT.Exp, scale=-1.0))
                        eng.activation(later_e, later_e, ACT.Ln, bias=1.0).then_inc(later_ln, 1)
                    if group == G_HGATE and i == LATER - 1:
                        eng.wait_ge(later_hf, 1)
                        eng.activation(buf_c, buf_c, ACT.Ln).then_inc(later_hf_ln, 1)

            def diagonals(t, place):
                _, of_values, tile = plan[t, place]
                for k in of_values:
                    n = value_rank[k]
                    if k == early_columns(tile)[0]:
                        eng.wait_ge(wgt_done, tile + 1)
                        eng.wait_ge(stored, 16 * LATER_STORES)
                    if n >= RING_V:
                        eng.wait_ge(v_free, n + 1)
                    base = consts[:, C_ID:C_ID + P] if tile else consts[:, C_FOLD:C_FOLD + P]
                    eng.activation(diag_v[:, (n % RING_V) * P:(n % RING_V + 1) * P], base, ACT.Copy,
                                   scale=dots_all[:, k:k + 1]).then_inc(vdiag_done, 1)

            for t in range(TILES):
                eng.wait_ge(qk_turned, t + 1)
                if t == 0:
                    eng.wait_ge(cleared, 7)
                eng.activation(qa[0:HD, :], PA[0:HD, :], ACT.Copy, scale=SCALE).then_inc(q_ready, 1)
                for b, (_, _, n, _, _, q0, _) in enumerate(f_blocks(t)):
                    if q0 is not None:
                        eng.wait_ge(f_k, 2 * (f_before(t) + b + 1))
                        eng.activation(qa[64:65, :].rearrange("p (h q) -> p h q", h=HEADS)[:, :, q0:q0 + n],
                                       PC[0:1, :].rearrange("p (h q) -> p h q", h=HEADS)[:, :, 0:n],
                                       ACT.Copy).then_inc(f_q, 1)
                    if t == 0 and b >= LATER - 1:
                        item_evacs(t, f"sum{b}")
                diagonals(t, "start")
                item_evacs(t, "start")

                def exponentials(a, q, h):
                    _, m, _, n, _ = q
                    eng.wait_ge(sc_max, a + 1)
                    if a >= 2:
                        eng.wait_ge(pt_done, a - 1)
                    eng.activation(w1[0:m, D * (a % 2):D * (a % 2) + n], score_psum(a, n)[0:m, :], ACT.Exp,
                                   bias=negmax[0:m, h:h + 1], accum_out=psums[0:m, h:h + 1]).then_inc(p_done, 1)

                def turned(a, q):
                    _, m, _, _, blocks = q
                    eng.wait_ge(pt_done, a + 1)
                    if a >= 2:
                        eng.wait_ge(o_done, a - 1)
                    src = PB[:, 0:5 * P].rearrange("p (b q) -> p b q", q=P)
                    dst = w2[:, D * (a % 2):D * (a % 2) + 5 * P].rearrange("p (b q) -> p b q", q=P)
                    whole = [i for i, (_, k) in enumerate(blocks) if k == P]
                    short = [(i, k) for i, (_, k) in enumerate(blocks) if k < P][0]
                    if whole:
                        eng.activation(dst[:, whole[0]:whole[-1] + 1, 0:m], src[:, whole[0]:whole[-1] + 1, 0:m],
                                       ACT.Copy).then_inc(pt_evac, 1)
                    i, k = short
                    eng.activation(dst[0:k, i, 0:m], src[0:k, i, 0:m], ACT.Copy).then_inc(pt_evac, 1 if whole else 2)

                a = heads_before(t)
                for n_q, q in enumerate(problems(t)):
                    if n_q:
                        eng.wait_ge(att_done, 1)
                    for h in range(HEADS):
                        exponentials(a + h, q, h)
                        if h:
                            turned(a + h - 1, q)
                        if n_q == 0:
                            diagonals(t, f"head{h}")
                        item_evacs(t, ("head", "meta")[n_q] + str(h))
                    turned(a + HEADS - 1, q)
                    a += HEADS

                eng.wait_ge(hg_in, t + 1)
                eng.activation(w1[:, 0:D], PA[:, :], ACT.Copy).then_inc(hg_in_evac, 1)
                eng.activation(w1[:, D:D + HW], PB[:, 0:HW], ACT.Copy).then_inc(hg_in_evac, 1)
                diagonals(t, "levels")
                item_evacs(t, "levels")
                eng.wait_ge(lev_ready, t + 1)
                exps = lev[:, first_level(t) * HW:(NL + 2) * HW]
                eng.activation(exps, exps, ACT.Exp).then_inc(lev_exp, 1)
                eng.wait_ge(ke_done, t + 1)
                eng.activation(w2[:, 0:HW], PB[:, HW:2 * HW], ACT.Copy).then_inc(ke_evac, 1)
                for place in ("masks", "gram1", "gram2"):
                    diagonals(t, place)
                    item_evacs(t, place)
                eng.wait_ge(ho_done, HG * (t + 1))
                eng.activation(w1[:, 0:HW], PC[:, HW:2 * HW], ACT.Copy).then_inc(ho_evac, 1)
                diagonals(t, "norm")
                item_evacs(t, "norm")
                inverse_root(HG)
                eng.wait_ge(mixt_done, t + 1)
                if t > 2:
                    eng.wait_ge(y_part_saved, 16 * (t - 2))
                eng.activation(rows_t[:, :], PA[:, :], ACT.Copy).then_inc(mixt_evac, 1)
                inverse_root(1)
                diagonals(t, "rows")
                eng.wait_ge(h2t_done, t + 1)
                eng.activation(rows_t[:, :], PA[:, :], ACT.Copy).then_inc(h2t_evac, 1)
                eng.wait_ge(pq_done, 2 * t + 1)
                nq = P if t else N_SAMPLE
                eng.activation(w1[0:nq, 0:D], PB[0:nq, :], ACT.Copy).then_inc(pq_evac, 1)
                if t:
                    cols = columns_of(t - 1)
                    eng.wait_ge(u_free, RING_U + cols[-1] + 1)
                n = P if t else N_SAMPLE
                eng.activation(h2[0:n, :], rows[0:n, :], ACT.Copy).then_inc(h2_copied, 1)
                if t:
                    eng.activation(dots_all[:, cols[0]:cols[-1] + 1], dots_all[:, cols[0]:cols[-1] + 1],
                                   ACT.Gelu).then_inc(gelu_done, 1)
                eng.wait_ge(pq_done, 2 * t + 2)
                eng.activation(w1[0:nq, D:2 * D], PC[0:nq, :], ACT.Copy).then_inc(pq_evac, 1)
                for n, psum in enumerate((PB, PC)):
                    eng.wait_ge(qt_done, 2 * t + n + 1)
                    eng.activation(queries_t[n].rearrange("p (m q) -> p m q", q=P)[:, :, 0:nq],
                                   psum[:, :].rearrange("p (m q) -> p m q", q=P)[:, :, 0:nq],
                                   ACT.Copy).then_inc(qt_evac, 1)
                if t >= 2:
                    eng.wait_ge(v_free, RING_V + value_rank[early_columns(t - 2)[-1]] + 1)
                    eng.activation(rows_t[:, :], PD[:, :], ACT.Copy).then_inc(y_part_ready, 1)
                diagonals(t, "top")
                if t == TILES - 1:
                    eng.wait_ge(y_part_saved, 16 * (PARTS - 1))
                    eng.wait_ge(v_free, RING_V + len(value_order))
                    eng.activation(rows_t[:, :], PD[:, :], ACT.Copy).then_inc(y_part_ready, 1)
                eng.wait_ge(less_max, t + 1)
                gates = gate_new[:, 0:TOPK * top_heads(t)]
                eng.activation(gates, gates, ACT.Exp).then_inc(gate_exp, 1)

            last = columns_of(TILES - 1)
            eng.wait_ge(ps_done, TILES)
            for t, group in late:
                if t == TILES - 1:
                    eng.wait_ge(l_free, RING_L + SLOTS)
                    eng.activation(dots_all[:, last[0]:last[-1] + 1], dots_all[:, last[0]:last[-1] + 1],
                                   ACT.Gelu).then_inc(gelu_done, 1)
                eng.wait_ge(wgt_done, t + 1)
                before = late_before[t]
                with eng.Fori(0, late_groups(t) // 2) as pair:
                    for half in range(2):
                        eng.wait_ge(p_free, pair * (2 * NPE) + ((before + half) * NPE + 1))
                        for i, j in enumerate(PE_SLOTS):
                            at = pair * (2 * GROUP) + ((group + half) * GROUP + j)
                            place = (half * NPE + i) * P
                            eng.activation(act[:, place:place + P], ident, ACT.Copy,
                                           scale=dots_all[:, bass.ds(at, 1)]).then_inc(diag_done, 1)
                if t == 1:
                    inverse_root(1)
                inverse_root(1)

        @block.tensor
        def _(pe):
            pe.wait_ge(const_in, 16)

            def product(out, x, weights, done):
                for c in range(DC):
                    last = pe.matmul(out, x[:, c * P:(c + 1) * P], weights[:, c, :], start=(c == 0), stop=(c == DC - 1))
                last.then_inc(done, 1)

            def turn_later(t):
                pe.wait_ge(later_ready, 1)
                if t:
                    pe.wait_ge(later_evac, t)
                for c in range(DC):
                    last = pe.transpose(PA[:, c * P:(c + 1) * P], x_all[:, t, c * P:(c + 1) * P], ident)
                last.then_inc(later_turned, 1)

            pe.wait_ge(h_ready, 1)
            for c in range(DC):
                last = pe.transpose(PA[:, c * P:(c + 1) * P], rows[:, c * P:(c + 1) * P], ident)
            last.then_inc(tr_done, 1)
            pe.wait_ge(ht_evac, 1)
            pe.wait_ge(w_fg_in, 16)
            product(PA[:, 0:HEADS], h2, w_fg, fg_done)
            psum_of = {G_HQ: PC[:, 0:512], G_HF: PC[:, 512:1024], G_HI: PD[:, 0:512], G_HGATE: PD[:, 512:1024],
                       G_Q: PB[:, 0:512], G_KV: PB[:, 512:1024]}
            for n, group in enumerate(FIRST_ORDER):
                pe.wait_ge(w_in_in[w_slot[n]], 16 * w_fills[n])
                product(psum_of[group], h2, w_ring[w_slot[n]], proj_done)
                if n >= len(FIRST_ORDER) - LATER:
                    if n == len(FIRST_ORDER) - LATER:
                        pe.wait_ge(fg_used, 1)
                    turn_later(n - len(FIRST_ORDER) + LATER)

            def later_forget_gates(i):
                if i >= LATER:
                    return
                if i == 0:
                    pe.wait_ge(staged_act, 4)
                    pe.wait_ge(staged_dve, 4)
                    pe.wait_ge(later_evac, LATER)
                for c in range(DC):
                    last = pe.matmul(PD[:, i * HEADS:(i + 1) * HEADS], xt_all[:, i, c * P:(c + 1) * P],
                                     w_fg[:, c, :], start=(c == 0), stop=(c == DC - 1))
                if i == LATER - 1:
                    last.then_inc(item_done, 1)

            def project_items(t, place):
                if t:
                    return
                for n in item_plan[place]:
                    if n >= 2:
                        pe.wait_ge(item_evac, n - 1)
                    psum = PD[:, 512 * (n % 2):512 * (n % 2) + 512]
                    if n == 0:
                        continue
                    g, i = group_of(n)
                    if i == 0 and g < 2:
                        n_load = len(GROUP_COLS) + g
                        pe.wait_ge(w_in_in[w_slot[n_load]], 16 * w_fills[n_load])
                    elif i == 0:
                        pe.wait_ge(w_late_in[g % 2], 16 * (g // 2))
                    product(psum, xt_all[:, i, :], w_ring[g % 2], item_done)

            def weighted(psum, diag, value, first, last):
                for half in range(2):
                    ins = pe.matmul(psum[:, half * 512:(half + 1) * 512], diag,
                                    value[:, half * 512:(half + 1) * 512], start=first, stop=last)
                return ins

            def early_values(t, place):
                _, of_values, tile = plan[t, place]
                for k in of_values:
                    n = value_rank[k]
                    run = early_columns(tile)
                    if k == run[0] and tile == 0:
                        pe.wait_ge(item_evac, ITEMS)
                    if k == run[0] and tile:
                        pe.wait_ge(y_part_ready, tile)
                    pe.wait_ge(v_in[n % RING_V], 16 * (n // RING_V + 1))
                    pe.wait_ge(vdiag_done, n + 1)
                    weighted(PD, diag_v[:, (n % RING_V) * P:(n % RING_V + 1) * P], ring_v[:, n % RING_V, :],
                             k == run[0], k == run[-1]).then_inc(v_free, 1)

            for t in range(TILES):
                if t:
                    pe.wait_ge(act_in, 16 * t)
                    pe.wait_ge(ps_read, t)
                else:
                    pe.wait_ge(staged_act, 4)
                    pe.wait_ge(later_evac, LATER)
                for h in range(HEADS):
                    pe.transpose(PA[0:HD, h * P:(h + 1) * P], act[:, SQ + HD * h:SQ + HD * (h + 1)], ident)
                for g in range(KV_HEADS):
                    last = pe.transpose(PB[0:HD, g * P:(g + 1) * P], act[:, SK + HD * g:SK + HD * (g + 1)], ident)
                last.then_inc(qk_turned, 1)
                if t == 0:
                    pe.wait_ge(past_in, 16 * 6)
                    pe.wait_ge(staged_dve, 4)
                if t == 1:
                    pe.wait_ge(v_in_later, 16)
                for b, (gates, r0, n, _, _, _, goes_on) in enumerate(f_blocks(t)):
                    i = f_before(t) + b
                    if i:
                        pe.wait_ge(f_k, 2 * i)
                    if fq_before(t) + (b == len(f_blocks(t)) - 1 and t == 0):
                        pe.wait_ge(f_q, fq_before(t) + (b == len(f_blocks(t)) - 1 and t == 0))
                    if t:
                        pe.wait_ge(qt_evac, 2 * t)
                    for h in range(HEADS):
                        out = PC[0:1, h * P:h * P + n]
                        last = pe.matmul(out, gates[r0:r0 + n, h:h + 1],
                                         consts[r0:r0 + n, C_TRI + r0:C_TRI + r0 + n], start=True, stop=not goes_on)
                        if goes_on:
                            last = pe.matmul(out, carry[:, h:h + 1], ones[:, 0:n], start=False, stop=True)
                    last.then_inc(f_done, 1)
                    if t == 0:
                        later_forget_gates(b)
                        if b >= LATER - 1:
                            project_items(t, f"sum{b}")

                early_values(t, "start")
                project_items(t, "start")
                pe.wait_ge(q_ready, t + 1)
                pe.wait_ge(k_ready, 2 * (t + 1))
                pe.wait_ge(f_q, fq_before(t + 1))
                pe.wait_ge(f_k, 2 * f_before(t + 1))

                def scores(a, q, h):
                    q0, m, keys, n, _ = q
                    if n > 512 or h == 0:
                        pe.wait_ge(p_done, a)
                    else:
                        pe.wait_ge(p_done, a - 1)
                    for k0 in range(0, n, 512):
                        k1 = min(n, k0 + 512)
                        last = pe.matmul(score_psum(a, n)[0:m, k0:k1], qa[:, h * P + q0:h * P + q0 + m],
                                         keys[:, h, k0:k1], start=True, stop=True)
                    last.then_inc(sc_done, 1)

                def turn_probs(a, q):
                    q0, m, _, _, blocks = q
                    pe.wait_ge(p_done, a + 1)
                    if a:
                        pe.wait_ge(pt_evac, 2 * a)
                    for i, (k0, k) in enumerate(blocks):
                        p0 = D * (a % 2) + k0
                        last = pe.transpose(PB[0:k, i * P:i * P + m], w1[0:m, p0:p0 + k], ident[0:m, 0:m])
                    last.then_inc(pt_done, 1)

                def values(a, q, h):
                    q0, m, _, _, blocks = q
                    pe.wait_ge(pt_evac, 2 * (a + 1))
                    for i, (k0, k) in enumerate(blocks):
                        at = D * (a % 2) + i * P
                        last = pe.matmul(PC[0:m, h * HD:(h + 1) * HD], w2[0:k, at:at + m],
                                         value_rows(t, q0, i, k, h // (HEADS // KV_HEADS)),
                                         start=(i == 0), stop=(i == len(blocks) - 1))
                    last.then_inc(o_done, 1)

                a = heads_before(t)
                for n_q, q in enumerate(problems(t)):
                    if n_q:
                        pe.wait_ge(att_done, 1)
                    for h in range(HEADS):
                        scores(a + h, q, h)
                        if h:
                            turn_probs(a + h - 1, q)
                        if n_q == 0:
                            early_values(t, f"head{h}")
                        project_items(t, ("head", "meta")[n_q] + str(h))
                        if h:
                            values(a + h - 1, q, h - 1)
                    turn_probs(a + HEADS - 1, q)
                    values(a + HEADS - 1, q, HEADS - 1)
                    a += HEADS

                pe.wait_ge(p_done, a)
                tri = consts[:, (C_TRI if t else C_TRIS):(C_TRI if t else C_TRIS) + P]
                for h in range(HG):
                    cols = slice(h * HK, (h + 1) * HK)
                    pe.matmul(PA[:, cols], act[:, SHL + h * HK:SHL + (h + 1) * HK], tri, start=True, stop=True)
                for h in range(HG):
                    pe.transpose(PA[:, HW + h * HK:HW + (h + 1) * HK], act[:, SHQ + h * HK:SHQ + (h + 1) * HK], ident)
                for h in range(HG):
                    last = pe.transpose(PB[:, h * HK:(h + 1) * HK], act[:, SHK + h * HK:SHK + (h + 1) * HK], ident)
                last.then_inc(hg_in, 1)
                early_values(t, "levels")
                project_items(t, "levels")
                pe.wait_ge(hg_in_evac, 2 * (t + 1))
                pe.wait_ge(lev_mul, t + 1)
                for h in range(HG):
                    last = pe.transpose(PB[:, HW + h * HK:HW + (h + 1) * HK],
                                        lev[:, NL * HW + h * HK:NL * HW + (h + 1) * HK], ident)
                last.then_inc(ke_done, 1)
                early_values(t, "masks")
                project_items(t, "masks")

                def grams(h):
                    if h == 1:
                        pe.wait_ge(ke_evac, t + 1)
                    if h >= 2:
                        pe.wait_ge(at_ready, HG * t + h - 1)
                    psum = (PA, PB)[h % 2]
                    for l in range(first_level(t), NL):
                        both = lev[:, l * HW + h * HK:l * HW + (h + 1) * HK]
                        pe.matmul(psum[:, l * P:(l + 1) * P], both, both, start=True, stop=True)
                    pe.matmul(psum[:, NL * P:(NL + 1) * P], w1[:, D + h * HK:D + (h + 1) * HK],
                              w1[:, HW + h * HK:HW + (h + 1) * HK], start=True, stop=True).then_inc(gram_done, 1)

                def outputs(h):
                    pe.wait_ge(at_ready, HG * t + h + 1)
                    m = P if t else N_SAMPLE
                    col = HW + h * HK
                    pe.matmul(PC[:, col:col + HK], w1[:, D + HW + h * P:D + HW + (h + 1) * P],
                              act[:, SHI + h * HK:SHI + (h + 1) * HK], start=True, stop=False, skip_group_check=True)
                    pe.matmul(PC[0:m, col:col + HK], lev[:, (NL + 1) * HW + h * HK:(NL + 1) * HW + h * HK + m],
                              state[:, 0 if t else 1, h * HK:(h + 1) * HK], start=False, stop=True,
                              skip_group_check=True).then_inc(ho_done, 1)

                if t:
                    pe.wait_ge(st_new, ends_before(t))
                for h in range(HG):
                    grams(h)
                    if h:
                        outputs(h - 1)
                    if h in (1, 2):
                        early_values(t, f"gram{h}")
                        project_items(t, f"gram{h}")
                outputs(HG - 1)
                pe.wait_ge(ke_evac, t + 1)
                pe.wait_ge(att_done, heads_before(t + 1) // HEADS)
                for _, r0, n, psum in ends(t):
                    for h in range(HG):
                        last = pe.matmul(psum[:, h * HK:(h + 1) * HK], w2[r0:r0 + n, h * HK:(h + 1) * HK],
                                         act[r0:r0 + n, SHI + h * HK:SHI + (h + 1) * HK], start=True, stop=True)
                    last.then_inc(st_done, 1)

                early_values(t, "norm")
                project_items(t, "norm")
                pe.wait_ge(mix_ready, t + 1)
                for c in range(DC):
                    last = pe.transpose(PA[:, c * P:(c + 1) * P], rows[:, c * P:(c + 1) * P], ident)
                last.then_inc(mixt_done, 1)
                pe.wait_ge(mixt_evac, t + 1)
                pe.wait_ge(st_new, ends_before(t + 1))
                for c in range(DC):
                    slot = c % WO_RING
                    per_tile = len(range(slot, DC, WO_RING))
                    pe.wait_ge(wo_in[slot], 16 * (per_tile * t + c // WO_RING + 1))
                    for half in range(2):
                        last = pe.matmul(PB[:, half * 512:(half + 1) * 512], rows_t[:, c * P:(c + 1) * P],
                                         w_out_sb[:, slot, half * 512:(half + 1) * 512],
                                         start=(c == 0), stop=(c == DC - 1))
                    last.then_inc(wo_used, 1)
                early_values(t, "rows")
                pe.wait_ge(h2_ready, t + 1)
                for c in range(DC):
                    last = pe.transpose(PA[:, c * P:(c + 1) * P], rows[:, c * P:(c + 1) * P], ident)
                last.then_inc(h2t_done, 1)
                pe.wait_ge(h2t_evac, t + 1)
                if t == 0:
                    pe.wait_ge(wq_in, 16 * DC)
                nq = P if t else N_SAMPLE
                for n, psum in enumerate((PB, PC)):
                    if n:
                        pe.wait_ge(ho_evac, t + 1)
                    else:
                        pe.wait_ge(x1_ready, t + 1)
                    for half in range(2):
                        first = n * D + half * 512
                        for c in range(DC):
                            last = pe.matmul(psum[0:nq, half * 512:half * 512 + 512], rows_t[:, c * P:c * P + nq],
                                             w_query_sb[:, c, first:first + 512], start=(c == 0), stop=(c == DC - 1))
                    last.then_inc(pq_done, 1)
                for n, psum in enumerate((PB, PC)):
                    pe.wait_ge(pq_evac, 2 * t + n + 1)
                    for m in range(PH):
                        i = n * PH + m
                        last = pe.transpose(psum[:, m * P:m * P + nq], w1[0:nq, i * P:(i + 1) * P], ident[0:nq, 0:nq])
                    last.then_inc(qt_done, 1)
                pe.wait_ge(keys_in, 16 * (t + 1))
                for n, psum in enumerate((PA, PB)):
                    pe.wait_ge(qt_evac, 2 * t + n + 1)
                    for m in range(PH):
                        i = n * PH + m
                        out = psum[:, :] if t else PA[n * N_SAMPLE:(n + 1) * N_SAMPLE, :]
                        last = pe.matmul(out[:, m * NKEY:(m + 1) * NKEY], queries_t[n][:, m * P:m * P + nq],
                                         keys_t[:, i * NKEY:(i + 1) * NKEY], start=True, stop=True)
                last.then_inc(ps_done, 1)
                early_values(t, "top")

            pe.sem_inc(p_free, NPE + 1)
            pe.sem_inc(d_free, ND)
            pe.sem_inc(y_even_added, 1)
            pe.sem_inc(y_odd_added, 1)
            pe.wait_ge(y_part_ready, PARTS)
            pe.wait_ge(qt_evac, 2 * TILES)
            with pe.Fori(0, late_total // 2) as pair:
                for half in range(2):
                    pe.wait_ge((y_even_added, y_odd_added)[half], pair + 1)
                    for i in range(NPE):
                        pe.wait_ge(p_in[i], pair * 32 + 16 * (half + 1))
                        pe.wait_ge(diag_done, pair * (2 * NPE) + (half * NPE + i + 1))
                        place = (half * NPE + i) * P
                        weighted((PC, PD)[half], act[:, place:place + P], ring_p[:, i, :],
                                 i == 0, i == NPE - 1).then_inc(p_free, 1)

        @block.vector
        def _(eng):
            steps = [0]

            def link(ins):
                steps[0] += 1
                ins.then_inc(dve_step, 1)
                eng.wait_ge(dve_step, steps[0])

            roots = [0]

            def inverse_root(n, width):
                roots[0] += 1
                x, y, z = ss[:, 0:n], rstd[:, 0:n], newton[:, 0:n]
                eng.tensor_scalar(x, x, 1.0 / width, EPS, ALU.mult, ALU.add).then_inc(square_ready, 1)
                eng.wait_ge(root_ready, roots[0])
                link(eng.tensor_tensor(z, y, y, ALU.mult))
                link(eng.tensor_tensor(z, z, x, ALU.mult))
                link(eng.tensor_scalar(z, z, -0.5, 1.5, ALU.mult, ALU.add))
                link(eng.tensor_tensor(y, y, z, ALU.mult))

            def mean_square(src, scratch):
                link(eng.tensor_tensor_reduce(scratch, src, src, 1.0, 0.0, ALU.mult, ALU.add, ss[:, 0:1]))
                inverse_root(1, D)

            eng.memset(xt[:, :], 0.0).then_inc(x_clear, 1)
            eng.wait_ge(x_clear, 1)
            eng.wait_ge(gain_in, 16)
            eng.wait_ge(x_in, 32)
            mean_square(xt[:, :], w1[:, 0:D])
            eng.scalar_tensor_tensor(out=rows[:, :], in0=xt[:, :], scalar=rstd[:, 0:1], in1=gain_1,
                                     op0=ALU.mult, op1=ALU.mult).then_inc(h_ready, 1)
            eng.wait_ge(lb_in, 48)
            most = w1[:, D:D + HW]
            link(eng.tensor_tensor(most, lb[:, 0:HW], lb[:, HW:2 * HW], ALU.max))
            link(eng.tensor_tensor(lb[:, 0:HW], lb[:, 0:HW], most, ALU.subtract))
            eng.tensor_tensor(lb[:, HW:2 * HW], lb[:, HW:2 * HW], most, ALU.subtract).then_inc(lb_less, 1)
            eng.wait_ge(x_later_in, 16)
            for i in range(LATER):
                link(eng.tensor_tensor_reduce(w1[:, 0:D], x_all[:, i, :], x_all[:, i, :], 1.0, 0.0, ALU.mult, ALU.add,
                                              ss[:, i:i + 1]))
            inverse_root(LATER, D)
            for i in range(LATER):
                last = eng.scalar_tensor_tensor(out=x_all[:, i, :], in0=x_all[:, i, :], scalar=rstd[:, i:i + 1],
                                                in1=gain_1, op0=ALU.mult, op1=ALU.mult)
            last.then_inc(later_ready, 1)
            eng.wait_ge(lb_exp, 1)
            link(eng.tensor_tensor(most, lb[:, 0:HW], lb[:, HW:2 * HW], ALU.add))
            link(eng.reciprocal(most, most))
            link(eng.tensor_tensor(lb[:, 0:HW], lb[:, 0:HW], most, ALU.mult))
            link(eng.tensor_scalar(lb[:, HW:2 * HW], lb[:, 0:HW], -1.0, 1.0, ALU.mult, ALU.add))
            eng.wait_ge(fg_done, 1)
            eng.tensor_tensor(fg_u, PA[:, 0:HEADS], b_fg, ALU.add).then_inc(fg_used, 1)
            eng.wait_ge(fg_used, 1)
            eng.scalar_tensor_tensor(out=fg_a, in0=fg_u, scalar=-1.0, in1=fg_u, op0=ALU.mult, op1=ALU.max).then_inc(fg_abs, 1)
            eng.wait_ge(fg_ln, 1)
            eng.scalar_tensor_tensor(out=act[:, SLF:SLF + HEADS], in0=fg_u, scalar=0.0, in1=fg_l,
                                     op0=ALU.min, op1=ALU.subtract).then_inc(staged_dve, 1)

            def sigmoid(e):
                link(eng.tensor_scalar(e, e, 1.0, None, ALU.add))
                link(eng.reciprocal(e, e))

            eng.wait_ge(e_done, 1)
            sigmoid(w2[:, 0:512])
            eng.tensor_tensor(act[:, SHQ:SHQ + 512], PC[:, 0:512], w2[:, 0:512], ALU.mult).then_inc(staged_dve, 1)
            eng.wait_ge(e_done, 2)
            f = w2[:, 512:1024]
            sigmoid(f)
            link(eng.tensor_tensor(f, f, lb[:, HW:2 * HW], ALU.mult))
            eng.tensor_tensor(f, f, lb[:, 0:HW], ALU.add).then_inc(f_ready, 1)
            eng.wait_ge(f_ready, 1)
            eng.tensor_scalar(act[:, SHK:SHK + 512], f, -1.0, 1.0, ALU.mult, ALU.add).then_inc(staged_dve, 1)
            eng.wait_ge(e_done, 3)
            sigmoid(w2[:, 1024:1536])
            eng.tensor_tensor(act[:, SHG:SHG + 512], PD[:, 512:1024], w2[:, 1024:1536],
                              ALU.mult).then_inc(staged_dve, 1)
            eng.wait_ge(masks_in, 16)
            eng.tensor_copy(level_masks[:, :], w1[:, 0:(NL + 1) * P]).then_inc(masks_ready, 1)
            eng.wait_ge(masks_ready, 1)

            def item_sigmoids(t, place):
                if t:
                    return
                for n in sigmoid_plan[place]:
                    if n == 0 or not with_sigmoid(group_of(n)[0]):
                        continue
                    g, i = group_of(n)
                    e = {G_HQ: buf_b, G_HF: buf_c, G_HGATE: buf_f}[LATER_ORDER[g]][:, i, :]
                    eng.wait_ge(item_evac, n + 1)
                    link(eng.tensor_scalar(e, e, 1.0, None, ALU.add))
                    eng.reciprocal(e, e).then_inc(item_sigmoid, 1)

            def dot(slot, out, free):
                eng.scalar_tensor_tensor(out=slot, in0=slot, scalar=1.0, in1=h2[:, :], op0=ALU.mult,
                                         op1=ALU.mult, accum_out=out).then_inc(free, 1)

            def some_dots(t, place):
                for k in plan[t, place][0]:
                    if k == columns_of(t - 1)[0]:
                        eng.wait_ge(h2_copied, t)
                        if t == 1:
                            eng.wait_ge(h2_doubled, 16)
                    eng.wait_ge(u_in[k % RING_U], 16 * (k // RING_U + 1))
                    dot(ring_u[:, k % RING_U, :], dots_all[:, k:k + 1], u_free)

            def weights(t):
                cols = columns_of(t)
                eng.wait_ge(gelu_done, t + 1)
                w = dots_all[:, cols[0]:cols[-1] + 1]
                eng.tensor_tensor(w, w, gate_all[:, cols[0]:cols[-1] + 1], ALU.mult).then_inc(wgt_done, 1)

            for t in range(TILES):
                eng.wait_ge(qk_turned, t + 1)
                turned = PB[0:HD, 0:KV_HEADS * P].rearrange("p (g q) -> p g q", q=P)
                eng.wait_ge(cleared, 7)
                for par in range(2):
                    if t:
                        first = N_META + P * (t - 1)
                        eng.tensor_copy(k_prompt[0:HD, par:HEADS:2, first:first + P], turned).then_inc(k_ready, 1)
                    else:
                        link(eng.tensor_copy(k_sample[0:HD, par:HEADS:2, PAST:SAMPLE_KEYS], turned[:, :, 0:N_SAMPLE]))
                        eng.tensor_copy(k_prompt[0:HD, par:HEADS:2, 0:N_META],
                                        turned[:, :, META0:META1]).then_inc(k_ready, 1)
                for b, (_, _, n, keys, first, _, _) in enumerate(f_blocks(t)):
                    eng.wait_ge(f_done, f_before(t) + b + 1)
                    sums = PC[0:1, :].rearrange("p (h q) -> p h q", h=HEADS)
                    eng.tensor_scalar(keys[96:97, :, first:first + n], sums[:, :, 0:n], -1.0, None,
                                      ALU.mult).then_inc(f_k, 1)
                    eng.tensor_copy(carry, sums[:, :, n - 1]).then_inc(f_k, 1)
                    if t == 0 and b >= LATER - 1:
                        item_sigmoids(t, f"sum{b}")
                some_dots(t, "start")
                item_sigmoids(t, "start")

                a = heads_before(t)
                for n_q, (q0, m, _, n, _) in enumerate(problems(t)):
                    for h in range(HEADS):
                        eng.wait_ge(sc_done, a + 1)
                        psum = score_psum(a, n)
                        for k0 in ([n - m] if n // 512 == (n - m) // 512 or n <= 512 else [n - m, 512]):
                            k1 = 512 if (n > 512 and k0 < 512) else n
                            j = k0 - (n - m)
                            link(eng.tensor_tensor(psum[0:m, k0:k1], psum[0:m, k0:k1],
                                                   consts[0:m, C_MASK + j:C_MASK + j + k1 - k0], ALU.add))
                        link(eng.tensor_reduce(negmax[0:m, h:h + 1], psum[0:m, 0:n], AX_X, ALU.max))
                        eng.tensor_scalar(negmax[0:m, h:h + 1], negmax[0:m, h:h + 1], -1.0, None,
                                          ALU.mult).then_inc(sc_max, 1)
                        a += 1
                        if n_q == 0:
                            some_dots(t, f"head{h}")
                        item_sigmoids(t, ("head", "meta")[n_q] + str(h))
                    eng.wait_ge(p_done, a)
                    link(eng.reciprocal(psums[0:m, :], psums[0:m, :]))
                    eng.wait_ge(o_done, a)
                    if t and n_q == 0:
                        eng.wait_ge(h2_copied, t)
                        eng.wait_ge(h2_doubled, 16)
                        eng.wait_ge(h2t_done, t)
                    eng.tensor_tensor(rows[q0:q0 + m, 0:HW].rearrange("p (h d) -> p h d", d=HD),
                                      PC[0:m, 0:HW].rearrange("p (h d) -> p h d", d=HD),
                                      psums[0:m, :].unsqueeze(2).to_broadcast([m, HEADS, HD]),
                                      ALU.mult).then_inc(att_done, 1)

                eng.wait_ge(hg_in_evac, 2 * (t + 1))
                sums = w1[:, 0:HW]
                sums_h = sums.rearrange("p (h q) -> p h q", h=HG)
                if t == 0:
                    link(eng.memset(lev[:, NL * HW:(NL + 1) * HW], 0.0))
                for l in range(first_level(t), NL):
                    m = LEVELS[l]
                    out, src = halves(lev[:, l * HW:(l + 1) * HW], HW // (2 * m), m), halves(sums, HW // (2 * m), m)
                    mid = src[:, :, 0, m - 1:m].to_broadcast([P, HW // (2 * m), m])
                    eng.tensor_tensor(out[:, :, 0, :], mid, src[:, :, 0, :], ALU.subtract)
                    eng.tensor_tensor(out[:, :, 1, :], src[:, :, 1, :], mid, ALU.subtract)
                to_end = lev[:, NL * HW:(NL + 1) * HW].rearrange("p (h q) -> p h q", h=HG)
                for _, r0, n, _ in ends(t):
                    eng.tensor_tensor(to_end[:, :, r0:r0 + n],
                                      sums_h[:, :, r0 + n - 1:r0 + n].to_broadcast([P, HG, n]),
                                      sums_h[:, :, r0:r0 + n], ALU.subtract)
                eng.tensor_copy(lev[:, (NL + 1) * HW:(NL + 2) * HW], sums).then_inc(lev_ready, 1)
                some_dots(t, "levels")
                item_sigmoids(t, "levels")
                eng.wait_ge(lev_exp, t + 1)
                queries, keys = w1[:, HW:2 * HW], w1[:, 2 * HW:3 * HW]
                for l in range(first_level(t), NL):
                    m = LEVELS[l]
                    both = halves(lev[:, l * HW:(l + 1) * HW], HW // (2 * m), m)
                    for side, what in ((0, keys), (1, queries)):
                        eng.tensor_tensor(both[:, :, side, :], both[:, :, side, :],
                                          halves(what, HW // (2 * m), m)[:, :, side, :], ALU.mult)
                eng.tensor_tensor(lev[:, NL * HW:(NL + 1) * HW], lev[:, NL * HW:(NL + 1) * HW], keys, ALU.mult)
                from_start = lev[:, (NL + 1) * HW:(NL + 2) * HW]
                if ends_before(t):
                    eng.wait_ge(st_new, ends_before(t))
                for i, (_, r0, n, _) in enumerate(ends(t)):
                    link(eng.tensor_copy(e_end[:, HG * i:HG * (i + 1)],
                                         from_start.rearrange("p (h q) -> p h q", h=HG)[:, :, r0 + n - 1]))
                eng.tensor_tensor(from_start, from_start, queries, ALU.mult).then_inc(lev_mul, 1)
                some_dots(t, "masks")
                item_sigmoids(t, "masks")
                for h in range(HG):
                    eng.wait_ge(gram_done, HG * t + h + 1)
                    masked = w2[:, D:2 * D]
                    c0 = first_level(t) * P
                    link(eng.tensor_tensor(masked[:, c0:D], (PA, PB)[h % 2][:, c0:D],
                                           level_masks[:, c0:D], ALU.mult))
                    eng.tensor_reduce(w1[:, D + HW + h * P:D + HW + (h + 1) * P],
                                      masked[:, c0:D].rearrange("p (l q) -> p q l", q=P),
                                      AX_X, ALU.add).then_inc(at_ready, 1)
                    eng.wait_ge(at_ready, HG * t + h + 1)
                for i, (which, _, _, psum) in enumerate(ends(t)):
                    eng.wait_ge(ho_done, HG * (t + 1))
                    eng.wait_ge(st_done, ends_before(t) + i + 1)
                    for h in range(HG):
                        s = state[:, which, h * HK:(h + 1) * HK]
                        last = eng.scalar_tensor_tensor(out=s, in0=s, scalar=e_end[:, HG * i + h:HG * i + h + 1],
                                                        in1=psum[:, h * HK:(h + 1) * HK], op0=ALU.mult, op1=ALU.add)
                    last.then_inc(st_new, 1)
                some_dots(t, "norm")
                item_sigmoids(t, "norm")
                eng.wait_ge(ho_evac, t + 1)
                eng.wait_ge(hgain_in, 16)
                o = w1[:, 0:HW]
                o_h = o.rearrange("p (h v) -> p h v", h=HG)
                link(eng.tensor_tensor(w2[:, 0:HW], o, o, ALU.mult))
                link(eng.tensor_reduce(ss[:, 0:HG], w2[:, 0:HW].rearrange("p (h v) -> p h v", h=HG), AX_X, ALU.add))
                inverse_root(HG, HK)
                link(eng.tensor_tensor(o_h, o_h, rstd[:, 0:HG].unsqueeze(2).to_broadcast([P, HG, HK]), ALU.mult))
                link(eng.tensor_tensor(o, o, hgain[:, :], ALU.mult))
                if t == 0:
                    link(eng.memset(rows[96:P, 0:HW], 0.0))
                eng.tensor_tensor(rows[:, HW:2 * HW], o, act[:, SHG:SHG + HW], ALU.mult).then_inc(mix_ready, 1)

                some_dots(t, "out")
                item_sigmoids(t, "out")
                if t == 0:
                    eng.wait_ge(item_done, ITEMS)
                    eng.sem_inc(u_free, RING_U)
                    eng.sem_inc(v_free, RING_V)
                eng.wait_ge(wo_used, DC * (t + 1))
                eng.wait_ge(x2_in, 16 * (t + 2))
                n = P if t else META1
                eng.tensor_tensor(xm[0:n, :], xm[0:n, :], PB[0:n, :], ALU.add).then_inc(x1_ready, 1)
                eng.wait_ge(x1_ready, t + 1)
                mean_square(xm, w1[:, D:2 * D])
                eng.wait_ge(mixt_done, t + 1)
                eng.wait_ge(gain_2_in, 16 * (t + 1))
                eng.scalar_tensor_tensor(out=rows[:, :], in0=xm, scalar=rstd[:, 0:1], in1=gain_2,
                                         op0=ALU.mult, op1=ALU.mult).then_inc(h2_ready, 1)
                some_dots(t, "rows")

                eng.wait_ge(ps_done, t + 1)
                eng.wait_ge(x1_saved, 16 * (t + 1))
                ph = top_heads(t)
                scores = [(PA, PB)[i // PH][:, (i % PH) * NKEY:(i % PH + 1) * NKEY] for i in range(2 * ph)]

                def sixteen(values, left, val, idx, read=None):
                    n = len(values)
                    for i in range(n):
                        last = eng.max(val[:, i, 0:8], values[i])
                    link(last)
                    for i in range(n):
                        eng.max_index(idx[:, i, 0:8], val[:, i, 0:8], values[i])
                        last = eng.match_replace(left[i], val[:, i, 0:8], values[i], NEG)
                    link(last)
                    if read is not None:
                        eng.sem_inc(read, 1)
                    for i in range(n):
                        last = eng.max(val[:, i, 8:16], left[i])
                    link(last)
                    for i in range(n):
                        last = eng.max_index(idx[:, i, 8:16], val[:, i, 8:16], left[i])
                    link(last)

                if t:
                    weights(t - 1)
                sixteen(scores, [tk_left[:, i, :] for i in range(2 * ph)], tk_val, tk_idx, ps_read)
                pairs = TOPK * TOPK
                cand = w1[:, 0:ph * pairs].rearrange("p (h i j) -> p h i j", h=ph, i=TOPK)
                val_h = tk_val[:, 0:2 * ph, :].rearrange("p (h c) k -> p h c k", c=2)
                link(eng.tensor_tensor(cand, val_h[:, :, 0, :].unsqueeze(3).to_broadcast([P, ph, TOPK, TOPK]),
                                       val_h[:, :, 1, :].unsqueeze(2).to_broadcast([P, ph, TOPK, TOPK]), ALU.add))
                sixteen([w1[:, h * pairs:(h + 1) * pairs] for h in range(ph)],
                        [w2[:, h * pairs:(h + 1) * pairs] for h in range(ph)], top_val, top_j)
                n = ph * TOPK
                gates = gate_new[:, 0:n].rearrange("p (h k) -> p h k", k=TOPK)
                eng.tensor_tensor(gates, top_val[:, 0:ph, :], top_val[:, 0:ph, 0:1].to_broadcast([P, ph, TOPK]),
                                  ALU.subtract).then_inc(less_max, 1)
                top_jf = lev[:, 2944:2944 + n].bitcast(U32)
                link(eng.tensor_scalar(j_part[0][:, 0:n], top_jf, 4, None, ALU.logical_shift_right))
                link(eng.tensor_scalar(j_part[1][:, 0:n], top_jf, 15, None, ALU.bitwise_and))
                link(eng.tensor_copy(tk_idxf[:, 0:2 * ph, :], tk_idx[:, 0:2 * ph, :]))
                idx_h = tk_idxf[:, 0:2 * ph, :].rearrange("p (h c) k -> p h c k", c=2)
                same = w2[:, 0:ph * pairs].rearrange("p (h k i) -> p h k i", h=ph, i=TOPK)
                shape = [P, ph, TOPK, TOPK]
                for c in range(2):
                    link(eng.tensor_copy(j_partf[c][:, 0:n], j_part[c][:, 0:n]))
                    j = j_partf[c][:, 0:n].rearrange("p (h k) -> p h k", k=TOPK)
                    iota = consts[:, C_IOTA:C_IOTA + TOPK].unsqueeze(1).unsqueeze(1)
                    link(eng.tensor_tensor(same, j.unsqueeze(3).to_broadcast(shape), iota.to_broadcast(shape),
                                           ALU.is_equal))
                    link(eng.tensor_tensor(same, same, idx_h[:, :, c, :].unsqueeze(2).to_broadcast(shape), ALU.mult))
                    link(eng.tensor_reduce(e_part[c][:, 0:n].rearrange("p (h k) -> p h k", k=TOPK), same, AX_X, ALU.add))
                link(eng.scalar_tensor_tensor(out=e_part[0][:, 0:n], in0=e_part[0][:, 0:n], scalar=float(NKEY),
                                              in1=e_part[1][:, 0:n], op0=ALU.mult, op1=ALU.add))
                first = columns_of(t)[0]
                eng.tensor_copy(idx_all[:, first:first + n], e_part[0][:, 0:n]).then_inc(chosen, 1)
                eng.wait_ge(gate_exp, t + 1)
                link(eng.tensor_reduce(gsum[:, 0:ph], gates, AX_X, ALU.add))
                link(eng.reciprocal(gsum[:, 0:ph], gsum[:, 0:ph]))
                eng.tensor_tensor(gate_all[:, first:first + n].rearrange("p (h k) -> p h k", k=TOPK), gates,
                                  gsum[:, 0:ph].unsqueeze(2).to_broadcast([P, ph, TOPK]), ALU.mult).then_inc(top_done, 1)

            def finish(t):
                x1 = x1_all[:, t * D:(t + 1) * D]
                if t < PARTS:
                    eng.wait_ge(y_part_in, 16)
                    link(eng.tensor_tensor(x1, x1, y_part[:, t, :], ALU.add))
                eng.wait_ge(final_gain_in, 16)
                mean_square(x1, rows_t[:, :])
                eng.scalar_tensor_tensor(out=x1, in0=x1, scalar=rstd[:, 0:1], in1=rows[:, :],
                                         op0=ALU.mult, op1=ALU.mult).then_inc(y_ready, 1)

            eng.wait_ge(h2_copied, TILES)
            eng.sem_inc(l_free, RING_L)
            eng.wait_ge(b_in, 16 * TILES)

            last_first = columns_of(TILES - 1)[0]
            for t, group in late:
                x1 = x1_all[:, t * D:(t + 1) * D]
                before = late_before[t]

                def groups(p0, p1, with_dots):
                    with eng.Fori(p0, p1) as pair:
                        for half in range(2):
                            for j in range(GROUP):
                                if j in DVE_SLOTS:
                                    i = DVE_SLOTS.index(j)
                                    at = pair * (2 * GROUP) + ((group + half) * GROUP + j)
                                    eng.wait_ge(d_in[i], pair * 32 + 16 * (before + half + 1))
                                    eng.wait_ge(d_free, pair * (2 * ND) + (ND * (before + half + 1) + i))
                                    eng.scalar_tensor_tensor(out=x1, in0=ring_d[:, i, :],
                                                             scalar=dots_all[:, bass.ds(at, 1)], in1=x1,
                                                             op0=ALU.mult, op1=ALU.add).then_inc(d_free, 1)
                                if with_dots:
                                    m = (before + half - KEYS_FROM) * GROUP + j
                                    slot = j % RING_L
                                    eng.wait_ge(l_in[slot], pair * (32 * GROUP // RING_L) + 16 * (m // RING_L + 1))
                                    k = pair * (2 * GROUP) + (last_first + m)
                                    dot(ring_l[:, slot, :], dots_all[:, bass.ds(k, 1)], l_free)
                            eng.wait_ge(d_free, pair * (2 * ND) + ND * (before + half + 2))
                            eng.wait_ge(p_free, pair * (2 * NPE) + (NPE * (before + half + 2) + 1))
                            added = (y_even_added, y_odd_added)[half]
                            eng.tensor_tensor(x1, x1, (PC, PD)[half][:, :], ALU.add).then_inc(added, 1)
                            eng.wait_ge(added, pair + (before // 2 + 2))

                first = max(0, (KEYS_FROM - before) // 2)
                end = min(late_groups(t) // 2, max(0, (KEYS_FROM + T_GROUPS - before) // 2))
                if t == TILES - 1:
                    weights(t)
                    eng.wait_ge(wgt_done, t + 1)
                for p0, p1, with_dots in ((0, first, False), (first, end, True), (end, late_groups(t) // 2, False)):
                    p1 = min(p1, late_groups(t) // 2)
                    if p0 < p1:
                        groups(p0, p1, with_dots)
                if t == 1:
                    finish(0)
                finish(t)


def constant_columns():
    import numpy as np
    r = np.arange(P)
    s, t = r[:, None], r[None, :]
    upper = (s <= t)
    cols = [s == t, (s % N_SAMPLE == t) & (t < N_SAMPLE), upper, upper & (s // 64 == t // 64),
            np.where(t <= s, 0.0, NEG), np.broadcast_to(np.arange(TOPK)[None, :], (P, TOPK))]
    for m in LEVELS:
        cols.append((s // (2 * m) == t // (2 * m)) & (s // m % 2 == 0) & (t // m % 2 == 1))
    cols.append(s == t)
    return np.concatenate([np.asarray(c, np.float32) for c in cols], axis=1)


_OUTS = [("y_prompt", (1, SEQ, D)), ("y_sample", (1, N_SAMPLE, D)),
         ("new_k_prompt", (N_META + SEQ, KV_W)), ("new_v_prompt", (N_META + SEQ, KV_W)),
         ("new_logf_prompt", (N_META + SEQ, HEADS)), ("new_state_prompt", (HG, HK, HK)),
         ("new_k_sample", (N_SAMPLE, KV_W)), ("new_v_sample", (N_SAMPLE, KV_W)),
         ("new_logf_sample", (N_SAMPLE, HEADS)), ("new_state_sample", (HG, HK, HK))]


def kernel(x_prompt, x_sample, cache_k, cache_v, cache_logf, state_hgrn, meta_tokens, w_in, b_forget,
           hg_lb_logits, hg_norm_gain, w_out, norm1_gain, norm2_gain, peer_w_query, peer_sub_keys,
           peer_expert_u, peer_expert_v, final_norm_gain):
    import numpy as np
    import concourse.bacc as bacc
    from concourse.bass_utils import run_bass_kernel_spmd

    def plain(a):
        return np.ascontiguousarray(np.asarray(a))

    cache_k, cache_v = plain(cache_k), plain(cache_v)
    arrays = {
        "x_prompt": plain(x_prompt), "x_sample": plain(x_sample),
        "cache_kt": plain(cache_k[0, 0].transpose(2, 1, 0)),
        "cache_v": cache_v.reshape(PAST, KV_W), "cache_logf": plain(cache_logf)[0, 0],
        "state_hgrn": plain(state_hgrn)[0, 0], "meta_tokens": plain(meta_tokens), "w_in": plain(w_in),
        "b_forget": plain(b_forget), "hg_lb_logits": plain(hg_lb_logits), "hg_norm_gain": plain(hg_norm_gain),
        "w_out": plain(w_out), "norm1_gain": plain(norm1_gain), "norm2_gain": plain(norm2_gain),
        "peer_w_query": plain(peer_w_query),
        "sub_keys_t": plain(plain(peer_sub_keys)[0].reshape(2 * PH, NKEY, P).transpose(2, 0, 1)).reshape(P, 2 * PH * NKEY),
        "peer_expert_u": plain(peer_expert_u), "peer_expert_v": plain(peer_expert_v),
        "final_norm_gain": plain(final_norm_gain), "constants": constant_columns(),
    }
    arrays = {n: plain(a) for n, a in arrays.items()}
    nc = bacc.Bacc("TRN2", target_bir_lowering=False, num_devices=1)
    args = {n: nc.dram_tensor(n, a.shape, F32, kind="ExternalInput").ap() for n, a in arrays.items()}
    for n, shape in _OUTS:
        args[n] = nc.dram_tensor(n, shape, F32, kind="ExternalOutput").ap()
    build(nc, **args)
    got = run_bass_kernel_spmd(nc, [arrays], core_ids=[0]).results[0]
    shapes = [(1, SEQ, D), (1, N_SAMPLE, D), (1, 1, N_META + SEQ, KV_HEADS, HD), (1, 1, N_META + SEQ, KV_HEADS, HD),
              (1, 1, N_META + SEQ, HEADS), (1, 1, HG, HK, HK), (1, 1, N_SAMPLE, KV_HEADS, HD),
              (1, 1, N_SAMPLE, KV_HEADS, HD), (1, 1, N_SAMPLE, HEADS), (1, 1, HG, HK, HK)]
    return tuple(np.asarray(got[n]).reshape(s) for (n, _), s in zip(_OUTS, shapes))
```
